# Optimizing a Trainium2 kernel written in Bass

```python
import jax, jax.numpy as jnp
from jax import lax
import numpy as np
import math

D_MODEL = 1024
BATCH = 1
SEQ = 256
DEPTH = 1

CTX_LEN = 256
GRID_W = 64

A_HEADS = 4
A_DK = 128
A_DV = 128
A_KW = A_HEADS * A_DK
A_VW = A_HEADS * A_DV
A_CHUNK = 64

B_GROUPS = 4
B_GW = 128
B_W = B_GROUPS * B_GW
B_CHUNK = 2 * GRID_W

D_FF = -(-8 * D_MODEL // (3 * 256)) * 256

N_MOD = 6
EPS = 1e-6

CTX_STATE_COLS = 2 * A_KW + A_VW
SPLIT_IDX = (A_KW, 2 * A_KW, 2 * A_KW + A_VW, 3 * A_KW + A_VW, 3 * A_KW + 2 * A_VW,
             3 * A_KW + 2 * A_VW + B_W, 3 * A_KW + 2 * A_VW + 2 * B_W,
             3 * A_KW + 2 * A_VW + 2 * B_W + D_MODEL)
IN_COLS = 3 * A_KW + 2 * A_VW + 2 * B_W + 2 * D_MODEL


def rmsnorm(x, g):
    xf = x.astype(jnp.float32)
    y = xf * lax.rsqrt(jnp.mean(xf * xf, axis=-1, keepdims=True) + EPS)
    return (y * g.astype(jnp.float32)).astype(x.dtype)

def layernorm(x, g, b):
    xf = x.astype(jnp.float32)
    mu = jnp.mean(xf, axis=-1, keepdims=True)
    var = jnp.mean(jnp.square(xf - mu), axis=-1, keepdims=True)
    y = (xf - mu) * lax.rsqrt(var + EPS) * g.astype(jnp.float32) + b.astype(jnp.float32)
    return y.astype(x.dtype)

def modulate(h, shift, scale):
    return h * (1 + scale) + shift

def split_heads(t):
    return t.reshape(t.shape[0], t.shape[1], A_HEADS, -1).astype(jnp.float32)

def flip_seq(t):
    return jnp.flip(t, axis=1)

def forget_gate(f_logit, lb):
    f = lb + (1 - lb) * jax.nn.sigmoid(f_logit.astype(jnp.float32))
    return jnp.log(f), 1 - f

def hgrn2_chunked(q, k, logf, v, s0):
    b_, L = q.shape[:2]
    n = L // A_CHUNK
    rs = lambda t: t.reshape(b_, n, A_CHUNK, *t.shape[2:])
    q, k, logf, v = rs(q), rs(k), rs(logf), rs(v)
    bcum = jnp.cumsum(logf, axis=2)
    blast = bcum[:, :, -1:]
    mid = 0.5 * blast
    q_in = q * jnp.exp(bcum - mid)
    k_in = k * jnp.exp(mid - bcum)
    scores = jnp.einsum('bnthd,bnshd->bnhts', q_in, k_in)
    mask = jnp.tril(jnp.ones((A_CHUNK, A_CHUNK), dtype=bool))
    scores = jnp.where(mask, scores, 0.0)
    o_intra = jnp.einsum('bnhts,bnshe->bnthe', scores, v)
    d_state = jnp.einsum('bnshd,bnshe->bnhde', k * jnp.exp(blast - bcum), v)
    decay = jnp.exp(blast[:, :, 0])

    def step(s, inp):
        a, d = inp
        return a[..., None] * s + d, s

    s_final, s_in = lax.scan(step, s0, (jnp.moveaxis(decay, 1, 0), jnp.moveaxis(d_state, 1, 0)))
    s_in = jnp.moveaxis(s_in, 0, 1)
    o_inter = jnp.einsum('bnthd,bnhde->bnthe', q * jnp.exp(bcum), s_in)
    o = (o_intra + o_inter).reshape(b_, L, A_HEADS, A_DV)
    return o, s_final

def hgrn2_final_state(k, logf, v):
    bcum = jnp.cumsum(logf, axis=1)
    w = k * jnp.exp(bcum[:, -1:] - bcum)
    return jnp.einsum('blhd,blhe->bhde', w, v)

def chunk_sgu(u, v, ln_g, ln_b, w_s, b_s, n_chunks):
    b_, L = u.shape[:2]
    v = layernorm(v, ln_g, ln_b)
    vc = v.reshape(b_, n_chunks, B_CHUNK, B_GROUPS, B_GW)
    mixed = jnp.einsum('gts,bnsgc->bntgc', w_s, vc) + jnp.transpose(b_s)[:, :, None]
    return u * mixed.reshape(b_, L, B_W)

def token_mixers(p, lb, g_norm_a, ln_v_g, ln_v_b, w_s, b_s, w_pa, w_pb, w_o, s0_f, s0_b, n_chunks_b):
    f_f, f_b, i_in, q, og, u, v, ga, gb = jnp.split(p, SPLIT_IDX, axis=-1)
    b_, L = p.shape[:2]
    logf_f, k_f = forget_gate(f_f, lb[0])
    logf_b, k_b = forget_gate(f_b, lb[1])
    qh, vh = split_heads(q), split_heads(i_in)
    o_f, s_f = hgrn2_chunked(qh, split_heads(k_f), split_heads(logf_f), vh, s0_f)
    o_b, s_b = hgrn2_chunked(flip_seq(qh), flip_seq(split_heads(k_b)), flip_seq(split_heads(logf_b)),
                             flip_seq(vh), s0_b)
    o_a = rmsnorm(o_f + flip_seq(o_b), g_norm_a).reshape(b_, L, A_VW).astype(p.dtype)
    o_a = o_a * jax.nn.silu(og)
    o_b_mlp = chunk_sgu(jax.nn.gelu(u), jax.nn.gelu(v), ln_v_g, ln_v_b, w_s, b_s, n_chunks_b)
    merged = jax.nn.sigmoid(ga) * (o_a @ w_pa) + jax.nn.sigmoid(gb) * (o_b_mlp @ w_pb)
    return merged @ w_o, s_f, s_b

def swiglu(h, w_up, w_down):
    a, b = jnp.split(h @ w_up, 2, axis=-1)
    return (jax.nn.silu(a) * b) @ w_down

def first_inputs(seed: int = 0) -> dict:
    key = jax.random.key(seed)
    ks = jax.random.split(key, 21)
    nrm = lambda k, shape, s: jax.random.normal(k, shape, jnp.float32) * s
    return {
        'x': nrm(ks[0], (BATCH, SEQ, D_MODEL), 1.0),
        'c': nrm(ks[1], (BATCH, D_MODEL), 1.0),
        'ctx': nrm(ks[2], (BATCH, CTX_LEN, D_MODEL), 1.0),
        'c_ctx': nrm(ks[3], (D_MODEL,), 1.0),
        'w_mod': nrm(ks[4], (DEPTH, D_MODEL, N_MOD * D_MODEL), 0.5 * D_MODEL ** -0.5),
        'b_mod': nrm(ks[5], (DEPTH, N_MOD * D_MODEL), 0.01),
        'g_mix': 1.0 + nrm(ks[6], (DEPTH, D_MODEL), 0.1),
        'g_ffn': 1.0 + nrm(ks[7], (DEPTH, D_MODEL), 0.1),
        'w_in': nrm(ks[8], (DEPTH, D_MODEL, IN_COLS), D_MODEL ** -0.5),
        'lb_gamma': nrm(ks[9], (DEPTH + 1, 2, A_KW), 0.5),
        'g_norm_a': 1.0 + nrm(ks[10], (DEPTH, A_DV), 0.1),
        'ln_v_g': 1.0 + nrm(ks[11], (DEPTH, B_W), 0.1),
        'ln_v_b': nrm(ks[12], (DEPTH, B_W), 0.02),
        'w_s': nrm(ks[13], (DEPTH, B_GROUPS, B_CHUNK, B_CHUNK), 0.5 * B_CHUNK ** -0.5),
        'b_s': 1.0 + nrm(ks[14], (DEPTH, B_GROUPS, B_CHUNK), 0.1),
        'w_pa': nrm(ks[15], (DEPTH, A_VW, D_MODEL), A_VW ** -0.5),
        'w_pb': nrm(ks[16], (DEPTH, B_W, D_MODEL), B_W ** -0.5),
        'w_o': nrm(ks[17], (DEPTH, D_MODEL, D_MODEL), D_MODEL ** -0.5),
        'w_up': nrm(ks[18], (DEPTH, D_MODEL, 2 * D_FF), D_MODEL ** -0.5),
        'w_down': nrm(ks[19], (DEPTH, D_FF, D_MODEL), D_FF ** -0.5),
        'g_final': 1.0 + nrm(ks[20], (D_MODEL,), 0.1),
    }

def first_block(x, c, ctx, c_ctx, w_mod, b_mod, g_mix, g_ffn, w_in, lb_gamma, g_norm_a,
              ln_v_g, ln_v_b, w_s, b_s, w_pa, w_pb, w_o, w_up, w_down, g_final):
    bsz, L = x.shape[0], x.shape[1]
    rows = L // GRID_W
    n_chunks_lat = rows // 2
    n_chunks_ctx = ctx.shape[1] // B_CHUNK
    lb_all = jnp.cumsum(jax.nn.softmax(lb_gamma.astype(jnp.float32), axis=0), axis=0)
    for l in range(DEPTH):
        last = l == DEPTH - 1
        lb = lb_all[l]
        mod = (jax.nn.silu(c) @ w_mod[l] + b_mod[l]).reshape(bsz, N_MOD, D_MODEL)
        mc = (jax.nn.silu(c_ctx) @ w_mod[l] + b_mod[l]).reshape(N_MOD, D_MODEL)
        hc = modulate(rmsnorm(ctx, g_mix[l]), mc[0], mc[1])
        if last:
            pc = hc @ w_in[l][:, :CTX_STATE_COLS]
            f_f, f_b, i_c = jnp.split(pc, (A_KW, 2 * A_KW), axis=-1)
            logf_f, k_f = forget_gate(f_f, lb[0])
            logf_b, k_b = forget_gate(f_b, lb[1])
            vh = split_heads(i_c)
            s_ctx_f = hgrn2_final_state(split_heads(k_f), split_heads(logf_f), vh)
            s_ctx_b = hgrn2_final_state(flip_seq(split_heads(k_b)), flip_seq(split_heads(logf_b)), flip_seq(vh))
        else:
            zeros = jnp.zeros((bsz, A_HEADS, A_DK, A_DV), jnp.float32)
            mix_c, s_ctx_f, s_ctx_b = token_mixers(hc @ w_in[l], lb, g_norm_a[l], ln_v_g[l], ln_v_b[l],
                                                   w_s[l], b_s[l], w_pa[l], w_pb[l], w_o[l],
                                                   zeros, zeros, n_chunks_ctx)
            ctx = ctx + mc[2] * mix_c
            hc2 = modulate(rmsnorm(ctx, g_ffn[l]), mc[3], mc[4])
            ctx = ctx + mc[5] * swiglu(hc2, w_up[l], w_down[l])
        h = modulate(rmsnorm(x, g_mix[l]), mod[:, 0, None], mod[:, 1, None])
        mix_x, _, _ = token_mixers(h @ w_in[l], lb, g_norm_a[l], ln_v_g[l], ln_v_b[l],
                                   w_s[l], b_s[l], w_pa[l], w_pb[l], w_o[l],
                                   s_ctx_f, s_ctx_b, n_chunks_lat)
        x = x + mod[:, 2, None] * mix_x
        h2 = modulate(rmsnorm(x, g_ffn[l]), mod[:, 3, None], mod[:, 4, None])
        x = x + mod[:, 5, None] * swiglu(h2, w_up[l], w_down[l])
    return rmsnorm(x, g_final)


DEPTH_2 = 2

N_MIXERS = 2
N_SB_LAYERS = (DEPTH_2 + 1) // 2
N_MLA_LAYERS = DEPTH_2 // 2
Q_BLOCK = 128

SB_HEADS = 16
SB_HEAD_DIM = D_MODEL // SB_HEADS

MLA_HEADS = 16
MLA_Q_LORA = 256
MLA_KV_LORA = 128
MLA_NOPE_DIM = 64
MLA_ROPE_DIM = 32
MLA_V_DIM = 64
ROPE_THETA = 10000.0

D_FF_2 = 2816
FFN_RESIDUAL_WEIGHT = 0.5
N_NORMS_PER_LAYER = 6


def rms_norm(x, g):
    xf = x.astype(jnp.float32)
    y = xf * lax.rsqrt(jnp.mean(xf * xf, axis=-1, keepdims=True) + EPS)
    return (y * g.astype(jnp.float32)).astype(x.dtype)

def swiglu_2(x, w_in, w_out):
    gate, up = jnp.split(x @ w_in, 2, axis=-1)
    return (jax.nn.silu(gate) * up) @ w_out

def apply_rope(x, positions):
    d = x.shape[-1]
    inv_freq = ROPE_THETA ** (-jnp.arange(0, d, 2, dtype=jnp.float32) / d)
    ang = positions.astype(jnp.float32)[..., None] * inv_freq
    cos = jnp.cos(ang)[:, :, None, :].astype(x.dtype)
    sin = jnp.sin(ang)[:, :, None, :].astype(x.dtype)
    x1, x2 = jnp.split(x, 2, axis=-1)
    return jnp.concatenate([x1 * cos - x2 * sin, x2 * cos + x1 * sin], axis=-1)

def query_blocks(q):
    b, s, h, d = q.shape
    return q.reshape(b, s // Q_BLOCK, Q_BLOCK, h, d).transpose(1, 0, 2, 3, 4)

def merge_blocks(o):
    nb, b, qb, h, dv = o.shape
    return o.transpose(1, 0, 2, 3, 4).reshape(b, nb * qb, h * dv)

def stick_breaking_attention(h, w_in, w_out):
    b, s, _ = h.shape
    qkv = (h @ w_in).reshape(b, s, 3, SB_HEADS, SB_HEAD_DIM)
    q, k, v = qkv[:, :, 0], qkv[:, :, 1], qkv[:, :, 2]
    scale = 1.0 / math.sqrt(SB_HEAD_DIM)
    k_idx = jnp.arange(s)

    def block(args):
        qb, bi = args
        q_idx = bi * Q_BLOCK + jnp.arange(Q_BLOCK)
        z = jnp.einsum('bqhd,bkhd->bhqk', qb, k).astype(jnp.float32) * scale
        mask = k_idx[None, :] < q_idx[:, None]
        sp = jnp.where(mask, jax.nn.softplus(z), 0.0)
        tail = lax.cumsum(sp, axis=sp.ndim - 1, reverse=True) - sp
        log_a = jax.nn.log_sigmoid(z) - tail
        a = jnp.where(mask, jnp.exp(log_a), 0.0).astype(v.dtype)
        return jnp.einsum('bhqk,bkhd->bqhd', a, v)

    nb = s // Q_BLOCK
    o = lax.map(block, (query_blocks(q), jnp.arange(nb)))
    return merge_blocks(o) @ w_out

def multi_head_latent_attention(h, positions, w_in, q_norm, w_uq, kv_norm, w_ukv, w_out):
    b, s, _ = h.shape
    proj = h @ w_in
    c_q = proj[..., :MLA_Q_LORA]
    c_kv = proj[..., MLA_Q_LORA:MLA_Q_LORA + MLA_KV_LORA]
    k_rope = proj[..., MLA_Q_LORA + MLA_KV_LORA:][:, :, None, :]
    k_rope = apply_rope(k_rope, positions)[:, :, 0, :]

    q = (rms_norm(c_q, q_norm) @ w_uq).reshape(b, s, MLA_HEADS, MLA_NOPE_DIM + MLA_ROPE_DIM)
    q_nope = q[..., :MLA_NOPE_DIM]
    q_rope = apply_rope(q[..., MLA_NOPE_DIM:], positions)
    q = jnp.concatenate([q_nope, q_rope], axis=-1)

    kv = (rms_norm(c_kv, kv_norm) @ w_ukv).reshape(b, s, MLA_HEADS, MLA_NOPE_DIM + MLA_V_DIM)
    k_nope = kv[..., :MLA_NOPE_DIM]
    v = kv[..., MLA_NOPE_DIM:]
    scale = 1.0 / math.sqrt(MLA_NOPE_DIM + MLA_ROPE_DIM)
    k_idx = jnp.arange(s)

    def block(args):
        qb, bi = args
        q_idx = bi * Q_BLOCK + jnp.arange(Q_BLOCK)
        qn, qr = qb[..., :MLA_NOPE_DIM], qb[..., MLA_NOPE_DIM:]
        scores = (jnp.einsum('bqhd,bkhd->bhqk', qn, k_nope)
                  + jnp.einsum('bqhr,bkr->bhqk', qr, k_rope)).astype(jnp.float32) * scale
        mask = k_idx[None, :] <= q_idx[:, None]
        scores = jnp.where(mask, scores, -jnp.inf)
        p = jax.nn.softmax(scores, axis=-1).astype(v.dtype)
        return jnp.einsum('bhqk,bkhd->bqhd', p, v)

    nb = s // Q_BLOCK
    o = lax.map(block, (query_blocks(q), jnp.arange(nb)))
    return merge_blocks(o) @ w_out

def second_inputs(seed: int = 0) -> dict:
    key = jax.random.key(seed)
    ks = jax.random.split(key, 16)

    def w(k, shape, fan_in):
        return jax.random.normal(k, shape, jnp.float32) * fan_in ** -0.5

    def gain(k, shape):
        return 1.0 + 0.05 * jax.random.normal(k, shape, jnp.float32)

    sb_width = SB_HEADS * SB_HEAD_DIM
    mla_in = MLA_Q_LORA + MLA_KV_LORA + MLA_ROPE_DIM
    return {
        "x": jax.random.normal(ks[0], (BATCH, SEQ, D_MODEL), jnp.float32),
        "positions": jnp.broadcast_to(jnp.arange(SEQ, dtype=jnp.int32)[None, :], (BATCH, SEQ)),
        "norm_g": gain(ks[1], (DEPTH_2, N_NORMS_PER_LAYER, D_MODEL)),
        "ffn_w_in": w(ks[2], (DEPTH_2, 2, D_MODEL, 2 * D_FF_2), D_MODEL),
        "ffn_w_out": w(ks[3], (DEPTH_2, 2, D_FF_2, D_MODEL), D_FF_2),
        "sb_w_in": w(ks[4], (N_SB_LAYERS, D_MODEL, 3 * sb_width), D_MODEL),
        "sb_w_out": w(ks[5], (N_SB_LAYERS, sb_width, D_MODEL), sb_width),
        "mla_w_in": w(ks[6], (N_MLA_LAYERS, D_MODEL, mla_in), D_MODEL),
        "mla_q_norm": gain(ks[7], (N_MLA_LAYERS, MLA_Q_LORA)),
        "mla_w_uq": w(ks[8], (N_MLA_LAYERS, MLA_Q_LORA, MLA_HEADS * (MLA_NOPE_DIM + MLA_ROPE_DIM)), MLA_Q_LORA),
        "mla_kv_norm": gain(ks[9], (N_MLA_LAYERS, MLA_KV_LORA)),
        "mla_w_ukv": w(ks[10], (N_MLA_LAYERS, MLA_KV_LORA, MLA_HEADS * (MLA_NOPE_DIM + MLA_V_DIM)), MLA_KV_LORA),
        "mla_w_out": w(ks[11], (N_MLA_LAYERS, MLA_HEADS * MLA_V_DIM, D_MODEL), MLA_HEADS * MLA_V_DIM),
    }

def second_block(x, positions, norm_g, ffn_w_in, ffn_w_out, sb_w_in, sb_w_out,
              mla_w_in, mla_q_norm, mla_w_uq, mla_kv_norm, mla_w_ukv, mla_w_out):
    for i in range(DEPTH_2):
        g = norm_g[i]
        f = swiglu_2(rms_norm(x, g[0]), ffn_w_in[i, 0], ffn_w_out[i, 0])
        x = x + FFN_RESIDUAL_WEIGHT * rms_norm(f, g[1])
        h = rms_norm(x, g[2])
        j = i // N_MIXERS
        if i % N_MIXERS == 0:
            m = stick_breaking_attention(h, sb_w_in[j], sb_w_out[j])
        else:
            m = multi_head_latent_attention(h, positions, mla_w_in[j], mla_q_norm[j], mla_w_uq[j],
                                            mla_kv_norm[j], mla_w_ukv[j], mla_w_out[j])
        x = x + rms_norm(m, g[3])
        f = swiglu_2(rms_norm(x, g[4]), ffn_w_in[i, 1], ffn_w_out[i, 1])
        x = x + FFN_RESIDUAL_WEIGHT * rms_norm(f, g[5])
    return x


def setup_inputs(seed=0):
    out = dict(first_inputs(seed))
    for name, value in second_inputs(seed + 1).items():
        if name != "x":
            out[name + "_2"] = value
    return out


def reference(
    x, c, ctx, c_ctx, w_mod, b_mod, g_mix, g_ffn, w_in, lb_gamma, g_norm_a, ln_v_g, ln_v_b, w_s,
    b_s, w_pa, w_pb, w_o, w_up, w_down, g_final, positions_2, norm_g_2, ffn_w_in_2, ffn_w_out_2,
    sb_w_in_2, sb_w_out_2, mla_w_in_2, mla_q_norm_2, mla_w_uq_2, mla_kv_norm_2, mla_w_ukv_2,
    mla_w_out_2,
):
    x = first_block(
        x, c, ctx, c_ctx, w_mod, b_mod, g_mix, g_ffn, w_in, lb_gamma, g_norm_a, ln_v_g, ln_v_b,
        w_s, b_s, w_pa, w_pb, w_o, w_up, w_down, g_final,
    )
    return second_block(
        x, positions_2, norm_g_2, ffn_w_in_2, ffn_w_out_2, sb_w_in_2, sb_w_out_2, mla_w_in_2,
        mla_q_norm_2, mla_w_uq_2, mla_kv_norm_2, mla_w_ukv_2, mla_w_out_2,
    )


_drawn_inputs = setup_inputs


def setup_inputs(seed=0):
    import zlib

    import numpy as np

    out = dict(_drawn_inputs(seed))
    spreads = {}
    factors = {'ctx': 4.762,
     'c_ctx': 6.229,
     'b_mod': 3.159,
     'g_norm_a': 2.827,
     'ln_v_g': 5.714,
     'ln_v_b': 36.357,
     'b_s': 3.184,
     'mla_q_norm_2': 3.235}
    for name, (base, spread) in spreads.items():
        noise = np.random.default_rng([zlib.crc32(name.encode()), seed]).standard_normal(out[name].shape)
        drawn = base * np.exp(spread * noise) if base else spread * noise
        out[name] = __import__('jax').numpy.asarray(drawn.astype(out[name].dtype))
    for name, factor in factors.items():
        out[name] = (out[name] * factor).astype(out[name].dtype)
    return out
```

```python
from contextlib import ExitStack

import concourse.bass as bass
from concourse import mybir

F32 = mybir.dt.float32
F32R = mybir.dt.float32r
I32 = mybir.dt.int32
ALU = mybir.AluOpType
ACT = mybir.ActivationFunctionType
AX = mybir.AxisListType.X

P = 128
T = 256
D = 1024
KD = D // P
FT = 22
EPS = 1e-6
NRAW = 3
NSPLIT = 3
SLOT = 2048
NEG = -1e30

C_ID, C_ONE, C_TRI, C_NEG, C_INV, C_SGN, C_END = 0, 128, 256, 384, 640, 641, 642
S_CC, S_BMOD, S_GMIX, S_GFFN, S_GFIN, S_GNA, S_LBG, S_NG2, S_QN, S_KVN, S_END = (
    0, 16, 64, 72, 80, 88, 89, 105, 201, 203, 204)


class Lane:

    def __init__(self, eng, sem):
        self.eng, self.sem, self.n, self.met = eng, sem, 0, {}

    def wait(self, *marks):
        for m in marks:
            if not m:
                continue
            if isinstance(m, list):
                self.wait(*m)
                continue
            sem, value = m
            if self.met.get(id(sem), 0) < value:
                self.met[id(sem)] = value
                self.eng.wait_ge(sem, value)

    def do(self, fn, *marks):
        self.wait(*marks)
        self.n += 1
        fn(self.eng).then_inc(self.sem, 1)
        return self.mark

    def quiet(self, fn, *marks):
        self.wait(*marks)
        fn(self.eng)

    @property
    def mark(self):
        return (self.sem, self.n)


class Slot:

    def __init__(self, t):
        self.t, self.busy = t, []


class Turn:
    def __init__(self, slots):
        self.slots, self.i = slots, 0

    def next(self):
        s = self.slots[self.i % len(self.slots)]
        self.i += 1
        return s


def weight_plan():
    plan = [("mod", i, 2048, False) for i in range(8)]
    plan += [("win", i, 2048, True) for i in range(10)]
    plan += [("mod", i, 2048, False) for i in range(8, 16)]
    plan += [("win", i, 2048, True) for i in range(10, 14)]
    plan += [("mod", i, 2048, False) for i in range(16, 24)]
    plan += [("win", i, 2048, True) for i in range(14, 22)]
    plan += [("wpa", i, 2048, True) for i in range(2)] + [("wpb", i, 2048, True) for i in range(2)]
    plan += [("wo", i, 2048, True) for i in range(4)]
    plan += [("up", i, 2048, True) for i in range(FT)]
    plan += [("down", i, 1408, True) for i in range(16)]
    for layer in range(2):
        plan += [("up2", 2 * layer * FT + i, 2048, True) for i in range(FT)]
        plan += [("down2", 2 * layer * 16 + i, 1408, True) for i in range(16)]
        if layer == 0:
            plan += [("sbv", i, 2048, True) for i in range(4)]
            plan += [("sbqk", i, 2048, True) for i in range(8)]
            plan += [("sbo", i, 2048, True) for i in range(4)]
        else:
            plan += [("mlain", i, 1280 if i < 2 else 2560, True) for i in range(0)]
            plan += [("mla0", 0, 2048, True), ("mla1", 0, 2048, True)]
            plan += [("mla2", 0, 1024, True)]
            plan += [("mlakv", 0, 2048, True)]
            plan += [("mlaq", i, 1536, True) for i in range(2)]
            plan += [("mlao", i, 2048, True) for i in range(4)]
        plan += [("up2", (2 * layer + 1) * FT + i, 2048, True) for i in range(FT)]
        plan += [("down2", (2 * layer + 1) * 16 + i, 1408, True) for i in range(16)]
    return plan


def build(nc, a, out, stop=None):
    plan = weight_plan()
    ctx = ExitStack()
    with ctx:
        base = [nc.sbuf_base]

        def at(name, shape, off, dt=F32):
            return nc.alloc_sbuf_tensor_at(name, shape, dt, offset=off)

        def fixed(name, cols, dt=F32, shape=None):
            off = (base[0] + 31) // 32 * 32
            base[0] = off + cols * 4
            return at(name, shape or [P, cols], off, dt)

        def sem(name):
            return ctx.enter_context(nc.semaphore(name))

        CST = fixed("CST", C_END)
        SM = fixed("SM", S_END)
        X = fixed("X", KD * T, shape=[P, KD, T])
        RAW = [fixed(f"RAW{i}", SLOT) for i in range(NRAW)]
        WH = [fixed(f"WH{i}", SLOT, F32R) for i in range(NSPLIT)]
        WL = [fixed(f"WL{i}", SLOT, F32R) for i in range(NSPLIT)]
        SILC = fixed("SILC", 16)
        MOD = fixed("MOD", 96, shape=[P, 48, 2])
        VEC = fixed("VEC", 64)
        LBV = fixed("LBV", 48)
        NG2H = fixed("NG2H", 96)
        RT = Turn([Slot(fixed(f"RT{i}", 2)) for i in range(2)])
        RS = Turn([Slot(fixed(f"RS{i}", 2)) for i in range(2)])
        DG = Turn([Slot(fixed(f"DG{i}", T)) for i in range(1)])
        RB = Turn([Slot(fixed(f"RB{i}", T)) for i in range(2)])
        SQ = Turn([Slot(fixed(f"SQ{i}", T)) for i in range(3)])
        ACC = Turn([Slot(fixed(f"ACC{i}", T)) for i in range(2)])
        TA = Turn([Slot(fixed(f"TA{i}", T)) for i in range(2)])
        TB = Turn([Slot(fixed(f"TB{i}", T)) for i in range(2)])
        TC = Turn([Slot(fixed(f"TC{i}", T)) for i in range(2)])
        COS = fixed("COS", T)
        SIN = fixed("SIN", T)
        PB = (base[0] + 31) // 32 * 32
        KB = 1024

        def ph(name, kb, shape, dt=F32):
            return at(name, shape, PB + int(kb * KB), dt)

        BANKS = Turn([Slot(ctx.enter_context(nc.psum_tensor(f"PS{i}", [P, 512], F32))) for i in range(8)])

        PE = Lane(nc.tensor, sem("s_pe"))
        AC = Lane(nc.scalar, sem("s_act"))
        DV = Lane(nc.vector, sem("s_dve"))
        PO = Lane(nc.gpsimd, sem("s_pool"))
        SP = Lane(nc.sync, sem("s_sp"))
        s_raw = [sem(f"s_raw{i}") for i in range(NRAW)]
        s_in = sem("s_in")
        s_row = sem("s_row")
        s_out = sem("s_out")
        ins = [0]

        def load_small(dst, src, lane=AC, s=None):
            ins[0] += 16
            lane.quiet(lambda e, d=dst, r=src: e.dma_start(d, r).then_inc(s_in, 16))
            return (s_in, ins[0])

        IDN = CST[:, C_ID:C_ID + 128]
        ONE = CST[:, C_ONE:C_ONE + 128]
        TRI = CST[:, C_TRI:C_TRI + 128]
        NEGM = CST[:, C_NEG:C_NEG + 256]

        loaded, raw_slot, raw_free, order = {}, {}, {}, []
        split_slot, halves, consumed = {}, {}, {}
        nsplit = 0
        sidx = {}
        for j, (_, _, _, sp) in enumerate(plan):
            if sp:
                sidx[j] = nsplit
                nsplit += 1
        at_split = {v: k for k, v in sidx.items()}
        state = {"load": 0, "split": 0, "use": 0}

        def pump():
            moved = True
            while moved:
                moved = False
                j = state["load"]
                if j < len(plan) and (j < NRAW or (j - NRAW) in raw_free):
                    src, i, cols, _ = plan[j]
                    r = j % NRAW
                    SP.quiet(lambda e, r=r, c=cols, s=a[src][i]:
                             e.dma_start(RAW[r][:, 0:c], s).then_inc(s_raw[r], 16),
                             raw_free.get(j - NRAW))
                    loaded[j] = (s_raw[r], 16 * (j // NRAW + 1))
                    state["load"] += 1
                    moved = True
                s = state["split"]
                if s < nsplit:
                    j = at_split[s]
                    if j in loaded and (s < NSPLIT or (s - NSPLIT) in consumed):
                        free = consumed.get(s - NSPLIT)
                        c = plan[j][2]
                        r, h = RAW[j % NRAW], s % NSPLIT
                        hi = AC.do(lambda e, r=r, h=h, c=c: e.activation(WH[h][:, 0:c], r[:, 0:c], ACT.Copy),
                                   loaded[j], free)
                        lo = DV.do(lambda e, r=r, h=h, c=c: e.tensor_tensor(
                            WL[h][:, 0:c], r[:, 0:c], WH[h][:, 0:c].bitcast(F32), ALU.subtract),
                            hi, free)
                        halves[j] = (WH[h], WL[h], [hi, lo])
                        raw_free[j] = [hi, lo]
                        state["split"] += 1
                        moved = True

        def take(kind):
            j = state["use"]
            assert plan[j][0] == kind, (plan[j], kind)
            state["use"] += 1
            pump()
            if plan[j][3]:
                return j, *halves[j]
            return j, RAW[j % NRAW], None, [loaded[j]]

        def done(j):
            if plan[j][3]:
                consumed[sidx[j]] = PE.mark
            else:
                raw_free[j] = PE.mark

        def mm3(out_, lh, ll, rh, rl, first, last, signal, marks=()):
            PE.wait(*marks)
            PE.quiet(lambda e: e.matmul(out_, lh, rh, start=first, stop=False))
            PE.quiet(lambda e: e.matmul(out_, lh, rl, start=False, stop=False))
            f = lambda e: e.matmul(out_, ll, rh, start=False, stop=last)
            if signal:
                return PE.do(f)
            PE.quiet(f)
            return None

        def project(w, wl, cols, kt, xh, xl, out_, marks):
            for k in range(kt):
                lo, hi_ = cols(k)
                m = mm3(out_, w[:, lo:hi_], wl[:, lo:hi_], xh[:, k, :], xl[:, k, :], k == 0, k == kt - 1,
                        k == kt - 1, marks if k == 0 else ())
            return m

        def pair(kind, xh, xl, ready, kt=KD, marks=()):
            j, w, wl, wm = take(kind)
            b = BANKS.next()
            ms = []
            for t in range(2):
                ms.append(project(w, wl, lambda k, t=t: (k * 256 + t * 128, k * 256 + t * 128 + 128), kt, xh, xl,
                                  b.t[:, t * T:(t + 1) * T], [wm, ready, b.busy]))
            return j, b, [ms[1], ms[1]]

        def barrier():
            marks = [PE.mark, AC.mark, DV.mark, PO.mark]
            for lane in (PE, AC, DV, PO):
                lane.wait(*marks)

        class Norm:

            def __init__(self):
                self.acc, self.n, self.last = ACC.next(), 0, None

            def add(self, src, marks, scale=1.0):
                q = SQ.next() if self.n else self.acc
                dst = q.t
                m = AC.do(lambda e: e.activation(dst[:, 0:T], src, ACT.Square), marks, q.busy)
                self.sq = m
                if self.n:
                    acc = self.acc.t
                    self.last = DV.do(lambda e: e.tensor_tensor(acc[:, :], acc[:, :], dst[:, :], ALU.add),
                                      m, self.last)
                    q.busy = [self.last]
                else:
                    self.last = m
                self.n += 1
                return m

            def finish(self, dim):
                acc, b = self.acc.t, BANKS.next()
                PE.wait(self.last, b.busy, const)
                for t in range(2):
                    f = lambda e, t=t: e.matmul(b.t[:, t:t + 1], acc[:, t * P:(t + 1) * P], ONE[:, 0:1],
                                                start=True, stop=True)
                    m = PE.do(f) if t else PE.quiet(f)
                self.acc.busy = [m]
                rs, rt, dg, rb = RS.next(), RT.next(), DG.next(), RB.next()
                m = AC.do(lambda e: e.activation(rs.t[:, :], b.t[:, 0:2], ACT.Sqrt, bias=epsb, scale=1.0 / dim),
                          m, rs.busy)
                r = DV.do(lambda e: e.reciprocal(rt.t[:, :], rs.t[:, :]), m, rt.busy)
                rs.busy = [r]
                for t in range(2):
                    g = DV.do(lambda e, t=t: e.tensor_scalar(dg.t[:, t * P:(t + 1) * P], IDN, rt.t[:, t:t + 1], None,
                                                             ALU.mult), r, dg.busy)
                m = PE.do(lambda e: e.matmul(b.t[:, 0:T], ONE, dg.t[:, :], start=True, stop=True), g, m)
                dg.busy = [m]
                m = AC.do(lambda e: e.activation(rb.t[:, :], b.t[:, 0:T], ACT.Copy), m, rb.busy)
                b.busy = [m]
                self.rt, self.rb = rt, rb
                rt.busy = [r, g]
                return rb, rt, m, r

        const = load_small(CST[:, :], a["cst"])
        small = load_small(SM[:, :], a["small"])
        XC = ph("XC", 80, [P, KD, T])
        xin = load_small(X[:, :, :], a["x"])
        cin = load_small(XC[:, :, :], a["ctx"])
        ROW = ph("ROW", 72, [P, 3, 512])
        WST = ph("WST", 78, [P, 4, P])
        for i in range(3):
            row = load_small(ROW[:, i, :], a["rows"][i:i + 1, :].to_broadcast([P, 512]))
        row = load_small(WST[:, :, :], a["wst"])
        POS = ph("POS", 91, [P, T], I32)
        posm = load_small(POS[:, :], a["pos"].to_broadcast([P, T]))
        all_in = posm

        V_AM, V_AC, V_LB = 0, 8, 16
        EPSV = VEC[:, 60:61]
        PIV = VEC[:, 61:62]
        DV.do(lambda e: e.memset(EPSV, EPS))
        vconst = DV.do(lambda e: e.memset(PIV, 1.5707963267948966))
        epsb = EPSV
        AC.wait(vconst)

        pump()
        AC.wait(all_in)
        DV.wait(all_in)
        PE.wait(all_in)

        ANG = ph("ANG", 88, [P, T])
        NN = ph("NN", 89, [P, T])
        NM = ph("NM", 90, [P, T])
        d = DV.do(lambda e: e.tensor_copy(ANG[:, :], POS[:, :]))
        d = DV.do(lambda e: e.tensor_scalar(ANG[:, :], ANG[:, :], CST[:, C_INV:C_INV + 1], None, ALU.mult), d)
        d = DV.do(lambda e: e.tensor_scalar(NN[:, :], ANG[:, :], 0.15915494309189535, 12582912.0, ALU.mult, ALU.add), d)
        d = DV.do(lambda e: e.tensor_scalar(NM[:, :], NN[:, :], 12582912.0, None, ALU.subtract), d)
        for c in (6.28125, 0.0019340515136718750, 1.2556659146e-06):
            d = DV.do(lambda e, c=c: e.scalar_tensor_tensor(ANG[:, :], NM[:, :], -c, ANG[:, :], ALU.mult, ALU.add), d)
        d = DV.do(lambda e: e.tensor_scalar(ANG[:, :], ANG[:, :], 3.1415925, -3.1415925, ALU.min, ALU.max), d)
        m = AC.do(lambda e: e.activation(SIN[:, :], ANG[:, :], ACT.Sin), d)
        m2 = AC.do(lambda e: e.activation(NN[:, :], ANG[:, :], ACT.Abs), d)
        m2 = AC.do(lambda e: e.activation(COS[:, :], NN[:, :], ACT.Sin, bias=PIV, scale=-1.0), m2)
        rope = DV.do(lambda e: e.tensor_scalar(SIN[:, :], SIN[:, :], CST[:, C_SGN:C_SGN + 1], None, ALU.mult), m)
        rope = [rope, m2]

        silc = AC.do(lambda e: e.activation(SILC[:, :], SM[:, S_CC:S_CC + 16], ACT.Silu))
        g2h = DV.do(lambda e: e.tensor_scalar(NG2H[:, :], SM[:, S_NG2:S_NG2 + 96], 0.5, None, ALU.mult))

        def mods(n, after=None):
            for _ in range(n):
                j, w, _, wm = take("mod")
                i = plan[j][1]
                b = BANKS.next()
                PE.wait(wm, silc, b.busy)
                for t in range(2):
                    for k in range(KD):
                        f = lambda e, t=t, k=k: e.matmul(
                            b.t[:, 2 * t:2 * t + 2], w[:, k * 256 + t * 128:k * 256 + t * 128 + 128],
                            SILC[:, 2 * k:2 * k + 2], start=(k == 0), stop=(k == KD - 1))
                        m = PE.do(f) if (t == 1 and k == KD - 1) else PE.quiet(f)
                done(j)
                m = DV.do(lambda e, i=i: e.tensor_tensor(
                    MOD[:, 2 * i:2 * i + 2, :], b.t[:, 0:4].rearrange("p (a b) -> p a b", a=2),
                    SM[:, S_BMOD + 2 * i:S_BMOD + 2 * i + 2].unsqueeze(2).to_broadcast([P, 2, 2]), ALU.add), m)
                b.busy = [m]
                pump()
            return m

        g0 = SM[:, S_LBG:S_LBG + 8]
        g1 = SM[:, S_LBG + 8:S_LBG + 16]
        L = lambda i: LBV[:, 8 * i:8 * i + 8]
        d = DV.do(lambda e: e.tensor_tensor(L(0), g0, g1, ALU.max))
        DV.do(lambda e: e.tensor_tensor(L(1), g0, L(0), ALU.subtract), d)
        d = DV.do(lambda e: e.tensor_tensor(L(2), g1, L(0), ALU.subtract), d)
        m = AC.do(lambda e: e.activation(LBV[:, 8:24], LBV[:, 8:24], ACT.Exp), d)
        d = DV.do(lambda e: e.tensor_tensor(L(0), L(1), L(2), ALU.add), m)
        d = DV.do(lambda e: e.reciprocal(L(3), L(0)), d)
        d = DV.do(lambda e: e.tensor_tensor(L(4), L(1), L(3), ALU.mult), d)
        lbm = DV.do(lambda e: e.tensor_scalar(L(5), L(4), -1.0, 1.0, ALU.mult, ALU.add), d)
        LB = lambda i: LBV[:, 32 + i:33 + i]
        OMLB = lambda i: LBV[:, 40 + i:41 + i]

        HH = ph("HH", 0, [P, KD, T], F32R)
        HL = ph("HL", 8, [P, KD, T], F32R)
        HCH = ph("HCH", 16, [P, KD, T], F32R)
        HCL = ph("HCL", 24, [P, KD, T], F32R)

        def norm_of(src, marks):
            n = Norm()
            for k in range(KD):
                n.add(src[:, k, :], marks)
            return n.finish(D)

        rx = norm_of(X, [])
        rc = norm_of(XC, [])
        modm = mods(8)

        def scale_of(dst, gcol, mcol, which, marks):
            d = DV.do(lambda e: e.tensor_scalar(VEC[:, dst:dst + 8], MOD[:, mcol:mcol + 8, which], 1.0, None,
                                                ALU.add), marks)
            return DV.do(lambda e: e.tensor_tensor(VEC[:, dst:dst + 8], VEC[:, dst:dst + 8], SM[:, gcol:gcol + 8],
                                                   ALU.mult), d)

        va = scale_of(0, S_GMIX, 8, 0, modm)
        vc = scale_of(8, S_GMIX, 8, 1, modm)

        def halves_of(tmp, dh, dl, marks_h=(), marks_l=()):
            h = AC.do(lambda e: e.activation(dh, tmp, ACT.Copy), marks_h)
            low = DV.do(lambda e: e.tensor_tensor(dl, tmp, dh.bitcast(F32), ALU.subtract), h, marks_l)
            return [h, low]

        def modulated(src, r, av, mcol, which, dh, dl, marks):
            ready = []
            for k in range(KD):
                ta, tb = TA.next(), TB.next()
                d = DV.do(lambda e, k=k: e.scalar_tensor_tensor(ta.t[:, :], src[:, k, :], VEC[:, av + k:av + k + 1],
                                                                r[0].t[:, :], ALU.mult, ALU.mult), r[2], marks, ta.busy)
                d = DV.do(lambda e, k=k: e.tensor_scalar(tb.t[:, :], ta.t[:, :], MOD[:, mcol + k, which:which + 1], None,
                                                         ALU.add), d, tb.busy)
                ta.busy = [d]
                h, low = halves_of(tb.t[:, :], dh[:, k, :], dl[:, k, :], d)
                tb.busy = [h, low]
                ready.append(low)
            return ready[-1]

        hx = modulated(X, rx, 0, 0, 0, HH, HL, [va])
        hc = modulated(XC, rc, 8, 0, 1, HCH, HCL, [vc])
        rx[0].busy = [hx]
        rc[0].busy = [hc]

        FX = ph("FX", 32, [P, 8, T])
        FC = ph("FC", 40, [P, 8, T])
        VTX = ph("VTX", 48, [P, 2, 512])
        VTC = ph("VTC", 52, [P, 2, 512])
        Q = ph("Q", 56, [P, 4, T])
        VB = ph("VB", 60, [P, 2, 512])
        S0 = ph("S0", 64, [P, 8, P])
        O = ph("O", 68, [P, 4, T])
        GA = ph("GA", 16, [P, 8, T])
        GB = ph("GB", 24, [P, 8, T])
        OG = ph("OG", 40, [P, 4, T])
        UU = ph("UU", 44, [P, 4, T])

        fmark = {}
        for c in range(4):
            j, w, wl, wm = take("win")
            for src, (xh, xl, rd, dst) in enumerate(((HH, HL, hx, FX), (HCH, HCL, hc, FC))):
                b = BANKS.next()
                for t in range(2):
                    m = project(w, wl, lambda k, t=t: (k * 256 + t * 128, k * 256 + t * 128 + 128), KD, xh, xl,
                                b.t[:, t * T:(t + 1) * T], [wm, rd, b.busy])
                if src:
                    done(j)
                m = AC.do(lambda e, dst=dst, c=c: e.activation(
                    dst[:, 2 * c:2 * c + 2, :], b.t[:, :].rearrange("p (a b) -> p a b", a=2), ACT.Sigmoid), m)
                b.busy = [m]
                for t in range(2):
                    i = 2 * c + t
                    fmark[(src, i)] = DV.do(lambda e, dst=dst, i=i: e.tensor_scalar(
                        dst[:, i, :], dst[:, i, :], OMLB(i), LB(i), ALU.mult, ALU.add), m, lbm)
            pump()

        def tokens(w, wl, xh, xl, kt, t, out_, cols, marks):
            for k in range(kt):
                m = mm3(out_, xh[:, k, t * P:(t + 1) * P], xl[:, k, t * P:(t + 1) * P], cols(w, k), cols(wl, k),
                        k == 0, k == kt - 1, k == kt - 1, marks if k == 0 else ())
            return m

        c256 = lambda w, k: w[:, k * 256:k * 256 + 256]
        vm = []
        for c in range(2):
            j, w, wl, wm = take("win")
            for src, (xh, xl, rd, dst) in enumerate(((HH, HL, hx, VTX), (HCH, HCL, hc, VTC))):
                b = BANKS.next()
                for t in range(2):
                    m = tokens(w, wl, xh, xl, KD, t, b.t[:, t * T:(t + 1) * T], c256, [wm, rd, b.busy])
                if src:
                    done(j)
                m = AC.do(lambda e, dst=dst, c=c: e.activation(
                    dst[:, :, c * 256:(c + 1) * 256], b.t[:, :].rearrange("p (a b) -> p a b", a=2), ACT.Copy), m)
                b.busy = [m]
                vm.append(m)
            pump()
        ctx_read = PE.mark

        def plain(dst, kind, col, marks=()):
            j, b, ms = pair(kind, HH, HL, hx)
            done(j)
            m = AC.do(lambda e: e.activation(dst[:, col:col + 2, :], b.t[:, :].rearrange("p (a b) -> p a b", a=2),
                                             ACT.Copy), ms[1], marks)
            b.busy = [m]
            pump()
            return m

        qm = [plain(Q, "win", 2 * c) for c in range(2)]
        vb = []
        for c in range(2):
            j, w, wl, wm = take("win")
            b = BANKS.next()
            for t in range(2):
                m = tokens(w, wl, HH, HL, KD, t, b.t[:, t * T:(t + 1) * T], c256, [wm, b.busy])
            done(j)
            m = AC.do(lambda e, c=c: e.activation(VB[:, :, c * 256:(c + 1) * 256],
                                                  b.t[:, :].rearrange("p (a b) -> p a b", a=2), ACT.Copy), m)
            b.busy = [m]
            vb.append(m)
            pump()

        tmp_at = [80]

        def tmp(name, kb, shape=None):
            t = ph(name, tmp_at[0], shape or [P, T])
            tmp_at[0] += kb
            return t

        pool = {n: Turn([Slot(tmp(f"{n}{i}", 1)) for i in range(2)])
                for n in ("Lg", "Pf", "Kk", "Dd", "E0", "E1", "Qi", "Ki", "Kd")}
        pool["Kt"] = Turn([Slot(tmp(f"Kt{i}", 1)) for i in range(2)])
        pool["Sc"] = Turn([Slot(tmp(f"Sc{i}", 0.5, [P, P])) for i in range(2)])
        SST = Turn([Slot(tmp(f"SS{i}", 2, [P, 4, P])) for i in range(2)])
        for s in [x for t in (*pool.values(), SST) for x in t.slots]:
            s.busy = [hc, rx[2], rc[2], rope]
        RM = tmp("RM", 1)
        rm = DV.do(lambda e: e.memset(RM[:, :], 1.0), hc)
        rm = DV.do(lambda e: e.memset(RM[:, 0:T:64], 0.0), rm)

        def unit_head(F, i, src, chunked):
            lg, pf, kk = (pool[n].next() for n in ("Lg", "Pf", "Kk"))
            a1 = AC.do(lambda e: e.activation(lg.t[:, :], F[:, i, :], ACT.Ln), fmark[(src, i)], lg.busy)
            k1 = DV.do(lambda e: e.tensor_scalar(kk.t[:, :], F[:, i, :], -1.0, 1.0, ALU.mult, ALU.add), kk.busy)
            p1 = DV.do(lambda e: e.tensor_tensor_scan(pf.t[:, :], RM[:, :] if chunked else ONE[:, 0:1].to_broadcast([P, T]), lg.t[:, :], 0.0,
                                                      ALU.mult, ALU.add), a1, pf.busy, rm)
            return lg, pf, kk, a1, k1, p1

        def transpose2(src, marks):
            b, kt = BANKS.next(), pool["Kt"].next()
            PE.wait(marks, b.busy)
            for t in range(2):
                f = lambda e, t=t: e.transpose(b.t[:, t * P:(t + 1) * P], src[:, t * P:(t + 1) * P], IDN)
                m = PE.do(f) if t else PE.quiet(f)
            c = AC.do(lambda e: e.activation(kt.t[:, :], b.t[:, 0:T], ACT.Copy), m, kt.busy)
            b.busy = [c]
            return kt, m, c

        s0m = {}

        def ctx_unit(i):
            dr, h = i // 4, i % 4
            lg, pf, kk, a1, k1, p1 = unit_head(FC, i, 1, False)
            dd, e0, kd = (pool[n].next() for n in ("Dd", "E0", "Kd"))
            if dr == 0:
                x1 = DV.do(lambda e: e.tensor_scalar(dd.t[:, :], pf.t[:, :], -1.0, pf.t[:, T - 1:T], ALU.mult, ALU.add),
                           p1, dd.busy)
            else:
                x1 = DV.do(lambda e: e.tensor_tensor(dd.t[:, :], pf.t[:, :], lg.t[:, :], ALU.subtract), p1, dd.busy)
            lg.busy = pf.busy = [x1]
            a2 = AC.do(lambda e: e.activation(e0.t[:, :], dd.t[:, :], ACT.Exp), x1, e0.busy)
            dd.busy = [a2]
            x2 = DV.do(lambda e: e.tensor_tensor(kd.t[:, :], kk.t[:, :], e0.t[:, :], ALU.mult), a2, k1, kd.busy)
            e0.busy = kk.busy = [x2]
            kt, m, c = transpose2(kd.t, [x2])
            kd.busy = [m]
            b = BANKS.next()
            PE.wait(c, b.busy, vm)
            for t in range(2):
                f = lambda e, t=t: e.matmul(b.t[:, 0:P], kt.t[:, t * P:(t + 1) * P],
                                            VTC[:, t, h * P:(h + 1) * P], start=(t == 0), stop=(t == 1))
                m = PE.do(f) if t else PE.quiet(f)
            kt.busy = [m]
            c = DV.do(lambda e: e.tensor_copy(S0[:, i, :], b.t[:, 0:P]), m)
            b.busy = [c]
            s0m[i] = c

        for i in range(8):
            ctx_unit(i)
            modm2 = mods(1)

        om = {}

        def bc(ap2, n):
            return ap2.unsqueeze(2).to_broadcast([P, ap2.shape[1], n])

        def x_unit(h, dr):
            i = 4 * dr + h
            lg, pf, kk, a1, k1, p1 = unit_head(FX, i, 0, True)
            c3 = lambda t: t[:, :].rearrange("p (a b) -> p a b", a=4)
            tot = bc(pf.t[:, 63:T:64], 64)
            dd, e0, e1 = (pool[n].next() for n in ("Dd", "E0", "E1"))
            qi, ki, kd = (pool[n].next() for n in ("Qi", "Ki", "Kd"))
            av = VEC[:, 24 + 4 * (i % 2):28 + 4 * (i % 2)]
            hv = VEC[:, 32 + 4 * (i % 2):36 + 4 * (i % 2)]
            busy = unit_busy[i % 2]
            d1 = DV.do(lambda e: e.tensor_scalar(hv, pf.t[:, 63:T:64], 0.5, None, ALU.mult), p1, busy)
            a2 = AC.do(lambda e: e.activation(av, pf.t[:, 63:T:64], ACT.Exp), p1, busy)
            if dr:
                d2 = DV.do(lambda e: e.tensor_tensor(lg.t[:, :], pf.t[:, :], lg.t[:, :], ALU.subtract), p1)
                base_, base_m = lg, d2
            else:
                base_, base_m = pf, p1
            d3 = DV.do(lambda e: e.tensor_tensor(c3(dd.t), c3(base_.t), bc(hv, 64), ALU.subtract), d1, base_m, dd.busy)
            sg = 1.0 if dr == 0 else -1.0
            a3 = AC.do(lambda e: e.activation(e0.t[:, :], dd.t[:, :], ACT.Exp, scale=sg), d3, e0.busy)
            a4 = AC.do(lambda e: e.activation(e1.t[:, :], dd.t[:, :], ACT.Exp, scale=-sg), d3, e1.busy)
            d4 = DV.do(lambda e: e.tensor_tensor(qi.t[:, :], Q[:, h, :], e0.t[:, :], ALU.mult), a3, qm, qi.busy)
            d5 = DV.do(lambda e: e.tensor_tensor(ki.t[:, :], kk.t[:, :], e1.t[:, :], ALU.mult), a4, k1, ki.busy)
            d6 = DV.do(lambda e: e.tensor_tensor(c3(dd.t), tot, c3(base_.t), ALU.subtract), a3, a4)
            a5 = AC.do(lambda e: e.activation(e0.t[:, :], base_.t[:, :], ACT.Exp), d4, base_m)
            a6 = AC.do(lambda e: e.activation(e1.t[:, :], dd.t[:, :], ACT.Exp), d5, d6)
            dd.busy = [a6]
            lg.busy = pf.busy = [a5, a6, a2, d6]
            eq, ek = (e0, e1) if dr == 0 else (e1, e0)
            d7 = DV.do(lambda e: e.tensor_tensor(kd.t[:, :], kk.t[:, :], ek.t[:, :], ALU.mult), a5, a6, kd.busy)
            kk.busy = [d7]
            b = BANKS.next()
            PE.wait(d4, d5, b.busy)
            for n in range(4):
                p0 = 64 * (n % 2)
                f = lambda e, n=n, p0=p0: e.matmul(
                    b.t[p0:p0 + 64, (n // 2) * 64:(n // 2) * 64 + 64], ki.t[:, n * 64:n * 64 + 64],
                    qi.t[:, n * 64:n * 64 + 64], start=True, stop=True)
                m = PE.do(f) if n == 3 else PE.quiet(f)
            ki.busy = [m]
            sc = pool["Sc"].next()
            c = AC.do(lambda e: e.activation(sc.t[:, 0:P], b.t[:, 0:P], ACT.Copy), m, sc.busy)
            b.busy = [c]
            d8 = DV.do(lambda e: e.tensor_tensor(qi.t[:, :], Q[:, h, :], eq.t[:, :], ALU.mult), m, a5, a6)
            e0.busy = e1.busy = [d7, d8]
            for p0 in (0, 64):
                v = sc.t[p0:p0 + 64, 0:P].rearrange("p (a b) -> p a b", a=2)
                s_ = 1 if dr == 0 else -1
                g = PO.do(lambda e, v=v, s_=s_: e.affine_select(
                    out=v, in_=v, compare_op=ALU.is_ge, fill=0.0, base=0, pattern=[[0, 2], [s_, 64]],
                    channel_multiplier=-s_), c)
            kt, m, c = transpose2(kd.t, [d7])
            kd.busy = [m]
            b2 = [BANKS.next(), BANKS.next()]
            PE.wait(c, b2[0].busy, b2[1].busy, vm)
            adds = [0, 1, 2] if dr == 0 else [3, 2, 1]
            for z, n in enumerate(adds):
                p0, t = 64 * (n % 2), n // 2
                f = lambda e, z=z, p0=p0, t=t: e.matmul(
                    b2[z % 2].t[:, z * P:(z + 1) * P], kt.t[p0:p0 + 64, t * P:(t + 1) * P],
                    VTX[p0:p0 + 64, t, h * P:(h + 1) * P], start=True, stop=True)
                m = PE.do(f) if z == 2 else PE.quiet(f)
            kt.busy = [m]
            ss = SST.next()
            prev, pm = S0[:, i, :], s0m[i]
            for z, n in enumerate(adds):
                pm = DV.do(lambda e, z=z, n=n, prev=prev: e.scalar_tensor_tensor(
                    ss.t[:, z, :], prev, av[:, n:n + 1], b2[z % 2].t[:, z * P:(z + 1) * P], ALU.mult, ALU.add),
                    m, pm, a2, ss.busy)
                prev = ss.t[:, z, :]
            b2[0].busy = b2[1].busy = [pm]
            unit_busy[i % 2] = [pm, d3]
            return dict(g=g, sc=sc, d8=d8, qi=qi, ss=ss, pm=pm, dr=dr, h=h, i=i)

        unit_busy = [[], []]

        def finish_head(h, us):
            b2 = [BANKS.next(), BANKS.next()]
            PE.wait(b2[0].busy, b2[1].busy, [u["g"] for u in us], [u["d8"] for u in us], [u["pm"] for u in us])
            for n in range(4):
                p0, t = 64 * (n % 2), n // 2
                o_ = b2[n % 2].t[:, t * 64:t * 64 + 64]
                for u in us:
                    PE.quiet(lambda e, u=u, p0=p0, t=t, o_=o_: e.matmul(
                        o_, VTX[p0:p0 + 64, t, h * P:(h + 1) * P], u["sc"].t[p0:p0 + 64, t * 64:t * 64 + 64],
                        start=(u["dr"] == 0), stop=False))
                for u in us:
                    z = n if u["dr"] == 0 else 3 - n
                    st = S0[:, u["i"], :] if z == 0 else u["ss"].t[:, z - 1, :]
                    f = lambda e, u=u, st=st, n=n, o_=o_: e.matmul(
                        o_, st, u["qi"].t[:, n * 64:n * 64 + 64], start=False, stop=(u["dr"] == 1))
                    m = PE.do(f) if (n == 3 and u["dr"]) else PE.quiet(f)
            for u in us:
                u["sc"].busy = u["qi"].busy = u["ss"].busy = [m]
            for z in range(2):
                c = DV.do(lambda e: e.tensor_copy(
                    O[:, h, :].rearrange("p (t z c) -> p t z c", t=2, z=2)[:, :, z, :],
                    b2[z].t[:, 0:P].rearrange("p (t c) -> p t c", t=2)), m)
                b2[z].busy = [c]
            om[h] = c

        fc_read = [s0m[i] for i in range(8)]
        ogm, um, gam, gbm = [], [], [], []
        fillers = [lambda c=c: ogm.append(plain(OG, "win", 2 * c, fc_read)) for c in range(2)]
        fillers += [lambda c=c: um.append(plain(UU, "win", 2 * c, fc_read)) for c in range(2)]
        fillers += [lambda: mods(1)] * 8
        fillers += [lambda c=c: gam.append(plain(GA, "win", 2 * c, [ctx_read])) for c in range(4)]
        fillers += [lambda c=c: gbm.append(plain(GB, "win", 2 * c, [ctx_read])) for c in range(4)]
        pend = None
        for h in range(4):
            us = []
            for dr in range(2):
                us.append(x_unit(h, dr))
                for _ in range(2):
                    if fillers:
                        fillers.pop(0)()
            finish_head(h, us)
        for f in fillers:
            f()
        barrier()

        AH = ph("AH", 0, [P, 8, T], F32R)
        AL = ph("AL", 8, [P, 8, T], F32R)
        for h in range(4):
            n = Norm()
            n.add(O[:, h, :], om[h])
            rb, rt, rm_, _ = n.finish(P)
            om[h] = DV.do(lambda e, h=h, rb=rb: e.scalar_tensor_tensor(
                O[:, h, :], O[:, h, :], SM[:, S_GNA:S_GNA + 1], rb.t[:, :], ALU.mult, ALU.mult), rm_, om[h])
            rb.busy = [om[h]]
        SG = ph("SG", 80, [P, 4, T])
        m = AC.do(lambda e: e.activation(SG[:, :, :], OG[:, :, :], ACT.Sigmoid))
        m3 = AC.do(lambda e: e.activation(GA[:, :, :], GA[:, :, :], ACT.Sigmoid))
        m3 = AC.do(lambda e: e.activation(GB[:, :, :], GB[:, :, :], ACT.Sigmoid))
        d = DV.do(lambda e: e.tensor_tensor(SG[:, :, :], SG[:, :, :], OG[:, :, :], ALU.mult), m)
        d = DV.do(lambda e: e.tensor_tensor(O[:, :, :], O[:, :, :], SG[:, :, :], ALU.mult), d, om[3])
        ah, al = halves_of(O[:, :, :], AH[:, 0:4, :], AL[:, 0:4, :], d)

        GV = ph("GV", 84, [P, 2, 512])
        GU = ph("GU", 88, [P, 4, T])
        ST = ph("ST", 92, [P, 24])
        m = AC.do(lambda e: e.activation(GV[:, :, :], VB[:, :, :], ACT.Gelu_apprx_tanh))
        m2 = AC.do(lambda e: e.activation(GU[:, :, :], UU[:, :, :], ACT.Gelu_apprx_tanh))
        for t in range(2):
            d = DV.do(lambda e, t=t: e.bn_stats(ST[:, 6 * t:6 * t + 6], GV[:, t, :]), m)
            d = DV.do(lambda e, t=t: e.bn_aggr(ST[:, 12 + 2 * t:14 + 2 * t], ST[:, 6 * t:6 * t + 6]), d)
        m = AC.do(lambda e: e.activation(ST[:, 16:18], ST[:, 13:17:2], ACT.Sqrt, bias=epsb, scale=1.0), d)
        d = DV.do(lambda e: e.reciprocal(ST[:, 18:20], ST[:, 16:18]), m)
        for t in range(2):
            d1 = DV.do(lambda e, t=t: e.tensor_scalar(GV[:, t, :], GV[:, t, :], ST[:, 12 + 2 * t:13 + 2 * t],
                                                      ST[:, 18 + t:19 + t], ALU.subtract, ALU.mult), d)
            d1 = DV.do(lambda e, t=t: e.tensor_tensor(GV[:, t, :], GV[:, t, :], ROW[:, 0, :], ALU.mult), d1)
            d1 = DV.do(lambda e, t=t: e.tensor_tensor(GV[:, t, :], GV[:, t, :], ROW[:, 1, :], ALU.add), d1)
        for g in range(4):
            b = BANKS.next()
            PE.wait(d1, b.busy)
            for n in range(2):
                f = lambda e, n=n, g=g: e.matmul(b.t[:, n * P:(n + 1) * P], GV[:, n, g * P:(g + 1) * P],
                                                 WST[:, g, :], start=True, stop=True)
                m = PE.do(f) if n else PE.quiet(f)
            ta = TA.next()
            d2 = DV.do(lambda e, g=g: e.tensor_tensor(
                ta.t[:, :].rearrange("p (a b) -> p a b", a=2), b.t[:, 0:T].rearrange("p (a b) -> p a b", a=2),
                ROW[:, 2, g * P:(g + 1) * P].unsqueeze(1).to_broadcast([P, 2, P]), ALU.add), m, ta.busy)
            b.busy = [d2]
            d2 = DV.do(lambda e, g=g: e.tensor_tensor(GU[:, g, :], GU[:, g, :], ta.t[:, :], ALU.mult), d2, m2)
            ta.busy = [d2]
        bh, bl = halves_of(GU[:, :, :], AH[:, 4:8, :], AL[:, 4:8, :], d2)

        MG = ph("MG", 32, [P, 8, T])
        MH = ph("MH", 48, [P, 8, T], F32R)
        ML = ph("ML", 56, [P, 8, T], F32R)
        for which, (kind, g_, rd) in enumerate((("wpa", GA, [ah, al]), ("wpb", GB, [bh, bl]))):
            for c in range(2):
                j, w, wl, wm = take(kind)
                for t2 in range(2):
                    b = BANKS.next()
                    for t in range(2):
                        col = (2 * t2 + t) * P
                        m = project(w, wl, lambda k, col=col: (k * 512 + col, k * 512 + col + P), 4,
                                    AH[:, 4 * which:4 * which + 4, :], AL[:, 4 * which:4 * which + 4, :],
                                    b.t[:, t * T:(t + 1) * T], [wm, rd, b.busy])
                    mt = 4 * c + 2 * t2
                    v = b.t[:, :].rearrange("p (a b) -> p a b", a=2)
                    if which == 0:
                        d = DV.do(lambda e, mt=mt, v=v: e.tensor_tensor(MG[:, mt:mt + 2, :], v, GA[:, mt:mt + 2, :],
                                                                        ALU.mult), m, m3)
                        b.busy = [d]
                    else:
                        d = DV.do(lambda e, mt=mt, v=v: e.tensor_tensor(GB[:, mt:mt + 2, :], v, GB[:, mt:mt + 2, :],
                                                                        ALU.mult), m, m3)
                        b.busy = [d]
                        d = DV.do(lambda e, mt=mt: e.tensor_tensor(MG[:, mt:mt + 2, :], MG[:, mt:mt + 2, :],
                                                                   GB[:, mt:mt + 2, :], ALU.add), d)
                        mh, ml = halves_of(MG[:, mt:mt + 2, :], MH[:, mt:mt + 2, :], ML[:, mt:mt + 2, :], d)
                done(j)
                pump()

        n2 = Norm()
        for c in range(4):
            j, b, ms = pair("wo", MH, ML, [mh, ml])
            done(j)
            for t in range(2):
                mt = 2 * c + t
                d = DV.do(lambda e, mt=mt, t=t: e.scalar_tensor_tensor(
                    X[:, mt, :], b.t[:, t * T:(t + 1) * T], MOD[:, 16 + mt, 0:1], X[:, mt, :], ALU.mult, ALU.add),
                    ms[t])
                n2.add(X[:, mt, :], d)
            b.busy = [d]
            pump()
        vf = scale_of(40, S_GFFN, 32, 0, [])
        r2 = n2.finish(D)
        barrier()
        XH = ph("XH", 0, [P, KD, T], F32R)
        XL = ph("XL", 8, [P, KD, T], F32R)
        GH = ph("GH", 16, [P, FT, T], F32R)
        GL = ph("GL", 38, [P, FT, T], F32R)
        FG = ph("FG", 60, [P, KD, T])
        hx2 = modulated(X, r2, 40, 24, 0, XH, XL, [vf])
        r2[0].busy = [hx2]

        def ffn_up(kind, ready, rb, rbm):
            last = None
            for c in range(FT):
                j, b, ms = pair(kind, XH, XL, ready)
                done(j)
                ta, tb, tc = TA.next(), TB.next(), TC.next()
                gate, up = b.t[:, 0:T], b.t[:, T:2 * T]
                if rb is None:
                    s1 = AC.do(lambda e: e.activation(tb.t[:, :], gate, ACT.Silu), ms[0], tb.busy)
                    rest = [s1]
                    d = DV.do(lambda e: e.tensor_tensor(tc.t[:, :], up, tb.t[:, :], ALU.mult), s1, ms[1], tc.busy)
                    tb.busy = [d]
                else:
                    g = DV.do(lambda e: e.tensor_tensor(ta.t[:, :], gate, rb.t[:, :], ALU.mult), ms[0], ta.busy, rbm)
                    s1 = AC.do(lambda e: e.activation(tb.t[:, :], ta.t[:, :], ACT.Silu), g, tb.busy)
                    s2 = PO.do(lambda e: e.tensor_tensor(ta.t[:, :], tb.t[:, :], rb.t[:, :], ALU.mult), s1, rbm)
                    d = DV.do(lambda e: e.tensor_tensor(tc.t[:, :], up, ta.t[:, :], ALU.mult), s2, ms[1], tc.busy)
                    ta.busy = [d]
                    tb.busy = [s2]
                b.busy = [d]
                h, low = halves_of(tc.t[:, :], GH[:, c, :], GL[:, c, :], d)
                tc.busy = [h, low]
                last = [h, low]
                pump()
            if rb is not None:
                rb.busy = [PO.mark, DV.mark]
            return last

        def ffn_down(kind, ready, each):
            for mt in range(KD):
                b = BANKS.next()
                for half in range(2):
                    j, w, wl, wm = take(kind)
                    for k in range(11):
                        kk = 11 * half + k
                        m = mm3(b.t[:, 0:T], w[:, k * P:(k + 1) * P], wl[:, k * P:(k + 1) * P], GH[:, kk, :],
                                GL[:, kk, :], kk == 0, kk == 21, k == 10, [wm, ready, b.busy] if k == 0 else ())
                    done(j)
                    if half == 0:
                        pump()
                each(mt, b, m)
                pump()

        up_ready = ffn_up("up", hx2, None, None)
        nf = Norm()

        def after_first(mt, b, m):
            d = DV.do(lambda e: e.scalar_tensor_tensor(X[:, mt, :], b.t[:, 0:T], MOD[:, 40 + mt, 0:1], X[:, mt, :],
                                                       ALU.mult, ALU.add), m)
            b.busy = [d]
            nf.add(X[:, mt, :], d)

        ffn_down("down", up_ready, after_first)

        def G2(layer, i, k):
            c = S_NG2 + (layer * 6 + i) * 8 + k
            return SM[:, c:c + 1]

        def G2H(layer, i, k):
            c = (layer * 6 + i) * 8 + k
            return NG2H[:, c:c + 1]

        def next_halves(k, layer, i, d):
            h = AC.do(lambda e: e.activation(XH[:, k, :], X[:, k, :], ACT.Copy, scale=G2(layer, i, k)), d)
            return DV.do(lambda e: e.scalar_tensor_tensor(XL[:, k, :], X[:, k, :], G2(layer, i, k),
                                                          XH[:, k, :].bitcast(F32), ALU.mult, ALU.subtract), h)

        r = nf.finish(D)
        n2 = Norm()
        xs = []
        for k in range(KD):
            d = DV.do(lambda e, k=k: e.scalar_tensor_tensor(X[:, k, :], X[:, k, :], SM[:, S_GFIN + k:S_GFIN + k + 1],
                                                            r[0].t[:, :], ALU.mult, ALU.mult), r[2])
            xs.append(next_halves(k, 0, 0, d))
            n2.add(X[:, k, :], d)
        r[0].busy = [d]

        def collect(layer, i, half):
            n = Norm()
            marks = {}

            def each(mt, src, m):
                g = G2H(layer, i, mt) if half else G2(layer, i, mt)
                marks[mt] = AC.do(lambda e: e.activation(FG[:, mt, :], src, ACT.Copy, scale=g), m)
                marks["sq"] = n.add(src, m)
                return [marks[mt], marks["sq"]]

            return n, marks, each

        def residual(n, marks, layer, i):
            rb, _, rbm, _ = n.finish(D)
            nn = Norm() if layer is not None else None
            last = []
            for k in range(KD):
                ta = TA.next()
                d = DV.do(lambda e, k=k: e.tensor_tensor(ta.t[:, :], FG[:, k, :], rb.t[:, :], ALU.mult), rbm, marks[k],
                          ta.busy)
                d = DV.do(lambda e, k=k: e.tensor_tensor(X[:, k, :], X[:, k, :], ta.t[:, :], ALU.add), d)
                ta.busy = [d]
                if layer is not None:
                    last.append(next_halves(k, layer, i, d))
                    nn.add(X[:, k, :], d)
                else:
                    last.append(d)
            rb.busy = [d]
            return nn, last

        def ffn2(layer, first, xs, n2):
            rb, _, rbm, _ = n2.finish(D)
            rd = ffn_up("up2", xs[-1], rb, rbm)
            n, marks, each = collect(layer, 1 if first else 5, True)

            def f(mt, b, m):
                b.busy = each(mt, b.t[:, 0:T], m)

            ffn_down("down2", rd, f)
            return n, marks

        def project_out(kind, AHt, ALt, rd, layer):
            n, marks, each = collect(layer, 3, False)
            for c in range(4):
                j, b, ms = pair(kind, AHt, ALt, rd)
                done(j)
                for t in range(2):
                    b.busy = each(2 * c + t, b.t[:, t * T:(t + 1) * T], ms[1])
                pump()
            return n, marks

        n, marks = ffn2(0, True, xs, n2)
        n2, xs = residual(n, marks, 0, 2)
        barrier()
        rb, rt, rbm, rtm = n2.finish(D)
        VT = ph("VT", 16, [P, 2, 1024])
        OH = ph("OH", 24, [P, 8, T], F32R)
        OL = ph("OL", 32, [P, 8, T], F32R)
        QK = Turn([Slot(ph(f"QK{i}", 40 + 2 * i, [P, 2, T])) for i in range(2)])
        AB = Turn([Slot(ph(f"AB{i}", 44 + 1.5 * i, [P, 384])) for i in range(2)])
        LNB = Turn([Slot(ph(f"LNB{i}", 47 + 1.5 * i, [P, 384])) for i in range(2)])
        SPB = Turn([Slot(ph(f"SPB{i}", 50 + 1.5 * i, [P, 384])) for i in range(2)])
        AW = Turn([Slot(ph(f"AW{i}", 53 + 1.5 * i, [P, 384])) for i in range(2)])
        NU = at("NU", [P, 2, P], PB + 57 * KB)
        nu = DV.do(lambda e: e.tensor_scalar(NU[:, 0, :], TRI, -1.0, None, ALU.mult))
        nu = DV.do(lambda e: e.tensor_scalar(NU[:, 1, :], ONE, -1.0, None, ALU.mult))
        vts = []
        for c in range(4):
            j, w, wl, wm = take("sbv")
            b = BANKS.next()
            for t in range(2):
                m = tokens(w, wl, XH, XL, KD, t, b.t[:, t * T:(t + 1) * T], c256, [wm, xs[-1], b.busy])
            done(j)
            for t in range(2):
                v = AC.do(lambda e, c=c, t=t: e.activation(VT[:, t, c * 256:(c + 1) * 256], b.t[:, t * T:(t + 1) * T],
                                                           ACT.Copy, scale=rt.t[:, t:t + 1]), m, rtm)
            b.busy = [v]
            vts.append(v)
            pump()
        rt.busy = [v]

        def sb_front(qk, e_, ready):
            p0 = 64 * e_
            b = BANKS.next()
            kT = lambda t: qk.t[p0:p0 + 64, 1, t * P:(t + 1) * P]
            PE.wait(ready, b.busy)
            PE.quiet(lambda e: e.matmul(b.t[:, 0:256], kT(0), qk.t[p0:p0 + 64, 0, :], start=True, stop=False,
                                        skip_group_check=True))
            m = PE.do(lambda e: e.matmul(b.t[:, 256:384], kT(1), qk.t[p0:p0 + 64, 0, P:T], start=False, stop=False,
                                         skip_group_check=True))
            ab, ln, sp = AB.next(), LNB.next(), SPB.next()
            z = b.t[:, 0:384]
            s1 = AC.do(lambda e: e.activation(ab.t[:, :], z, ACT.Abs), m, ab.busy)
            s2 = AC.do(lambda e: e.activation(ab.t[:, :], ab.t[:, :], ACT.Exp, scale=-1.0), s1)
            s3 = AC.do(lambda e: e.activation(ln.t[:, :], ab.t[:, :], ACT.Ln, bias=ONE[:, 0:1]), s2, ln.busy)
            ab.busy = [s3]
            d = DV.do(lambda e: e.scalar_tensor_tensor(sp.t[:, :], z, 0.0, ln.t[:, :], ALU.max, ALU.add), s3, sp.busy)
            ln.busy = [d]
            for o in (0, 256):
                g = PO.do(lambda e, o=o: e.affine_select(
                    out=sp.t[:, o:o + P], in_=sp.t[:, o:o + P], compare_op=ALU.is_gt, fill=0.0, base=0,
                    pattern=[[1, P]], channel_multiplier=-1), d)
            return b, sp, g, m

        def sb_mid(b, sp, g):
            PE.wait(g, nu)
            PE.quiet(lambda e: e.matmul(b.t[:, 0:256], NU[:, 0, :], sp.t[:, 0:256], start=False, stop=False,
                                        skip_group_check=True))
            PE.quiet(lambda e: e.matmul(b.t[:, 128:256], NU[:, 1, :], sp.t[:, 256:384], start=False, stop=False,
                                        skip_group_check=True))
            m = PE.do(lambda e: e.matmul(b.t[:, 256:384], NU[:, 0, :], sp.t[:, 256:384], start=False, stop=True,
                                         skip_group_check=True))
            sp.busy = [m]
            aw = AW.next()
            s = AC.do(lambda e: e.activation(aw.t[:, :], b.t[:, 0:384], ACT.Exp), m, aw.busy)
            b.busy = [s]
            for o in (0, 256):
                g = PO.do(lambda e, o=o: e.affine_select(
                    out=aw.t[:, o:o + P], in_=aw.t[:, o:o + P], compare_op=ALU.is_gt, fill=0.0, base=0,
                    pattern=[[1, P]], channel_multiplier=-1), s)
            return aw, g

        def sb_back(ob, h, aw, g):
            p0 = 64 * (h % 2)
            PE.wait(g, vts, ob.busy if h % 2 == 0 else [])
            v = lambda t: VT[:, t, h * 64:h * 64 + 64]
            PE.quiet(lambda e: e.matmul(ob.t[p0:p0 + 64, 0:256], v(0), aw.t[:, 0:256], start=True, stop=False,
                                        skip_group_check=True))
            m = PE.do(lambda e: e.matmul(ob.t[p0:p0 + 64, 128:256], v(1), aw.t[:, 256:384], start=False, stop=True,
                                         skip_group_check=True))
            aw.busy = [m]
            return m

        def heads_out(ob, pr, m):
            h = AC.do(lambda e: e.activation(OH[:, pr, :], ob.t[:, 0:T], ACT.Copy), m)
            low = DV.do(lambda e: e.tensor_tensor(OL[:, pr, :], ob.t[:, 0:T], OH[:, pr, :].bitcast(F32),
                                                  ALU.subtract), h)
            ob.busy = [low]
            return [h, low]

        for pr in range(8):
            j, b, ms = pair("sbqk", XH, XL, xs[-1])
            done(j)
            qk = QK.next()
            DV.do(lambda e: e.scalar_tensor_tensor(qk.t[:, 0, :], b.t[:, 0:T], 0.125, rb.t[:, :], ALU.mult, ALU.mult),
                  ms[1], qk.busy, rbm)
            d = DV.do(lambda e: e.tensor_tensor(qk.t[:, 1, :], b.t[:, T:2 * T], rb.t[:, :], ALU.mult))
            b.busy = [d]
            pump()
            fr = [sb_front(qk, e_, d) for e_ in range(2)]
            qk.busy = [fr[1][3]]
            md = [sb_mid(*f[0:3]) for f in fr]
            ob = BANKS.next()
            for e_ in range(2):
                m = sb_back(ob, 2 * pr + e_, *md[e_])
            oready = heads_out(ob, pr, m)
        rb.busy = [d]
        n, marks = project_out("sbo", OH, OL, oready, 0)
        n2, xs = residual(n, marks, 0, 4)
        barrier()
        n, marks = ffn2(0, False, xs, n2)
        n2, xs = residual(n, marks, 1, 0)

        n, marks = ffn2(1, True, xs, n2)
        n2, xs = residual(n, marks, 1, 2)
        barrier()
        rb, rt, rbm, rtm = n2.finish(D)
        VT1 = ph("VT1", 16, [P, 2, 1024])
        OH = ph("OH1", 24, [P, 8, T], F32R)
        OL = ph("OL1", 32, [P, 8, T], F32R)
        CQ = ph("CQ", 40, [P, 5, T])
        CH = ph("CH", 45, [P, 3, T], F32R)
        CL = ph("CL", 48, [P, 3, T], F32R)
        QF = ph("QF", 51, [P, 16, T])
        KF = ph("KF", 67, [P, 16, T])
        SW = Turn([Slot(ph(f"SW{i}", 83 + 4 * i, [P, 4, T])) for i in range(2)])
        SM_ = Turn([Slot(ph(f"SX{i}", 91 + 1.5 * i, [P, 384])) for i in range(3)])
        PT = Turn([Slot(ph(f"PT{i}", 96 + 1.5 * i, [P, 384])) for i in range(2)])
        MX = Turn([Slot(ph(f"MX{i}", 100 + 0.125 * i, [P, 8])) for i in range(4)])
        cq = []
        for c in range(3):
            j, w, wl, wm = take(f"mla{c}")
            wd = 256 if c < 2 else 128
            b = BANKS.next()
            for t in range(wd // P):
                m = project(w, wl, lambda k, t=t, wd=wd: (k * wd + t * P, k * wd + t * P + P), KD, XH, XL,
                            b.t[:, t * T:(t + 1) * T], [wm, xs[-1], b.busy])
            done(j)
            for t in range(wd // P):
                d = DV.do(lambda e, c=c, t=t: e.tensor_tensor(CQ[:, 2 * c + t, :], b.t[:, t * T:(t + 1) * T],
                                                              rb.t[:, :], ALU.mult), m, rbm)
                cq.append(d)
            b.busy = [d]
            pump()
        rb.busy = [d]
        nq = Norm()
        nq.add(CQ[:, 0, :], cq[0])
        nq.add(CQ[:, 1, :], cq[1])
        rq = nq.finish(256)
        nk = Norm()
        nk.add(CQ[:, 2, :], cq[2])
        rk = nk.finish(128)
        for t in range(3):
            g = SM[:, S_QN + t:S_QN + t + 1]
            rr = rq if t < 2 else rk
            ta = TA.next()
            d = DV.do(lambda e, t=t, g=g, rr=rr: e.scalar_tensor_tensor(ta.t[:, :], CQ[:, t, :], g, rr[0].t[:, :],
                                                                        ALU.mult, ALU.mult), rr[2], ta.busy)
            ch = halves_of(ta.t[:, :], CH[:, t, :], CL[:, t, :], d)
            ta.busy = [*ch]
            rr[0].busy = [d]
        R4 = slice(64, 96)
        swap = [(i + 16) % 32 for i in range(32)]

        def rotate(dst, n, marks, eng=None):
            sw = SW.next()
            d = DV.do(lambda e: e.stream_shuffle(sw.t[R4, 0:n, :], dst, swap), marks, sw.busy)
            d1 = DV.do(lambda e: e.tensor_tensor(sw.t[R4, 0:n, :], sw.t[R4, 0:n, :],
                                                 SIN[R4, :].unsqueeze(1).to_broadcast([32, n, T]), ALU.mult), d, rope)
            d2 = DV.do(lambda e: e.tensor_tensor(dst, dst, COS[R4, :].unsqueeze(1).to_broadcast([32, n, T]), ALU.mult),
                       d)
            d3 = DV.do(lambda e: e.tensor_tensor(dst, dst, sw.t[R4, 0:n, :], ALU.add), d1, d2)
            sw.busy = [d3]
            return d3

        kr = rotate(CQ[R4, 3:4, :], 1, cq[3])
        krc = AC.do(lambda e: e.activation(KF[R4, :, :], CQ[R4, 3, :].unsqueeze(1).to_broadcast([32, 16, T]),
                                           ACT.Copy), kr)
        j, w, wl, wm = take("mlakv")
        kfm = {}
        for h2 in range(8):
            b = BANKS.next()
            for e_ in range(2):
                h = 2 * h2 + e_
                m = mm3(b.t[:, e_ * T:(e_ + 1) * T], w[:, h * P:(h + 1) * P], wl[:, h * P:(h + 1) * P],
                        CH[:, 2, :], CL[:, 2, :], True, True, True, [wm, ch, b.busy])
            c = AC.do(lambda e, h2=h2: e.activation(KF[0:64, 2 * h2:2 * h2 + 2, :],
                                                    b.t[0:64, :].rearrange("p (a b) -> p a b", a=2), ACT.Copy), m)
            b.busy = [c]
            kfm[h2] = c
        vts = []
        for t in range(2):
            for g in range(4):
                b = BANKS.next()
                vv = lambda w_, g=g: w_[:, g * 512:(g + 1) * 512].rearrange("p (a b) -> p a b", a=4)[:, :, 64:128]
                m = mm3(b.t[:, 0:256].rearrange("p (a b) -> p a b", a=4), CH[:, 2, t * P:(t + 1) * P],
                        CL[:, 2, t * P:(t + 1) * P], vv(w), vv(wl), True, True, True, [b.busy])
                c = DV.do(lambda e, t=t, g=g: e.tensor_copy(VT1[:, t, g * 256:(g + 1) * 256], b.t[:, 0:256]), m)
                b.busy = [c]
                vts.append(c)
        done(j)
        pump()
        MSC = 1.0 / 96 ** 0.5
        qfm = {}

        def mla_q(c):
            j, w, wl, wm = take("mlaq")
            for h2 in range(4):
                b = BANKS.next()
                for e_ in range(2):
                    o = (2 * h2 + e_) * 96
                    m = project(w, wl, lambda k, o=o: (k * 768 + o, k * 768 + o + 96), 2, CH, CL,
                                b.t[0:96, e_ * T:(e_ + 1) * T], [wm, b.busy])
                hh = 8 * c + 2 * h2
                q = AC.do(lambda e, hh=hh: e.activation(QF[0:96, hh:hh + 2, :],
                                                        b.t[0:96, :].rearrange("p (a b) -> p a b", a=2), ACT.Copy), m)
                b.busy = [q]
                if h2 % 2:
                    r_ = rotate(QF[R4, hh - 2:hh + 2, :], 4, q)
                    for x in range(hh - 2, hh + 2):
                        qfm[x] = [r_, q]
            done(j)
            pump()

        def mla_front(h):
            b = BANKS.next()
            PE.wait(qfm[h], kfm[h // 2], krc, b.busy)
            PE.quiet(lambda e: e.matmul(b.t[:, 0:128], QF[0:96, h, 0:P], KF[0:96, h, 0:P], start=True, stop=True))
            m = PE.do(lambda e: e.matmul(b.t[:, 128:384], QF[0:96, h, P:T], KF[0:96, h, :], start=True, stop=True))
            sx, mx = SM_.next(), MX.next()
            d = DV.do(lambda e: e.tensor_tensor(sx.t[:, 0:128], b.t[:, 0:128], NEGM[:, 128:256], ALU.add), m, sx.busy)
            d = DV.do(lambda e: e.tensor_tensor(sx.t[:, 128:384], b.t[:, 128:384], NEGM, ALU.add))
            b.busy = [d]
            DV.do(lambda e: e.tensor_reduce(mx.t[:, 0:1], sx.t[:, 0:128], AX, ALU.max), d, mx.busy)
            d = DV.do(lambda e: e.tensor_reduce(mx.t[:, 1:2], sx.t[:, 128:384], AX, ALU.max))
            d = DV.do(lambda e: e.tensor_scalar(mx.t[:, 2:4], mx.t[:, 0:2], -MSC, None, ALU.mult), d)
            AC.do(lambda e: e.activation(sx.t[:, 0:128], sx.t[:, 0:128], ACT.Exp, bias=mx.t[:, 2:3], scale=MSC,
                                         accum_out=mx.t[:, 4:5]), d)
            s = AC.do(lambda e: e.activation(sx.t[:, 128:384], sx.t[:, 128:384], ACT.Exp, bias=mx.t[:, 3:4], scale=MSC,
                                             accum_out=mx.t[:, 5:6]), d)
            d = DV.do(lambda e: e.reciprocal(mx.t[:, 6:8], mx.t[:, 4:6]), s)
            DV.do(lambda e: e.tensor_scalar(sx.t[:, 0:128], sx.t[:, 0:128], mx.t[:, 6:7], None, ALU.mult), d)
            d = DV.do(lambda e: e.tensor_scalar(sx.t[:, 128:384], sx.t[:, 128:384], mx.t[:, 7:8], None, ALU.mult))
            mx.busy = [d]
            return sx, d

        def mla_mid(sx, d):
            b = BANKS.next()
            PE.wait(d, b.busy)
            for z in range(3):
                f = lambda e, z=z: e.transpose(b.t[:, z * P:(z + 1) * P], sx.t[:, z * P:(z + 1) * P], IDN)
                m = PE.do(f) if z == 2 else PE.quiet(f)
            sx.busy = [m]
            pt = PT.next()
            c = AC.do(lambda e: e.activation(pt.t[:, :], b.t[:, 0:384], ACT.Copy), m, pt.busy)
            b.busy = [c]
            return pt, c

        def mla_back(ob, h, pt, c):
            p0 = 64 * (h % 2)
            PE.wait(c, vts, ob.busy if h % 2 == 0 else [])
            v = lambda t: VT1[:, t, h * 64:h * 64 + 64]
            PE.quiet(lambda e: e.matmul(ob.t[p0:p0 + 64, 0:256], v(0), pt.t[:, 0:256], start=True, stop=False,
                                        skip_group_check=True))
            m = PE.do(lambda e: e.matmul(ob.t[p0:p0 + 64, 128:256], v(1), pt.t[:, 256:384], start=False, stop=True,
                                         skip_group_check=True))
            pt.busy = [m]
            return m

        mla_q(0)
        fr = {0: mla_front(0), 1: mla_front(1)}
        mla_q(1)
        for pr in range(8):
            md = []
            for e_ in range(2):
                md.append(mla_mid(*fr.pop(2 * pr + e_)))
                if 2 * pr + 2 + e_ < 16:
                    fr[2 * pr + 2 + e_] = mla_front(2 * pr + 2 + e_)
            ob = BANKS.next()
            for e_ in range(2):
                m = mla_back(ob, 2 * pr + e_, *md[e_])
            oready = heads_out(ob, pr, m)
        n, marks = project_out("mlao", OH, OL, oready, 1)
        n2, xs = residual(n, marks, 1, 4)
        barrier()
        n, marks = ffn2(1, False, xs, n2)
        _, last = residual(n, marks, None, None)
        SP.quiet(lambda e: e.dma_start(out, X[:, :, :]).then_inc(s_out, 16), last)
        SP.wait((s_out, 16))


def kernel(**inputs):
    import numpy as np
    import concourse.bacc as _bacc
    from concourse.bass_utils import run_bass_kernel_spmd as _run

    g = {k: np.asarray(v) for k, v in inputs.items()}

    def con(a):
        return np.ascontiguousarray(a)

    def cols(w, n):
        K, N = w.shape
        return con(w.reshape(K // P, P, N // n, n).transpose(2, 1, 0, 3)).reshape(N // n, P, K // P * n)

    def paired(w):
        K, N = w.shape
        F = N // 2 // P
        return con(w.reshape(K // P, P, 2, F, P).transpose(3, 1, 0, 2, 4)).reshape(F, P, K // P * 2 * P)

    def down(w):
        return con(w.reshape(2, 11, P, KD, P).transpose(3, 0, 2, 1, 4)).reshape(16, P, 11 * P)

    def vec(v):
        return v.reshape(-1, P).T

    win = g["w_in"][0]
    AK = 512
    parts = [win[:, 0:3 * AK], win[:, 3 * AK:4 * AK], win[:, 6 * AK:7 * AK], win[:, 4 * AK:5 * AK],
             win[:, 5 * AK:6 * AK], win[:, 7 * AK:]]
    win = np.concatenate(parts, axis=1)
    cst = np.zeros((P, C_END), np.float32)
    cst[:, C_ID:C_ID + P] = np.eye(P)
    cst[:, C_ONE:C_ONE + P] = 1
    cst[:, C_TRI:C_TRI + P] = np.tril(np.ones((P, P)))
    cst[:, C_NEG + P:C_NEG + 2 * P] = np.triu(np.full((P, P), NEG), 1)
    inv = (np.float32(10000.0) ** (-np.arange(0, 32, 2, dtype=np.float32) / np.float32(32))).astype(np.float32)
    cst[:, C_INV] = np.tile(inv, 8)
    cst[:, C_SGN] = np.tile(np.repeat([-1.0, 1.0], 16), 4)
    cc = np.stack([vec(g["c"][0]), vec(g["c_ctx"])], axis=2).reshape(P, 16)
    small = np.concatenate(
        [cc, vec(g["b_mod"][0]), vec(g["g_mix"][0]), vec(g["g_ffn"][0]), vec(g["g_final"]), vec(g["g_norm_a"][0]),
         vec(g["lb_gamma"].reshape(-1)), vec(g["norm_g_2"].reshape(-1)), vec(g["mla_q_norm_2"][0]),
         vec(g["mla_kv_norm_2"][0])], axis=1)
    sb = g["sb_w_in_2"][0]
    mla = g["mla_w_in_2"][0]
    mla = np.concatenate([mla[:, 0:384]] + [mla[:, 384:416]] * 8, axis=1)
    wu2 = g["ffn_w_in_2"].reshape(4, D, 2 * FT * P)
    wd2 = g["ffn_w_out_2"].reshape(4, FT * P, D)
    arr = {
        "cst": cst,
        "small": small,
        "x": g["x"][0].T.reshape(KD, P, T).transpose(1, 0, 2),
        "ctx": g["ctx"][0].T.reshape(KD, P, T).transpose(1, 0, 2),
        "rows": np.concatenate([g["ln_v_g"], g["ln_v_b"], g["b_s"].reshape(1, 512)], axis=0),
        "wst": g["w_s"][0].transpose(2, 0, 1),
        "pos": g["positions_2"],
        "mod": cols(g["w_mod"][0], 256),
        "win": cols(win, 256),
        "wpa": cols(g["w_pa"][0], 512),
        "wpb": cols(g["w_pb"][0], 512),
        "wo": cols(g["w_o"][0], 256),
        "up": paired(g["w_up"][0]),
        "down": down(g["w_down"][0]),
        "up2": np.concatenate([paired(w) for w in wu2], axis=0),
        "down2": np.concatenate([down(w) for w in wd2], axis=0),
        "sbv": cols(sb[:, 2048:3072], 256),
        "sbqk": paired(sb[:, 0:2048]),
        "sbo": cols(g["sb_w_out_2"][0], 256),
        "mla0": cols(mla[:, 0:256], 256),
        "mla1": cols(mla[:, 256:512], 256),
        "mla2": cols(mla[:, 512:640], 128),
        "mlakv": cols(g["mla_w_ukv_2"][0], 2048),
        "mlaq": cols(g["mla_w_uq_2"][0], 768),
        "mlao": cols(g["mla_w_out_2"][0], 256),
    }
    nc = _bacc.Bacc("TRN2", target_bir_lowering=False, num_devices=1)
    arrays, aps = {}, {}
    for name, v in arr.items():
        v = con(v)
        arrays[f"in_{name}"] = v
        aps[name] = nc.dram_tensor(f"in_{name}", v.shape, mybir.dt.from_np(v.dtype), kind="ExternalInput").ap()
    o = nc.dram_tensor("out_0", (P, KD, T), F32, kind="ExternalOutput").ap()
    build(nc, aps, o)
    r = _run(nc, [arrays], core_ids=[0])
    y = r.results[0]["out_0"]
    return con(y.transpose(1, 0, 2).reshape(D, T).T).reshape(1, T, D)
```

```python
from contextlib import ExitStack

import concourse.bass as bass
from concourse import mybir

F32 = mybir.dt.float32
F32R = mybir.dt.float32r
I32 = mybir.dt.int32
ALU = mybir.AluOpType
ACT = mybir.ActivationFunctionType
AX = mybir.AxisListType.X

P = 128
T = 256
D = 1024
KD = D // P
FT = 22
EPS = 1e-6
NRAW = 3
NSPLIT = 3
SLOT = 2048
NEG = -1e30

C_ID, C_ONE, C_TRI, C_NEG, C_INV, C_SGN, C_END = 0, 128, 256, 384, 640, 641, 642
S_CC, S_BMOD, S_GMIX, S_GFFN, S_GFIN, S_GNA, S_LBG, S_NG2, S_QN, S_KVN, S_END = (
    0, 16, 64, 72, 80, 88, 89, 105, 201, 203, 204)


class Lane:

    def __init__(self, eng, sem):
        self.eng, self.sem, self.n, self.met = eng, sem, 0, {}

    def wait(self, *marks):
        for m in marks:
            if not m:
                continue
            if isinstance(m, list):
                self.wait(*m)
                continue
            sem, value = m
            if self.met.get(id(sem), 0) < value:
                self.met[id(sem)] = value
                self.eng.wait_ge(sem, value)

    def do(self, fn, *marks):
        self.wait(*marks)
        self.n += 1
        fn(self.eng).then_inc(self.sem, 1)
        return self.mark

    def quiet(self, fn, *marks):
        self.wait(*marks)
        fn(self.eng)

    @property
    def mark(self):
        return (self.sem, self.n)


class Slot:

    def __init__(self, t):
        self.t, self.busy = t, []


class Turn:
    def __init__(self, slots):
        self.slots, self.i = slots, 0

    def next(self):
        s = self.slots[self.i % len(self.slots)]
        self.i += 1
        return s


def weight_plan():
    plan = [("mod", i, 2048, True) for i in range(8)]
    plan += [("win", i, 2048, True) for i in range(10)]
    nxt = 8
    for i in range(10, 22):
        n = 2 if i < 14 else 1
        plan += [("mod", nxt + z, 2048, True) for z in range(n)]
        nxt += n
        plan += [("win", i, 2048, True)]
    plan += [("wpa", i, 2048, True) for i in range(2)] + [("wpb", i, 2048, True) for i in range(2)]
    plan += [("wo", i, 2048, True) for i in range(4)]
    plan += [("up", i, 2048, True) for i in range(FT)]
    plan += [("down", i, 1408, True) for i in range(16)]
    for layer in range(2):
        plan += [("up2", 2 * layer * FT + i, 2048, True) for i in range(FT)]
        plan += [("down2", 2 * layer * 16 + i, 1408, True) for i in range(16)]
        if layer == 0:
            plan += [("sbv", i, 2048, True) for i in range(4)]
            plan += [("sbqk", i, 2048, True) for i in range(8)]
            plan += [("sbo", i, 2048, True) for i in range(4)]
        else:
            plan += [("mla0", 0, 2048, True), ("mla1", 0, 2048, True)]
            plan += [("mla2", 0, 1024, True)]
            plan += [("mlakv", 0, 2048, True)]
            plan += [("mlaq", i, 1536, True) for i in range(2)]
            plan += [("mlao", i, 2048, True) for i in range(4)]
        plan += [("up2", (2 * layer + 1) * FT + i, 2048, True) for i in range(FT)]
        plan += [("down2", (2 * layer + 1) * 16 + i, 1408, True) for i in range(16)]
    return plan


def build(nc, a, out, stop=None):
    plan = weight_plan()
    ctx = ExitStack()
    with ctx:
        base = [nc.sbuf_base]

        def at(name, shape, off, dt=F32):
            return nc.alloc_sbuf_tensor_at(name, shape, dt, offset=off)

        def fixed(name, cols, dt=F32, shape=None):
            off = (base[0] + 31) // 32 * 32
            base[0] = off + cols * 4
            return at(name, shape or [P, cols], off, dt)

        def sem(name):
            return ctx.enter_context(nc.semaphore(name))

        CST = fixed("CST", C_END)
        SM = fixed("SM", S_END)
        X = fixed("X", KD * T, shape=[P, KD, T])
        RAW = [fixed(f"RAW{i}", SLOT) for i in range(NRAW)]
        WH = [fixed(f"WH{i}", SLOT, F32R) for i in range(NSPLIT)]
        WL = [fixed(f"WL{i}", SLOT, F32R) for i in range(NSPLIT)]
        SILC = fixed("SILC", 16)
        SILH = fixed("SILH", 32, F32R, [P, 8, 4])
        MOD = fixed("MOD", 96, shape=[P, 48, 2])
        VEC = fixed("VEC", 64)
        LBV = fixed("LBV", 48)
        NG2H = fixed("NG2H", 96)
        RT = Turn([Slot(fixed(f"RT{i}", 2)) for i in range(2)])
        RS = Turn([Slot(fixed(f"RS{i}", 2)) for i in range(2)])
        DG = Turn([Slot(fixed(f"DG{i}", T)) for i in range(2)])
        RB = Turn([Slot(fixed(f"RB{i}", T)) for i in range(2)])
        SQ = Turn([Slot(fixed(f"SQ{i}", T)) for i in range(3)])
        ACC = Turn([Slot(fixed(f"ACC{i}", T)) for i in range(2)])
        ss_at = (base[0] + 31) // 32 * 32
        TA = Turn([Slot(fixed(f"TA{i}", T)) for i in range(2)])
        TB = Turn([Slot(fixed(f"TB{i}", T)) for i in range(2)])
        TC = Turn([Slot(fixed(f"TC{i}", T)) for i in range(2)])
        COS = fixed("COS", T)
        SIN = fixed("SIN", T)
        PB = (base[0] + 31) // 32 * 32
        KB = 1024

        def ph(name, kb, shape, dt=F32):
            return at(name, shape, PB + int(kb * KB), dt)

        BANKS = Turn([Slot(ctx.enter_context(nc.psum_tensor(f"PS{i}", [P, 512], F32))) for i in range(8)])

        PE = Lane(nc.tensor, sem("s_pe"))
        AC = Lane(nc.scalar, sem("s_act"))
        DV = Lane(nc.vector, sem("s_dve"))
        PO = Lane(nc.gpsimd, sem("s_pool"))
        SP = Lane(nc.sync, sem("s_sp"))
        s_raw = [sem(f"s_raw{i}") for i in range(NRAW)]
        s_in = sem("s_in")
        s_out = sem("s_out")
        ins = [0]

        def load_small(dst, src, lane=AC, s=None):
            ins[0] += 16
            lane.quiet(lambda e, d=dst, r=src: e.dma_start(d, r).then_inc(s_in, 16))
            return (s_in, ins[0])

        IDN = CST[:, C_ID:C_ID + 128]
        ONE = CST[:, C_ONE:C_ONE + 128]
        TRI = CST[:, C_TRI:C_TRI + 128]
        NEGM = CST[:, C_NEG:C_NEG + 256]

        loaded, raw_slot, raw_free, order = {}, {}, {}, []
        split_slot, halves, consumed = {}, {}, {}
        nsplit = 0
        sidx = {}
        for j, (_, _, _, sp) in enumerate(plan):
            if sp:
                sidx[j] = nsplit
                nsplit += 1
        at_split = {v: k for k, v in sidx.items()}
        state = {"load": 0, "split": 0, "use": 0}

        def pump():
            moved = True
            while moved:
                moved = False
                j = state["load"]
                if j < len(plan) and (j < NRAW or (j - NRAW) in raw_free):
                    src, i, cols, _ = plan[j]
                    r = j % NRAW
                    SP.quiet(lambda e, r=r, c=cols, s=a[src][i]:
                             e.dma_start(RAW[r][:, 0:c], s).then_inc(s_raw[r], 16),
                             raw_free.get(j - NRAW))
                    loaded[j] = (s_raw[r], 16 * (j // NRAW + 1))
                    state["load"] += 1
                    moved = True
                s = state["split"]
                if s < nsplit:
                    j = at_split[s]
                    if j in loaded and (s < NSPLIT or (s - NSPLIT) in consumed):
                        free = consumed.get(s - NSPLIT)
                        c = plan[j][2]
                        r, h = RAW[j % NRAW], s % NSPLIT
                        for x0, x1 in ((0, c // 2), (c // 2, c)):
                            hi = AC.do(lambda e: e.activation(WH[h][:, x0:x1], r[:, x0:x1], ACT.Copy),
                                       loaded[j], free)
                            lo = DV.do(lambda e: e.tensor_tensor(
                                WL[h][:, x0:x1], r[:, x0:x1], WH[h][:, x0:x1].bitcast(F32), ALU.subtract),
                                hi, free)
                        halves[j] = (WH[h], WL[h], [hi, lo])
                        raw_free[j] = [hi, lo]
                        state["split"] += 1
                        moved = True

        def take(kind):
            j = state["use"]
            assert plan[j][0] == kind, (plan[j], kind)
            state["use"] += 1
            pump()
            if plan[j][3]:
                return j, *halves[j]
            return j, RAW[j % NRAW], None, [loaded[j]]

        def done(j):
            if plan[j][3]:
                consumed[sidx[j]] = PE.mark
            else:
                raw_free[j] = PE.mark

        def mm3(out_, lh, ll, rh, rl, first, last, signal, marks=()):
            PE.wait(*marks)
            PE.quiet(lambda e: e.matmul(out_, lh, rh, start=first, stop=False))
            PE.quiet(lambda e: e.matmul(out_, lh, rl, start=False, stop=False))
            f = lambda e: e.matmul(out_, ll, rh, start=False, stop=last)
            if signal:
                return PE.do(f)
            PE.quiet(f)
            return None

        def project(w, wl, cols, kt, xh, xl, out_, marks):
            for k in range(kt):
                lo, hi_ = cols(k)
                m = mm3(out_, w[:, lo:hi_], wl[:, lo:hi_], xh[:, k, :], xl[:, k, :], k == 0, k == kt - 1,
                        k == kt - 1, marks if k == 0 else ())
            return m

        def pair(kind, xh, xl, ready, kt=KD, marks=()):
            j, w, wl, wm = take(kind)
            b = BANKS.next()
            ms = []
            for t in range(2):
                ms.append(project(w, wl, lambda k, t=t: (k * 256 + t * 128, k * 256 + t * 128 + 128), kt, xh, xl,
                                  b.t[:, t * T:(t + 1) * T], [wm, ready, b.busy]))
            return j, b, [ms[1], ms[1]]

        def pairs_by_k(kind, n, xh, xl, ready):
            got = [take(kind) for _ in range(n)]
            banks = [BANKS.next() for _ in range(n)]
            for k in range(KD):
                for z, ((j, w, wl, wm), b) in enumerate(zip(got, banks)):
                    for t in range(2):
                        c = k * 256 + t * P
                        o_ = b.t[:, t * T:(t + 1) * T]
                        last = k == KD - 1
                        PE.wait(wm, ready[k], b.busy)
                        PE.quiet(lambda e: e.matmul(o_, w[:, c:c + P], xh[:, k, :], start=(k == 0 and t == 0),
                                                    stop=False, skip_group_check=True))
                        PE.quiet(lambda e: e.matmul(o_, w[:, c:c + P], xl[:, k, :], start=False, stop=False,
                                                    skip_group_check=True))
                        f = lambda e: e.matmul(o_, wl[:, c:c + P], xh[:, k, :], start=False, stop=last,
                                               skip_group_check=True)
                        if last and t == 1:
                            m = PE.do(f)
                            done(j)
                            b.done = m
                        else:
                            PE.quiet(f)
            return banks

        def barrier():
            marks = [PE.mark, AC.mark, DV.mark, PO.mark]
            for lane in (PE, AC, DV, PO):
                lane.wait(*marks)

        class Norm:

            def __init__(self, lane=DV):
                self.acc, self.n, self.last, self.lane = ACC.next(), 0, None, lane

            def add(self, src, marks):
                q = SQ.next() if self.n else self.acc
                dst = q.t
                m = AC.do(lambda e: e.activation(dst[:, 0:T], src, ACT.Square), marks, q.busy)
                if self.n:
                    acc = self.acc.t
                    self.last = self.lane.do(lambda e: e.tensor_tensor(acc[:, :], acc[:, :], dst[:, :], ALU.add),
                                             m, self.last)
                    q.busy = [self.last]
                else:
                    self.last = m
                self.n += 1
                return m

            def sums(self, dim):
                acc, b = self.acc.t, BANKS.next()
                self.b = b
                PE.wait(self.last, b.busy, const)
                for t in range(2):
                    f = lambda e: e.matmul(b.t[:, t:t + 1], acc[:, t * P:(t + 1) * P], ONE[:, 0:1],
                                           start=True, stop=True)
                    m = PE.do(f) if t else PE.quiet(f)
                self.acc.busy = [m]
                rs, self.rt, self.dg = RS.next(), RT.next(), DG.next()
                rt, dg = self.rt, self.dg
                self.m = AC.do(lambda e: e.activation(rs.t[:, :], b.t[:, 0:2], ACT.Sqrt, bias=EPSV, scale=1.0 / dim),
                               m, rs.busy)
                self.r = DV.do(lambda e: e.reciprocal(rt.t[:, :], rs.t[:, :]), self.m, rt.busy)
                rs.busy = [self.r]
                for t in range(2):
                    self.g = DV.do(lambda e: e.tensor_scalar(dg.t[:, t * P:(t + 1) * P], IDN, rt.t[:, t:t + 1], None,
                                                             ALU.mult), self.r, dg.busy)
                rt.busy = [self.r, self.g]

            def spread(self, copy=True):
                b, dg = self.b, self.dg
                m = PE.do(lambda e: e.matmul(b.t[:, 0:T], ONE, dg.t[:, :], start=True, stop=True), self.g, self.m)
                dg.busy = [m]
                if not copy:
                    return b, m
                rb = RB.next()
                m = AC.do(lambda e: e.activation(rb.t[:, :], b.t[:, 0:T], ACT.Copy), m, rb.busy)
                b.busy = [m]
                return rb, m

            def finish(self, dim):
                self.sums(dim)
                rb, m = self.spread()
                return rb, self.rt, m, self.r

        const = load_small(CST[:, :], a["cst"], SP)
        small = load_small(SM[:, :], a["small"], SP)
        XC = ph("XC", 80, [P, KD, T])
        cin = load_small(XC[:, :, :], a["ctx"], SP)
        xin = load_small(X[:, :, :], a["x"], SP)
        ROW = ph("ROW", 72, [P, 3, 512])
        WST = ph("WST", 78, [P, 4, P])
        EPSV = VEC[:, 60:61]
        PIV = VEC[:, 61:62]
        DV.do(lambda e: e.memset(EPSV, EPS))
        epsb = DV.do(lambda e: e.memset(PIV, 1.5707963267948966))
        AC.wait(epsb)
        pump()
        for lane in (AC, DV, PE):
            lane.wait(xin)
        for i in range(3):
            row = load_small(ROW[:, i, :], a["rows"][i:i + 1, :].to_broadcast([P, 512]))
        row = load_small(WST[:, :, :], a["wst"])

        def rope_tables():
            POS, ANG, NN, NM = (ph(n, 68 + i, [P, T], I32 if i == 0 else F32)
                                for i, n in enumerate(("POS", "ANG", "NN", "NM")))
            d = load_small(POS[:, :], a["pos"].to_broadcast([P, T]))
            d = DV.do(lambda e: e.tensor_copy(ANG[:, :], POS[:, :]), d)
            d = DV.do(lambda e: e.tensor_scalar(ANG[:, :], ANG[:, :], CST[:, C_INV:C_INV + 1], None, ALU.mult), d)
            d = DV.do(lambda e: e.tensor_scalar(NN[:, :], ANG[:, :], 0.15915494309189535, 12582912.0, ALU.mult,
                                                ALU.add), d)
            d = DV.do(lambda e: e.tensor_scalar(NM[:, :], NN[:, :], 12582912.0, None, ALU.subtract), d)
            for c in (6.28125, 0.0019340515136718750, 1.2556659146e-06):
                d = DV.do(lambda e: e.scalar_tensor_tensor(ANG[:, :], NM[:, :], -c, ANG[:, :], ALU.mult, ALU.add), d)
            d = DV.do(lambda e: e.tensor_scalar(ANG[:, :], ANG[:, :], 3.1415925, -3.1415925, ALU.min, ALU.max), d)
            m = AC.do(lambda e: e.activation(SIN[:, :], ANG[:, :], ACT.Sin), d)
            m2 = AC.do(lambda e: e.activation(NN[:, :], ANG[:, :], ACT.Abs), d)
            m2 = AC.do(lambda e: e.activation(COS[:, :], NN[:, :], ACT.Sin, bias=PIV, scale=-1.0), m2)
            return [DV.do(lambda e: e.tensor_scalar(SIN[:, :], SIN[:, :], CST[:, C_SGN:C_SGN + 1], None, ALU.mult), m),
                    m2]

        silc = AC.do(lambda e: e.activation(SILC[:, :], SM[:, S_CC:S_CC + 16], ACT.Silu))
        c2 = SILC[:, :].rearrange("p (k c) -> p k c", c=2)
        silc = AC.do(lambda e: e.activation(SILH[:, :, 0:2], c2, ACT.Copy), silc)
        silc = DV.do(lambda e: e.tensor_tensor(SILH[:, :, 2:4], c2, SILH[:, :, 0:2].bitcast(F32), ALU.subtract), silc)
        g2h = DV.do(lambda e: e.tensor_scalar(NG2H[:, :], SM[:, S_NG2:S_NG2 + 96], 0.5, None, ALU.mult))

        def mods(n):
            for _ in range(n):
                j, w, wl, wm = take("mod")
                i = plan[j][1]
                b = BANKS.next()
                PE.wait(wm, silc, b.busy)
                for t in range(2):
                    for k in range(KD):
                        c = k * 256 + t * P
                        PE.quiet(lambda e: e.matmul(b.t[:, 4 * t:4 * t + 4], w[:, c:c + P], SILH[:, k, :],
                                                    start=(k == 0), stop=False, skip_group_check=True))
                        f = lambda e: e.matmul(b.t[:, 4 * t:4 * t + 2], wl[:, c:c + P], SILH[:, k, 0:2],
                                               start=False, stop=(k == KD - 1), skip_group_check=True)
                        m = PE.do(f) if (t == 1 and k == KD - 1) else PE.quiet(f)
                done(j)
                v = b.t[:, 0:8].rearrange("p (a c b) -> p a c b", a=2, c=2)
                d = DV.do(lambda e: e.tensor_tensor(
                    MOD[:, 2 * i:2 * i + 2, :], v[:, :, 0, :],
                    SM[:, S_BMOD + 2 * i:S_BMOD + 2 * i + 2].unsqueeze(2).to_broadcast([P, 2, 2]), ALU.add), m)
                m = DV.do(lambda e: e.tensor_tensor(MOD[:, 2 * i:2 * i + 2, :], MOD[:, 2 * i:2 * i + 2, :],
                                                    v[:, :, 1, :], ALU.add), d)
                b.busy = [m]
                pump()
            return m

        g0 = SM[:, S_LBG:S_LBG + 8]
        g1 = SM[:, S_LBG + 8:S_LBG + 16]
        L = lambda i: LBV[:, 8 * i:8 * i + 8]
        d = DV.do(lambda e: e.tensor_tensor(L(0), g0, g1, ALU.max))
        DV.do(lambda e: e.tensor_tensor(L(1), g0, L(0), ALU.subtract), d)
        d = DV.do(lambda e: e.tensor_tensor(L(2), g1, L(0), ALU.subtract), d)
        m = AC.do(lambda e: e.activation(LBV[:, 8:24], LBV[:, 8:24], ACT.Exp), d)
        d = DV.do(lambda e: e.tensor_tensor(L(0), L(1), L(2), ALU.add), m)
        d = DV.do(lambda e: e.reciprocal(L(3), L(0)), d)
        d = DV.do(lambda e: e.tensor_tensor(L(4), L(1), L(3), ALU.mult), d)
        lbm = DV.do(lambda e: e.tensor_scalar(L(5), L(4), -1.0, 1.0, ALU.mult, ALU.add), d)
        LB = lambda i: LBV[:, 32 + i:33 + i]
        OMLB = lambda i: LBV[:, 40 + i:41 + i]

        HH = ph("HH", 0, [P, KD, T], F32R)
        HL = ph("HL", 8, [P, KD, T], F32R)
        HCH = ph("HCH", 16, [P, KD, T], F32R)
        HCL = ph("HCL", 24, [P, KD, T], F32R)

        def norm_of(src, marks):
            n = Norm()
            for k in range(KD):
                n.add(src[:, k, :], marks)
            return n.finish(D)

        rc = norm_of(XC, [])
        rx = norm_of(X, [])
        AC.quiet(lambda e: e.preload_act_table_set("sigmoid_and_others"))
        modm = mods(8)

        def scale_of(dst, gcol, mcol, which, marks):
            d = DV.do(lambda e: e.tensor_scalar(VEC[:, dst:dst + 8], MOD[:, mcol:mcol + 8, which], 1.0, None,
                                                ALU.add), marks)
            return DV.do(lambda e: e.tensor_tensor(VEC[:, dst:dst + 8], VEC[:, dst:dst + 8], SM[:, gcol:gcol + 8],
                                                   ALU.mult), d)

        va = scale_of(0, S_GMIX, 8, 0, modm)
        vc = scale_of(8, S_GMIX, 8, 1, modm)

        def halves_of(tmp, dh, dl, marks_h=(), marks_l=()):
            h = AC.do(lambda e: e.activation(dh, tmp, ACT.Copy), marks_h)
            low = DV.do(lambda e: e.tensor_tensor(dl, tmp, dh.bitcast(F32), ALU.subtract), h, marks_l)
            return [h, low]

        def modulated(src, r, av, mcol, which, dh, dl, marks):
            ready = []
            for k in range(KD):
                ta, tb = TA.next(), TB.next()
                d = DV.do(lambda e, k=k: e.scalar_tensor_tensor(ta.t[:, :], src[:, k, :], VEC[:, av + k:av + k + 1],
                                                                r[0].t[:, :], ALU.mult, ALU.mult), r[2], marks, ta.busy)
                d = DV.do(lambda e, k=k: e.tensor_scalar(tb.t[:, :], ta.t[:, :], MOD[:, mcol + k, which:which + 1], None,
                                                         ALU.add), d, tb.busy)
                ta.busy = [d]
                h, low = halves_of(tb.t[:, :], dh[:, k, :], dl[:, k, :], d)
                tb.busy = [h, low]
                ready.append(low)
            return ready[-1]

        hx = modulated(X, rx, 0, 0, 0, HH, HL, [va])
        hc = modulated(XC, rc, 8, 0, 1, HCH, HCL, [vc])
        rx[0].busy = [hx]
        rc[0].busy = [hc]

        FX = ph("FX", 32, [P, 8, T])
        FC = ph("FC", 40, [P, 8, T])
        VTX = ph("VTX", 48, [P, 2, 512])
        VTC = ph("VTC", 52, [P, 2, 512])
        Q = ph("Q", 56, [P, 4, T])
        VB = ph("VB", 60, [P, 2, 512])
        S0 = ph("S0", 64, [P, 8, P])
        O = ph("O", 68, [P, 4, T])
        GA = ph("GA", 16, [P, 8, T])
        GB = ph("GB", 24, [P, 8, T])
        OG = ph("OG", 40, [P, 4, T])
        UU = ph("UU", 44, [P, 4, T])

        fmark = {}
        for c in range(4):
            j, w, wl, wm = take("win")
            for src, (xh, xl, rd, dst) in enumerate(((HH, HL, hx, FX), (HCH, HCL, hc, FC))):
                b = BANKS.next()
                for t in range(2):
                    m = project(w, wl, lambda k, t=t: (k * 256 + t * 128, k * 256 + t * 128 + 128), KD, xh, xl,
                                b.t[:, t * T:(t + 1) * T], [wm, rd, b.busy])
                if src:
                    done(j)
                m = AC.do(lambda e, dst=dst, c=c: e.activation(
                    dst[:, 2 * c:2 * c + 2, :], b.t[:, :].rearrange("p (a b) -> p a b", a=2), ACT.Sigmoid), m)
                b.busy = [m]
                for t in range(2):
                    i = 2 * c + t
                    fmark[(src, i)] = DV.do(lambda e, dst=dst, i=i: e.tensor_scalar(
                        dst[:, i, :], dst[:, i, :], OMLB(i), LB(i), ALU.mult, ALU.add), m, lbm)
            pump()

        def tokens(w, wl, xh, xl, kt, t, out_, cols, marks):
            for k in range(kt):
                m = mm3(out_, xh[:, k, t * P:(t + 1) * P], xl[:, k, t * P:(t + 1) * P], cols(w, k), cols(wl, k),
                        k == 0, k == kt - 1, k == kt - 1, marks if k == 0 else ())
            return m

        c256 = lambda w, k: w[:, k * 256:k * 256 + 256]
        vm = []
        for c in range(2):
            j, w, wl, wm = take("win")
            for src, (xh, xl, rd, dst) in enumerate(((HH, HL, hx, VTX), (HCH, HCL, hc, VTC))):
                b = BANKS.next()
                for t in range(2):
                    m = tokens(w, wl, xh, xl, KD, t, b.t[:, t * T:(t + 1) * T], c256, [wm, rd, b.busy])
                if src:
                    done(j)
                m = AC.do(lambda e, dst=dst, c=c: e.activation(
                    dst[:, :, c * 256:(c + 1) * 256], b.t[:, :].rearrange("p (a b) -> p a b", a=2), ACT.Copy), m)
                b.busy = [m]
                vm.append(m)
            pump()
        ctx_read = PE.mark

        def plain(dst, kind, col, marks=()):
            j, b, ms = pair(kind, HH, HL, hx)
            done(j)
            m = AC.do(lambda e: e.activation(dst[:, col:col + 2, :], b.t[:, :].rearrange("p (a b) -> p a b", a=2),
                                             ACT.Copy), ms[1], marks)
            b.busy = [m]
            pump()
            return m

        def vb_chunk(c):
            j, w, wl, wm = take("win")
            b = BANKS.next()
            for t in range(2):
                m = tokens(w, wl, HH, HL, KD, t, b.t[:, t * T:(t + 1) * T], c256, [wm, b.busy])
            done(j)
            m = AC.do(lambda e: e.activation(VB[:, :, c * 256:(c + 1) * 256],
                                             b.t[:, :].rearrange("p (a b) -> p a b", a=2), ACT.Copy), m)
            b.busy = [m]
            pump()

        Lc = ph("Lc", 80, [P, 8, T])
        Pc = ph("Pc", 88, [P, 8, T])
        Kc = ph("Kc", 96, [P, 8, T])
        AC.quiet(lambda e: e.preload_act_table_set("natural_log_exp_and_others"))
        a1 = AC.do(lambda e: e.activation(Lc[:, :, :], FC[:, :, :], ACT.Ln), [fmark[(1, i)] for i in range(8)], hc)
        kc = DV.do(lambda e: e.tensor_scalar(FC[:, :, :], FC[:, :, :], -1.0, 1.0, ALU.mult, ALU.add), a1)
        for i in range(8):
            p1 = DV.do(lambda e: e.tensor_tensor_scan(Pc[:, i, :], ONE[:, 0:1].to_broadcast([P, T]), Lc[:, i, :], 0.0,
                                                      ALU.mult, ALU.add), a1)
        cx = []
        for i in range(4):
            d = DV.do(lambda e: e.tensor_scalar(Pc[:, i, :], Pc[:, i, :], -1.0, Pc[:, i, T - 1:T], ALU.mult, ALU.add), p1)
        a2 = AC.do(lambda e: e.activation(Pc[:, 0:4, :], Pc[:, 0:4, :], ACT.Exp), d)
        d = DV.do(lambda e: e.tensor_tensor(Pc[:, 4:8, :], Pc[:, 4:8, :], Lc[:, 4:8, :], ALU.subtract), p1)
        a3 = AC.do(lambda e: e.activation(Pc[:, 4:8, :], Pc[:, 4:8, :], ACT.Exp), d)
        cx.append(DV.do(lambda e: e.tensor_tensor(Pc[:, 0:4, :], Pc[:, 0:4, :], FC[:, 0:4, :], ALU.mult), a2, kc))
        cx.append(DV.do(lambda e: e.tensor_tensor(Pc[:, 4:8, :], Pc[:, 4:8, :], FC[:, 4:8, :], ALU.mult), a3))
        fc_read = cx[1]
        qm = [plain(Q, "win", 2 * c) for c in range(2)]

        def transposed(src, dst, hs, marks, busy=()):
            b = BANKS.next()
            PE.wait(marks, b.busy)
            for z in range(4):
                f = lambda e: e.transpose(b.t[:, z * P:(z + 1) * P],
                                          src[:, hs + z // 2, (z % 2) * P:(z % 2 + 1) * P], IDN)
                m = PE.do(f) if z == 3 else PE.quiet(f)
            c = AC.do(lambda e: e.activation(dst[:, hs:hs + 2, :], b.t[:, :].rearrange("p (a b) -> p a b", a=2),
                                             ACT.Copy), m, *busy)
            b.busy = [c]
            return c, m

        kcm = [transposed(Pc, Kc, 2 * z, cx[z // 2])[0] for z in range(4)]

        LG = ph("LG", 16, [P, 4, T])
        PF = ph("PF", 20, [P, 4, T])
        DD = ph("DD", 24, [P, 4, T])
        RM = ph("RM", 28, [P, T])
        E0 = ph("E0", 80, [P, 4, T])
        E1 = ph("E1", 84, [P, 4, T])
        QI = ph("QI", 88, [P, 4, T])
        KI = ph("KI", 92, [P, 4, T])
        KD_ = ph("KD_", 96, [P, 4, T])
        KT = ph("KT", 100, [P, 4, T])
        SC = ph("SC", 104, [P, 4, P])
        SS = at("SS", [P, 12, P], ss_at)
        AV = VEC[:, 24:40]
        HV = VEC[:, 44:60]
        rm = DV.do(lambda e: e.memset(RM[:, :], 1.0), ctx_read)
        rm = DV.do(lambda e: e.memset(RM[:, 0:T:64], 0.0), rm)
        use = {n: [] for n in ("lg", "pf", "dd", "e0", "e1", "qi", "ki", "kd", "kt", "sc", "ss", "av", "hv")}

        def c16(t):
            return t[:, :, :].rearrange("p h (n c) -> p (h n) c", c=64)

        def bc(v, n=64):
            return v.unsqueeze(2).to_broadcast([P, v.shape[1], n])

        def gla_terms(dr, first):
            u = {}
            hs = slice(4 * dr, 4 * dr + 4)
            F = FX[:, hs, :]
            a1 = AC.do(lambda e: e.activation(LG[:, :, :], F, ACT.Ln), [fmark[(0, i)] for i in range(8)], first,
                       use["lg"])
            k1 = DV.do(lambda e: e.tensor_scalar(F, F, -1.0, 1.0, ALU.mult, ALU.add), a1)
            for h in range(4):
                p1 = DV.do(lambda e: e.tensor_tensor_scan(PF[:, h, :], RM[:, :], LG[:, h, :], 0.0, ALU.mult, ALU.add),
                           a1, rm, use["pf"])
            tot = c16(PF)[:, :, 63]
            d1 = DV.do(lambda e: e.tensor_scalar(HV, tot, 0.5, None, ALU.mult), p1, use["hv"])
            a2 = AC.do(lambda e: e.activation(AV, tot, ACT.Exp), p1, use["av"])
            if dr:
                d2 = DV.do(lambda e: e.tensor_tensor(LG[:, :, :], PF[:, :, :], LG[:, :, :], ALU.subtract), p1)
                B_, bm = LG, d2
            else:
                B_, bm = PF, p1
            d3 = DV.do(lambda e: e.tensor_tensor(c16(DD), c16(B_), bc(HV), ALU.subtract), d1, bm, use["dd"])
            use["hv"] = [d3]
            sg = 1.0 if dr == 0 else -1.0
            a3 = AC.do(lambda e: e.activation(E0[:, :, :], DD[:, :, :], ACT.Exp, scale=sg), d3, use["e0"], first)
            a4 = AC.do(lambda e: e.activation(E1[:, :, :], DD[:, :, :], ACT.Exp, scale=-sg), d3, use["e1"])
            d4 = DV.do(lambda e: e.tensor_tensor(QI[:, :, :], Q[:, :, :], E0[:, :, :], ALU.mult), a3, qm, use["qi"])
            u["d5"] = DV.do(lambda e: e.tensor_tensor(KI[:, :, :], F, E1[:, :, :], ALU.mult), a4, k1, use["ki"])
            d6 = DV.do(lambda e: e.tensor_tensor(c16(DD), bc(tot), c16(B_), ALU.subtract), a3, a4)
            a5 = AC.do(lambda e: e.activation(E0[:, :, :], B_[:, :, :], ACT.Exp), d4, bm)
            a6 = AC.do(lambda e: e.activation(E1[:, :, :], DD[:, :, :], ACT.Exp), u["d5"], d6)
            use["dd"] = [a6]
            use["lg"] = use["pf"] = [a5, a6, a2, d6]
            eq, ek = (E0, E1) if dr == 0 else (E1, E0)
            u["d7"] = DV.do(lambda e: e.tensor_tensor(KD_[:, :, :], F, ek[:, :, :], ALU.mult), a5, a6, use["kd"], first)
            u.update(d4=d4, a2=a2, eq=eq, am=[a5, a6])
            return u

        def gla_scores(dr, u, first):
            b = BANKS.next()
            PE.wait(u["d4"], u["d5"], b.busy)
            for h in range(4):
                for n in range(4):
                    p0 = 64 * (n % 2)
                    c = h * P + (n // 2) * 64
                    f = lambda e: e.matmul(b.t[p0:p0 + 64, c:c + 64], KI[:, h, n * 64:n * 64 + 64],
                                           QI[:, h, n * 64:n * 64 + 64], start=True, stop=True)
                    m = PE.do(f) if (h == 3 and n == 3) else PE.quiet(f)
            use["ki"] = [m]
            c = AC.do(lambda e: e.activation(SC[:, :, :], b.t[:, :].rearrange("p (a b) -> p a b", a=4), ACT.Copy), m,
                      use["sc"], first)
            b.busy = [c]
            u["d8"] = DV.do(lambda e: e.tensor_tensor(QI[:, :, :], Q[:, :, :], u["eq"][:, :, :], ALU.mult), m, u["am"])
            use["e0"] = use["e1"] = [u["d7"], u["d8"]]
            s_ = 1 if dr == 0 else -1
            for p0 in (0, 64):
                v = SC[p0:p0 + 64, :, :].rearrange("p h (a b) -> p (h a) b", a=2)
                u["g"] = PO.do(lambda e: e.affine_select(out=v, in_=v, compare_op=ALU.is_ge, fill=0.0, base=0,
                                                         pattern=[[0, 8], [s_, 64]], channel_multiplier=-s_), c)
            for z in range(2):
                u["kt"], m = transposed(KD_, KT, 2 * z, u["d7"], (use["kt"], first))
            use["kd"] = [m]

        def gla_states(dr, u):
            b3 = [BANKS.next() for _ in range(3)]
            PE.wait(u["kt"], [b.busy for b in b3], vm)
            adds = [0, 1, 2] if dr == 0 else [3, 2, 1]

            def at_(h, z):
                return (b3[2], h * P) if z == 1 else (b3[h // 2], (2 * (h % 2) + z // 2) * P)

            for h in range(4):
                for z, n in enumerate(adds):
                    p0, t = 64 * (n % 2), n // 2
                    b, c = at_(h, z)
                    f = lambda e: e.matmul(b.t[:, c:c + P], KT[p0:p0 + 64, h, t * P:(t + 1) * P],
                                           VTX[p0:p0 + 64, t, h * P:(h + 1) * P], start=True, stop=True)
                    m = PE.do(f) if (h == 3 and z == 2) else PE.quiet(f)
            use["kt"] = [m]
            pm = [s0m[dr]] * 4
            for z, n in enumerate(adds):
                for h in range(4):
                    b, c = at_(h, z)
                    prev = S0[:, 4 * dr + h, :] if z == 0 else SS[:, 3 * h + z - 1, :]
                    pm[h] = DV.do(lambda e: e.scalar_tensor_tensor(
                        SS[:, 3 * h + z, :], prev, AV[:, 4 * h + n:4 * h + n + 1], b.t[:, c:c + P], ALU.mult, ALU.add),
                        m, pm[h], u["a2"], use["ss"])
            for b in b3:
                b.busy = [pm[3]]
            use["av"] = [pm[3]]
            u["pm"] = pm[3]

        def gla_out(dr, u):
            b2 = [BANKS.next(), BANKS.next()]
            PE.wait(b2[0].busy, b2[1].busy, u["g"], u["d8"], u["pm"])
            for h in range(4):
                for n in range(4):
                    p0, t = 64 * (n % 2), n // 2
                    c = h * P + t * 64
                    z = n if dr == 0 else 3 - n
                    st = S0[:, 4 * dr + h, :] if z == 0 else SS[:, 3 * h + z - 1, :]
                    o_ = b2[n % 2].t[:, c:c + 64]
                    PE.quiet(lambda e: e.matmul(o_, VTX[p0:p0 + 64, t, h * P:(h + 1) * P],
                                                SC[p0:p0 + 64, h, t * 64:t * 64 + 64], start=True, stop=False))
                    f = lambda e: e.matmul(o_, st, QI[:, h, n * 64:n * 64 + 64], start=False, stop=True)
                    m = PE.do(f) if (h == 3 and n == 3) else PE.quiet(f)
            for n in ("sc", "qi", "ss"):
                use[n] = [m]
            for z in range(2):
                v = O[:, :, :].rearrange("p h (t z c) -> p h t z c", t=2, z=2)[:, :, :, z, :]
                s_ = b2[z].t[:, :].rearrange("p (h t c) -> p h t c", h=4, t=2)
                if dr == 0:
                    u["o"] = DV.do(lambda e: e.tensor_copy(v, s_), m)
                else:
                    u["o"] = DV.do(lambda e: e.tensor_tensor(v, v, s_, ALU.add), m, u0["o"])
                b2[z].busy = [u["o"]]

        vb_chunk(0)
        s0m = []
        for dr in range(2):
            b = BANKS.next()
            PE.wait(kcm, b.busy, vm)
            for h in range(4):
                for t in range(2):
                    f = lambda e: e.matmul(b.t[:, h * P:(h + 1) * P], Kc[:, 4 * dr + h, t * P:(t + 1) * P],
                                           VTC[:, t, h * P:(h + 1) * P], start=(t == 0), stop=(t == 1))
                    m = PE.do(f) if (h == 3 and t == 1) else PE.quiet(f)
            s0m.append(DV.do(lambda e: e.tensor_copy(S0[:, 4 * dr:4 * dr + 4, :],
                                                     b.t[:, :].rearrange("p (a b) -> p a b", a=4)), m))
            b.busy = [s0m[-1]]
        ctx_done = [m, s0m[1]]
        u0 = gla_terms(0, ctx_done)
        vb_chunk(1)
        ogm, um, gam, gbm = [], [], [], []
        mods(2)
        ogm.append(plain(OG, "win", 0, fc_read))
        gla_scores(0, u0, ctx_done)
        mods(2)
        gla_states(0, u0)
        ogm.append(plain(OG, "win", 2, fc_read))
        mods(1)
        gla_out(0, u0)
        u1 = gla_terms(1, [])
        mods(1)
        um.append(plain(UU, "win", 0, fc_read))
        gla_scores(1, u1, [])
        mods(2)
        gla_states(1, u1)
        um.append(plain(UU, "win", 2, fc_read))
        mods(1)
        gla_out(1, u1)
        gla_free = [use["lg"], use["dd"], DV.mark]
        gam.append(plain(GA, "win", 0, gla_free))
        om = u1["o"]
        head_norms = []
        for c in range(1, 8):
            mods(1)
            if c < 4:
                gam.append(plain(GA, "win", 2 * c, []))
            else:
                gbm.append(plain(GB, "win", 2 * (c - 4), []))
            if c < 5:
                h = c - 1
                n = Norm()
                n.add(O[:, h, :], om)
                n.sums(P)
                head_norms.append(n)
            if 2 <= c < 6:
                h = c - 2
                rb, m = head_norms[h].spread()
                d = DV.do(lambda e: e.scalar_tensor_tensor(O[:, h, :], O[:, h, :], SM[:, S_GNA:S_GNA + 1], rb.t[:, :],
                                                           ALU.mult, ALU.mult), m, om)
                rb.busy = [d]
        om = d
        barrier()

        AH = ph("AH", 0, [P, 8, T], F32R)
        AL = ph("AL", 8, [P, 8, T], F32R)
        SG = ph("SG", 80, [P, 4, T])
        m = AC.do(lambda e: e.activation(SG[:, :, :], OG[:, :, :], ACT.Sigmoid))
        m3 = AC.do(lambda e: e.activation(GA[:, :, :], GA[:, :, :], ACT.Sigmoid))
        m3 = AC.do(lambda e: e.activation(GB[:, :, :], GB[:, :, :], ACT.Sigmoid))
        d = DV.do(lambda e: e.tensor_tensor(SG[:, :, :], SG[:, :, :], OG[:, :, :], ALU.mult), m)
        d = DV.do(lambda e: e.tensor_tensor(O[:, :, :], O[:, :, :], SG[:, :, :], ALU.mult), d, om)
        ah, al = halves_of(O[:, :, :], AH[:, 0:4, :], AL[:, 0:4, :], d)

        GV = ph("GV", 84, [P, 2, 512])
        GU = ph("GU", 88, [P, 4, T])
        ST = ph("ST", 92, [P, 24])
        m = AC.do(lambda e: e.activation(GV[:, :, :], VB[:, :, :], ACT.Gelu_apprx_tanh))
        m2 = AC.do(lambda e: e.activation(GU[:, :, :], UU[:, :, :], ACT.Gelu_apprx_tanh))
        for t in range(2):
            d = DV.do(lambda e, t=t: e.bn_stats(ST[:, 6 * t:6 * t + 6], GV[:, t, :]), m)
            d = DV.do(lambda e, t=t: e.bn_aggr(ST[:, 12 + 2 * t:14 + 2 * t], ST[:, 6 * t:6 * t + 6]), d)
        m = AC.do(lambda e: e.activation(ST[:, 16:18], ST[:, 13:17:2], ACT.Sqrt, bias=EPSV, scale=1.0), d)
        d = DV.do(lambda e: e.reciprocal(ST[:, 18:20], ST[:, 16:18]), m)
        for t in range(2):
            d1 = DV.do(lambda e, t=t: e.tensor_scalar(GV[:, t, :], GV[:, t, :], ST[:, 12 + 2 * t:13 + 2 * t],
                                                      ST[:, 18 + t:19 + t], ALU.subtract, ALU.mult), d)
            d1 = DV.do(lambda e, t=t: e.tensor_tensor(GV[:, t, :], GV[:, t, :], ROW[:, 0, :], ALU.mult), d1, row)
            d1 = DV.do(lambda e, t=t: e.tensor_tensor(GV[:, t, :], GV[:, t, :], ROW[:, 1, :], ALU.add), d1)
        for g in range(4):
            b = BANKS.next()
            PE.wait(d1, row, b.busy)
            for n in range(2):
                f = lambda e, n=n, g=g: e.matmul(b.t[:, n * P:(n + 1) * P], GV[:, n, g * P:(g + 1) * P],
                                                 WST[:, g, :], start=True, stop=True)
                m = PE.do(f) if n else PE.quiet(f)
            ta = TA.next()
            d2 = DV.do(lambda e, g=g: e.tensor_tensor(
                ta.t[:, :].rearrange("p (a b) -> p a b", a=2), b.t[:, 0:T].rearrange("p (a b) -> p a b", a=2),
                ROW[:, 2, g * P:(g + 1) * P].unsqueeze(1).to_broadcast([P, 2, P]), ALU.add), m, ta.busy)
            b.busy = [d2]
            d2 = DV.do(lambda e, g=g: e.tensor_tensor(GU[:, g, :], GU[:, g, :], ta.t[:, :], ALU.mult), d2, m2)
            ta.busy = [d2]
        bh, bl = halves_of(GU[:, :, :], AH[:, 4:8, :], AL[:, 4:8, :], d2)

        MG = ph("MG", 32, [P, 8, T])
        MH = ph("MH", 48, [P, 8, T], F32R)
        ML = ph("ML", 56, [P, 8, T], F32R)
        for which, (kind, g_, rd) in enumerate((("wpa", GA, [ah, al]), ("wpb", GB, [bh, bl]))):
            for c in range(2):
                j, w, wl, wm = take(kind)
                for t2 in range(2):
                    b = BANKS.next()
                    for t in range(2):
                        col = (2 * t2 + t) * P
                        m = project(w, wl, lambda k, col=col: (k * 512 + col, k * 512 + col + P), 4,
                                    AH[:, 4 * which:4 * which + 4, :], AL[:, 4 * which:4 * which + 4, :],
                                    b.t[:, t * T:(t + 1) * T], [wm, rd, b.busy])
                    mt = 4 * c + 2 * t2
                    v = b.t[:, :].rearrange("p (a b) -> p a b", a=2)
                    if which == 0:
                        d = DV.do(lambda e, mt=mt, v=v: e.tensor_tensor(MG[:, mt:mt + 2, :], v, GA[:, mt:mt + 2, :],
                                                                        ALU.mult), m, m3)
                        b.busy = [d]
                    else:
                        d = DV.do(lambda e, mt=mt, v=v: e.tensor_tensor(GB[:, mt:mt + 2, :], v, GB[:, mt:mt + 2, :],
                                                                        ALU.mult), m, m3)
                        b.busy = [d]
                        d = DV.do(lambda e, mt=mt: e.tensor_tensor(MG[:, mt:mt + 2, :], MG[:, mt:mt + 2, :],
                                                                   GB[:, mt:mt + 2, :], ALU.add), d)
                        mh, ml = halves_of(MG[:, mt:mt + 2, :], MH[:, mt:mt + 2, :], ML[:, mt:mt + 2, :], d)
                done(j)
                pump()

        n2 = Norm()
        for c in range(4):
            j, b, ms = pair("wo", MH, ML, [mh, ml])
            done(j)
            for t in range(2):
                mt = 2 * c + t
                d = DV.do(lambda e, mt=mt, t=t: e.scalar_tensor_tensor(
                    X[:, mt, :], b.t[:, t * T:(t + 1) * T], MOD[:, 16 + mt, 0:1], X[:, mt, :], ALU.mult, ALU.add),
                    ms[t])
                n2.add(X[:, mt, :], d)
            b.busy = [d]
            pump()
        vf = scale_of(40, S_GFFN, 32, 0, [])
        r2 = n2.finish(D)
        barrier()
        XH = ph("XH", 0, [P, KD, T], F32R)
        XL = ph("XL", 8, [P, KD, T], F32R)
        GH = ph("GH", 16, [P, FT, T], F32R)
        GL = ph("GL", 38, [P, FT, T], F32R)
        FG = ph("FG", 60, [P, KD, T])
        hx2 = modulated(X, r2, 40, 24, 0, XH, XL, [vf])
        r2[0].busy = [hx2]

        def ffn_up(kind, ready, rb, rbm):
            last = None
            for c in range(FT):
                j, b, ms = pair(kind, XH, XL, ready)
                done(j)
                ta, tb, tc = TA.next(), TB.next(), TC.next()
                gate, up = b.t[:, 0:T], b.t[:, T:2 * T]
                if rb is None:
                    s1 = AC.do(lambda e: e.activation(tb.t[:, :], gate, ACT.Silu), ms[0], tb.busy)
                    rest = [s1]
                    d = DV.do(lambda e: e.tensor_tensor(tc.t[:, :], up, tb.t[:, :], ALU.mult), s1, ms[1], tc.busy)
                    tb.busy = [d]
                else:
                    g = DV.do(lambda e: e.tensor_tensor(ta.t[:, :], gate, rb.t[:, :], ALU.mult), ms[0], ta.busy, rbm)
                    s1 = AC.do(lambda e: e.activation(tb.t[:, :], ta.t[:, :], ACT.Silu), g, tb.busy)
                    s2 = PO.do(lambda e: e.tensor_tensor(ta.t[:, :], tb.t[:, :], rb.t[:, :], ALU.mult), s1, rbm)
                    d = DV.do(lambda e: e.tensor_tensor(tc.t[:, :], up, ta.t[:, :], ALU.mult), s2, ms[1], tc.busy)
                    ta.busy = [d]
                    tb.busy = [s2]
                b.busy = [d]
                h, low = halves_of(tc.t[:, :], GH[:, c, :], GL[:, c, :], d)
                tc.busy = [h, low]
                last = [h, low]
                pump()
            if rb is not None:
                rb.busy = [PO.mark, DV.mark]
            return last

        def ffn_down(kind, ready, each):
            for mt in range(KD):
                b = BANKS.next()
                for half in range(2):
                    j, w, wl, wm = take(kind)
                    for k in range(11):
                        kk = 11 * half + k
                        m = mm3(b.t[:, 0:T], w[:, k * P:(k + 1) * P], wl[:, k * P:(k + 1) * P], GH[:, kk, :],
                                GL[:, kk, :], kk == 0, kk == 21, k == 10, [wm, ready, b.busy] if k == 0 else ())
                    done(j)
                    if half == 0:
                        pump()
                each(mt, b, m)
                pump()

        up_ready = ffn_up("up", hx2, None, None)
        nf = Norm()

        def after_first(mt, b, m):
            d = DV.do(lambda e: e.scalar_tensor_tensor(X[:, mt, :], b.t[:, 0:T], MOD[:, 40 + mt, 0:1], X[:, mt, :],
                                                       ALU.mult, ALU.add), m)
            b.busy = [d]
            nf.add(X[:, mt, :], d)

        ffn_down("down", up_ready, after_first)

        def G2(layer, i, k):
            c = S_NG2 + (layer * 6 + i) * 8 + k
            return SM[:, c:c + 1]

        def G2H(layer, i, k):
            c = (layer * 6 + i) * 8 + k
            return NG2H[:, c:c + 1]

        def next_halves(k, layer, i, d):
            h = AC.do(lambda e: e.activation(XH[:, k, :], X[:, k, :], ACT.Copy, scale=G2(layer, i, k)), d)
            return DV.do(lambda e: e.scalar_tensor_tensor(XL[:, k, :], X[:, k, :], G2(layer, i, k),
                                                          XH[:, k, :].bitcast(F32), ALU.mult, ALU.subtract), h)

        r = nf.finish(D)
        n2 = Norm()
        xs = []
        for k in range(KD):
            d = DV.do(lambda e, k=k: e.scalar_tensor_tensor(X[:, k, :], X[:, k, :], SM[:, S_GFIN + k:S_GFIN + k + 1],
                                                            r[0].t[:, :], ALU.mult, ALU.mult), r[2])
            xs.append(next_halves(k, 0, 0, d))
            n2.add(X[:, k, :], d)
        r[0].busy = [d]

        def collect(layer, i, half):
            n = Norm()
            marks = {}

            def each(mt, src, m):
                g = G2H(layer, i, mt) if half else G2(layer, i, mt)
                marks[mt] = AC.do(lambda e: e.activation(FG[:, mt, :], src, ACT.Copy, scale=g), m)
                marks["sq"] = n.add(src, m)
                return [marks[mt], marks["sq"]]

            return n, marks, each

        def residual(n, marks, layer, i):
            rb, _, rbm, _ = n.finish(D)
            nn = Norm() if layer is not None else None
            last = []
            for k in range(KD):
                ta = TA.next()
                d = DV.do(lambda e, k=k: e.tensor_tensor(ta.t[:, :], FG[:, k, :], rb.t[:, :], ALU.mult), rbm, marks[k],
                          ta.busy)
                d = DV.do(lambda e, k=k: e.tensor_tensor(X[:, k, :], X[:, k, :], ta.t[:, :], ALU.add), d)
                ta.busy = [d]
                if layer is not None:
                    last.append(next_halves(k, layer, i, d))
                    nn.add(X[:, k, :], d)
                else:
                    last.append(d)
            rb.busy = [d]
            return nn, last

        def ffn2(layer, first, xs, n2):
            rb, _, rbm, _ = n2.finish(D)
            rd = ffn_up("up2", xs[-1], rb, rbm)
            n, marks, each = collect(layer, 1 if first else 5, True)

            def f(mt, b, m):
                b.busy = each(mt, b.t[:, 0:T], m)

            ffn_down("down2", rd, f)
            return n, marks

        def project_out(kind, AHt, ALt, rd, layer):
            n, marks, each = collect(layer, 3, False)
            for c in range(4):
                j, b, ms = pair(kind, AHt, ALt, rd)
                done(j)
                for t in range(2):
                    b.busy = each(2 * c + t, b.t[:, t * T:(t + 1) * T], ms[1])
                pump()
            return n, marks

        n, marks = ffn2(0, True, xs, n2)
        n2, xs = residual(n, marks, 0, 2)
        barrier()
        rb, rt, rbm, rtm = n2.finish(D)
        VT = ph("VT", 16, [P, 2, 1024])
        OH = ph("OH", 24, [P, 8, T], F32R)
        OL = ph("OL", 32, [P, 8, T], F32R)
        QK = Turn([Slot(ph(f"QK{i}", 40 + 2 * i, [P, 2, T])) for i in range(2)])
        AB = Turn([Slot(ph(f"AB{i}", 44 + 1.5 * i, [P, 384])) for i in range(2)])
        LNB = Turn([Slot(ph(f"LNB{i}", 47 + 1.5 * i, [P, 384])) for i in range(2)])
        SPB = Turn([Slot(ph(f"SPB{i}", 50 + 1.5 * i, [P, 384])) for i in range(2)])
        AW = Turn([Slot(ph(f"AW{i}", 53 + 1.5 * i, [P, 384])) for i in range(2)])
        NU = at("NU", [P, 2, P], PB + 57 * KB)
        nu = DV.do(lambda e: e.tensor_scalar(NU[:, 0, :], TRI, -1.0, None, ALU.mult))
        nu = DV.do(lambda e: e.tensor_scalar(NU[:, 1, :], ONE, -1.0, None, ALU.mult))
        vts = []
        for c in range(4):
            j, w, wl, wm = take("sbv")
            b = BANKS.next()
            for t in range(2):
                m = tokens(w, wl, XH, XL, KD, t, b.t[:, t * T:(t + 1) * T], c256, [wm, xs[-1], b.busy])
            done(j)
            for t in range(2):
                v = AC.do(lambda e, c=c, t=t: e.activation(VT[:, t, c * 256:(c + 1) * 256], b.t[:, t * T:(t + 1) * T],
                                                           ACT.Copy, scale=rt.t[:, t:t + 1]), m, rtm)
            b.busy = [v]
            vts.append(v)
            pump()
        rt.busy = [v]

        def sb_front(qk, e_, ready):
            p0 = 64 * e_
            b = BANKS.next()
            kT = lambda t: qk.t[p0:p0 + 64, 1, t * P:(t + 1) * P]
            PE.wait(ready, b.busy)
            PE.quiet(lambda e: e.matmul(b.t[:, 0:256], kT(0), qk.t[p0:p0 + 64, 0, :], start=True, stop=False,
                                        skip_group_check=True))
            m = PE.do(lambda e: e.matmul(b.t[:, 256:384], kT(1), qk.t[p0:p0 + 64, 0, P:T], start=False, stop=False,
                                         skip_group_check=True))
            ab, ln, sp = AB.next(), LNB.next(), SPB.next()
            z = b.t[:, 0:384]
            s1 = AC.do(lambda e: e.activation(ab.t[:, :], z, ACT.Abs), m, ab.busy)
            s2 = AC.do(lambda e: e.activation(ab.t[:, :], ab.t[:, :], ACT.Exp, scale=-1.0), s1)
            s3 = AC.do(lambda e: e.activation(ln.t[:, :], ab.t[:, :], ACT.Ln, bias=ONE[:, 0:1]), s2, ln.busy)
            ab.busy = [s3]
            d = DV.do(lambda e: e.scalar_tensor_tensor(sp.t[:, :], z, 0.0, ln.t[:, :], ALU.max, ALU.add), s3, sp.busy)
            ln.busy = [d]
            for o in (0, 256):
                g = PO.do(lambda e, o=o: e.affine_select(
                    out=sp.t[:, o:o + P], in_=sp.t[:, o:o + P], compare_op=ALU.is_gt, fill=0.0, base=0,
                    pattern=[[1, P]], channel_multiplier=-1), d)
            return b, sp, g, m

        def sb_mid(b, sp, g):
            PE.wait(g, nu)
            PE.quiet(lambda e: e.matmul(b.t[:, 0:256], NU[:, 0, :], sp.t[:, 0:256], start=False, stop=False,
                                        skip_group_check=True))
            PE.quiet(lambda e: e.matmul(b.t[:, 128:256], NU[:, 1, :], sp.t[:, 256:384], start=False, stop=False,
                                        skip_group_check=True))
            m = PE.do(lambda e: e.matmul(b.t[:, 256:384], NU[:, 0, :], sp.t[:, 256:384], start=False, stop=True,
                                         skip_group_check=True))
            sp.busy = [m]
            aw = AW.next()
            s = AC.do(lambda e: e.activation(aw.t[:, :], b.t[:, 0:384], ACT.Exp), m, aw.busy)
            b.busy = [s]
            for o in (0, 256):
                g = PO.do(lambda e, o=o: e.affine_select(
                    out=aw.t[:, o:o + P], in_=aw.t[:, o:o + P], compare_op=ALU.is_gt, fill=0.0, base=0,
                    pattern=[[1, P]], channel_multiplier=-1), s)
            return aw, g

        def sb_back(ob, h, aw, g):
            p0 = 64 * (h % 2)
            PE.wait(g, vts, ob.busy if h % 2 == 0 else [])
            v = lambda t: VT[:, t, h * 64:h * 64 + 64]
            PE.quiet(lambda e: e.matmul(ob.t[p0:p0 + 64, 0:256], v(0), aw.t[:, 0:256], start=True, stop=False,
                                        skip_group_check=True))
            m = PE.do(lambda e: e.matmul(ob.t[p0:p0 + 64, 128:256], v(1), aw.t[:, 256:384], start=False, stop=True,
                                         skip_group_check=True))
            aw.busy = [m]
            return m

        def heads_out(ob, pr, m):
            h = AC.do(lambda e: e.activation(OH[:, pr, :], ob.t[:, 0:T], ACT.Copy), m)
            low = DV.do(lambda e: e.tensor_tensor(OL[:, pr, :], ob.t[:, 0:T], OH[:, pr, :].bitcast(F32),
                                                  ALU.subtract), h)
            ob.busy = [low]
            return [h, low]

        for pr in range(8):
            j, b, ms = pair("sbqk", XH, XL, xs[-1])
            done(j)
            qk = QK.next()
            DV.do(lambda e: e.scalar_tensor_tensor(qk.t[:, 0, :], b.t[:, 0:T], 0.125, rb.t[:, :], ALU.mult, ALU.mult),
                  ms[1], qk.busy, rbm)
            d = DV.do(lambda e: e.tensor_tensor(qk.t[:, 1, :], b.t[:, T:2 * T], rb.t[:, :], ALU.mult))
            b.busy = [d]
            pump()
            fr = [sb_front(qk, e_, d) for e_ in range(2)]
            qk.busy = [fr[1][3]]
            md = [sb_mid(*f[0:3]) for f in fr]
            ob = BANKS.next()
            for e_ in range(2):
                m = sb_back(ob, 2 * pr + e_, *md[e_])
            oready = heads_out(ob, pr, m)
        rb.busy = [d]
        n, marks = project_out("sbo", OH, OL, oready, 0)
        n2, xs = residual(n, marks, 0, 4)
        barrier()
        n, marks = ffn2(0, False, xs, n2)
        n2, xs = residual(n, marks, 1, 0)

        rope = rope_tables()
        n, marks = ffn2(1, True, xs, n2)
        n2, xs = residual(n, marks, 1, 2)
        barrier()
        rb, rt, rbm, rtm = n2.finish(D)
        VT1 = ph("VT1", 16, [P, 2, 1024])
        OH = ph("OH1", 24, [P, 8, T], F32R)
        OL = ph("OL1", 32, [P, 8, T], F32R)
        CQ = ph("CQ", 40, [P, 5, T])
        CH = ph("CH", 45, [P, 3, T], F32R)
        CL = ph("CL", 48, [P, 3, T], F32R)
        QF = ph("QF", 51, [P, 16, T])
        KF = ph("KF", 67, [P, 16, T])
        SW = Turn([Slot(ph(f"SW{i}", 83 + 4 * i, [P, 4, T])) for i in range(2)])
        SM_ = Turn([Slot(ph(f"SX{i}", 91 + 1.5 * i, [P, 384])) for i in range(3)])
        PT = Turn([Slot(ph(f"PT{i}", 96 + 1.5 * i, [P, 384])) for i in range(2)])
        MX = Turn([Slot(ph(f"MX{i}", 100 + 0.125 * i, [P, 8])) for i in range(4)])
        cq = []
        for c in range(3):
            j, w, wl, wm = take(f"mla{c}")
            wd = 256 if c < 2 else 128
            b = BANKS.next()
            for t in range(wd // P):
                m = project(w, wl, lambda k, t=t, wd=wd: (k * wd + t * P, k * wd + t * P + P), KD, XH, XL,
                            b.t[:, t * T:(t + 1) * T], [wm, xs[-1], b.busy])
            done(j)
            for t in range(wd // P):
                d = DV.do(lambda e, c=c, t=t: e.tensor_tensor(CQ[:, 2 * c + t, :], b.t[:, t * T:(t + 1) * T],
                                                              rb.t[:, :], ALU.mult), m, rbm)
                cq.append(d)
            b.busy = [d]
            pump()
        rb.busy = [d]
        nq = Norm()
        nq.add(CQ[:, 0, :], cq[0])
        nq.add(CQ[:, 1, :], cq[1])
        rq = nq.finish(256)
        nk = Norm()
        nk.add(CQ[:, 2, :], cq[2])
        rk = nk.finish(128)
        for t in range(3):
            g = SM[:, S_QN + t:S_QN + t + 1]
            rr = rq if t < 2 else rk
            ta = TA.next()
            d = DV.do(lambda e, t=t, g=g, rr=rr: e.scalar_tensor_tensor(ta.t[:, :], CQ[:, t, :], g, rr[0].t[:, :],
                                                                        ALU.mult, ALU.mult), rr[2], ta.busy)
            ch = halves_of(ta.t[:, :], CH[:, t, :], CL[:, t, :], d)
            ta.busy = [*ch]
            rr[0].busy = [d]
        R4 = slice(64, 96)
        swap = [(i + 16) % 32 for i in range(32)]

        def rotate(dst, n, marks, eng=None):
            sw = SW.next()
            d = DV.do(lambda e: e.stream_shuffle(sw.t[R4, 0:n, :], dst, swap), marks, sw.busy)
            d1 = DV.do(lambda e: e.tensor_tensor(sw.t[R4, 0:n, :], sw.t[R4, 0:n, :],
                                                 SIN[R4, :].unsqueeze(1).to_broadcast([32, n, T]), ALU.mult), d, rope)
            d2 = DV.do(lambda e: e.tensor_tensor(dst, dst, COS[R4, :].unsqueeze(1).to_broadcast([32, n, T]), ALU.mult),
                       d)
            d3 = DV.do(lambda e: e.tensor_tensor(dst, dst, sw.t[R4, 0:n, :], ALU.add), d1, d2)
            sw.busy = [d3]
            return d3

        kr = rotate(CQ[R4, 3:4, :], 1, cq[3])
        krc = AC.do(lambda e: e.activation(KF[R4, :, :], CQ[R4, 3, :].unsqueeze(1).to_broadcast([32, 16, T]),
                                           ACT.Copy), kr)
        j, w, wl, wm = take("mlakv")
        kfm = {}
        for h2 in range(8):
            b = BANKS.next()
            for e_ in range(2):
                h = 2 * h2 + e_
                m = mm3(b.t[:, e_ * T:(e_ + 1) * T], w[:, h * P:(h + 1) * P], wl[:, h * P:(h + 1) * P],
                        CH[:, 2, :], CL[:, 2, :], True, True, True, [wm, ch, b.busy])
            c = AC.do(lambda e, h2=h2: e.activation(KF[0:64, 2 * h2:2 * h2 + 2, :],
                                                    b.t[0:64, :].rearrange("p (a b) -> p a b", a=2), ACT.Copy), m)
            b.busy = [c]
            kfm[h2] = c
        vts = []
        for t in range(2):
            for g in range(4):
                b = BANKS.next()
                vv = lambda w_, g=g: w_[:, g * 512:(g + 1) * 512].rearrange("p (a b) -> p a b", a=4)[:, :, 64:128]
                m = mm3(b.t[:, 0:256].rearrange("p (a b) -> p a b", a=4), CH[:, 2, t * P:(t + 1) * P],
                        CL[:, 2, t * P:(t + 1) * P], vv(w), vv(wl), True, True, True, [b.busy])
                c = DV.do(lambda e, t=t, g=g: e.tensor_copy(VT1[:, t, g * 256:(g + 1) * 256], b.t[:, 0:256]), m)
                b.busy = [c]
                vts.append(c)
        done(j)
        pump()
        MSC = 1.0 / 96 ** 0.5
        qfm = {}

        def mla_q(c):
            j, w, wl, wm = take("mlaq")
            for h2 in range(4):
                b = BANKS.next()
                for e_ in range(2):
                    o = (2 * h2 + e_) * 96
                    m = project(w, wl, lambda k, o=o: (k * 768 + o, k * 768 + o + 96), 2, CH, CL,
                                b.t[0:96, e_ * T:(e_ + 1) * T], [wm, b.busy])
                hh = 8 * c + 2 * h2
                q = AC.do(lambda e, hh=hh: e.activation(QF[0:96, hh:hh + 2, :],
                                                        b.t[0:96, :].rearrange("p (a b) -> p a b", a=2), ACT.Copy), m)
                b.busy = [q]
                if h2 % 2:
                    r_ = rotate(QF[R4, hh - 2:hh + 2, :], 4, q)
                    for x in range(hh - 2, hh + 2):
                        qfm[x] = [r_, q]
            done(j)
            pump()

        def mla_front(h):
            b = BANKS.next()
            PE.wait(qfm[h], kfm[h // 2], krc, b.busy)
            PE.quiet(lambda e: e.matmul(b.t[:, 0:128], QF[0:96, h, 0:P], KF[0:96, h, 0:P], start=True, stop=True))
            m = PE.do(lambda e: e.matmul(b.t[:, 128:384], QF[0:96, h, P:T], KF[0:96, h, :], start=True, stop=True))
            sx, mx = SM_.next(), MX.next()
            d = DV.do(lambda e: e.tensor_tensor(sx.t[:, 0:128], b.t[:, 0:128], NEGM[:, 128:256], ALU.add), m, sx.busy)
            d = DV.do(lambda e: e.tensor_tensor(sx.t[:, 128:384], b.t[:, 128:384], NEGM, ALU.add))
            b.busy = [d]
            DV.do(lambda e: e.tensor_reduce(mx.t[:, 0:1], sx.t[:, 0:128], AX, ALU.max), d, mx.busy)
            d = DV.do(lambda e: e.tensor_reduce(mx.t[:, 1:2], sx.t[:, 128:384], AX, ALU.max))
            d = DV.do(lambda e: e.tensor_scalar(mx.t[:, 2:4], mx.t[:, 0:2], -MSC, None, ALU.mult), d)
            AC.do(lambda e: e.activation(sx.t[:, 0:128], sx.t[:, 0:128], ACT.Exp, bias=mx.t[:, 2:3], scale=MSC,
                                         accum_out=mx.t[:, 4:5]), d)
            s = AC.do(lambda e: e.activation(sx.t[:, 128:384], sx.t[:, 128:384], ACT.Exp, bias=mx.t[:, 3:4], scale=MSC,
                                             accum_out=mx.t[:, 5:6]), d)
            d = DV.do(lambda e: e.reciprocal(mx.t[:, 6:8], mx.t[:, 4:6]), s)
            DV.do(lambda e: e.tensor_scalar(sx.t[:, 0:128], sx.t[:, 0:128], mx.t[:, 6:7], None, ALU.mult), d)
            d = DV.do(lambda e: e.tensor_scalar(sx.t[:, 128:384], sx.t[:, 128:384], mx.t[:, 7:8], None, ALU.mult))
            mx.busy = [d]
            return sx, d

        def mla_mid(sx, d):
            b = BANKS.next()
            PE.wait(d, b.busy)
            for z in range(3):
                f = lambda e, z=z: e.transpose(b.t[:, z * P:(z + 1) * P], sx.t[:, z * P:(z + 1) * P], IDN)
                m = PE.do(f) if z == 2 else PE.quiet(f)
            sx.busy = [m]
            pt = PT.next()
            c = AC.do(lambda e: e.activation(pt.t[:, :], b.t[:, 0:384], ACT.Copy), m, pt.busy)
            b.busy = [c]
            return pt, c

        def mla_back(ob, h, pt, c):
            p0 = 64 * (h % 2)
            PE.wait(c, vts, ob.busy if h % 2 == 0 else [])
            v = lambda t: VT1[:, t, h * 64:h * 64 + 64]
            PE.quiet(lambda e: e.matmul(ob.t[p0:p0 + 64, 0:256], v(0), pt.t[:, 0:256], start=True, stop=False,
                                        skip_group_check=True))
            m = PE.do(lambda e: e.matmul(ob.t[p0:p0 + 64, 128:256], v(1), pt.t[:, 256:384], start=False, stop=True,
                                         skip_group_check=True))
            pt.busy = [m]
            return m

        mla_q(0)
        fr = {0: mla_front(0), 1: mla_front(1)}
        mla_q(1)
        for pr in range(8):
            md = []
            for e_ in range(2):
                md.append(mla_mid(*fr.pop(2 * pr + e_)))
                if 2 * pr + 2 + e_ < 16:
                    fr[2 * pr + 2 + e_] = mla_front(2 * pr + 2 + e_)
            ob = BANKS.next()
            for e_ in range(2):
                m = mla_back(ob, 2 * pr + e_, *md[e_])
            oready = heads_out(ob, pr, m)
        n, marks = project_out("mlao", OH, OL, oready, 1)
        n2, xs = residual(n, marks, 1, 4)
        barrier()
        n, marks = ffn2(1, False, xs, n2)
        _, last = residual(n, marks, None, None)
        SP.quiet(lambda e: e.dma_start(out, X[:, :, :]).then_inc(s_out, 16), last)
        SP.wait((s_out, 16))


def kernel(**inputs):
    import numpy as np
    import concourse.bacc as _bacc
    from concourse.bass_utils import run_bass_kernel_spmd as _run

    g = {k: np.asarray(v) for k, v in inputs.items()}

    def con(a):
        return np.ascontiguousarray(a)

    def cols(w, n):
        K, N = w.shape
        return con(w.reshape(K // P, P, N // n, n).transpose(2, 1, 0, 3)).reshape(N // n, P, K // P * n)

    def paired(w):
        K, N = w.shape
        F = N // 2 // P
        return con(w.reshape(K // P, P, 2, F, P).transpose(3, 1, 0, 2, 4)).reshape(F, P, K // P * 2 * P)

    def down(w):
        return con(w.reshape(2, 11, P, KD, P).transpose(3, 0, 2, 1, 4)).reshape(16, P, 11 * P)

    def vec(v):
        return v.reshape(-1, P).T

    win = g["w_in"][0]
    AK = 512
    parts = [win[:, 0:3 * AK], win[:, 3 * AK:4 * AK], win[:, 6 * AK:7 * AK], win[:, 4 * AK:5 * AK],
             win[:, 5 * AK:6 * AK], win[:, 7 * AK:]]
    win = np.concatenate(parts, axis=1)
    cst = np.zeros((P, C_END), np.float32)
    cst[:, C_ID:C_ID + P] = np.eye(P)
    cst[:, C_ONE:C_ONE + P] = 1
    cst[:, C_TRI:C_TRI + P] = np.tril(np.ones((P, P)))
    cst[:, C_NEG + P:C_NEG + 2 * P] = np.triu(np.full((P, P), NEG), 1)
    inv = (np.float32(10000.0) ** (-np.arange(0, 32, 2, dtype=np.float32) / np.float32(32))).astype(np.float32)
    cst[:, C_INV] = np.tile(inv, 8)
    cst[:, C_SGN] = np.tile(np.repeat([-1.0, 1.0], 16), 4)
    cc = np.stack([vec(g["c"][0]), vec(g["c_ctx"])], axis=2).reshape(P, 16)
    small = np.concatenate(
        [cc, vec(g["b_mod"][0]), vec(g["g_mix"][0]), vec(g["g_ffn"][0]), vec(g["g_final"]), vec(g["g_norm_a"][0]),
         vec(g["lb_gamma"].reshape(-1)), vec(g["norm_g_2"].reshape(-1)), vec(g["mla_q_norm_2"][0]),
         vec(g["mla_kv_norm_2"][0])], axis=1)
    sb = g["sb_w_in_2"][0]
    mla = g["mla_w_in_2"][0]
    mla = np.concatenate([mla[:, 0:384]] + [mla[:, 384:416]] * 8, axis=1)
    wu2 = g["ffn_w_in_2"].reshape(4, D, 2 * FT * P)
    wd2 = g["ffn_w_out_2"].reshape(4, FT * P, D)
    arr = {
        "cst": cst,
        "small": small,
        "x": g["x"][0].T.reshape(KD, P, T).transpose(1, 0, 2),
        "ctx": g["ctx"][0].T.reshape(KD, P, T).transpose(1, 0, 2),
        "rows": np.concatenate([g["ln_v_g"], g["ln_v_b"], g["b_s"].reshape(1, 512)], axis=0),
        "wst": g["w_s"][0].transpose(2, 0, 1),
        "pos": g["positions_2"],
        "mod": cols(g["w_mod"][0], 256),
        "win": cols(win, 256),
        "wpa": cols(g["w_pa"][0], 512),
        "wpb": cols(g["w_pb"][0], 512),
        "wo": cols(g["w_o"][0], 256),
        "up": paired(g["w_up"][0]),
        "down": down(g["w_down"][0]),
        "up2": np.concatenate([paired(w) for w in wu2], axis=0),
        "down2": np.concatenate([down(w) for w in wd2], axis=0),
        "sbv": cols(sb[:, 2048:3072], 256),
        "sbqk": paired(sb[:, 0:2048]),
        "sbo": cols(g["sb_w_out_2"][0], 256),
        "mla0": cols(mla[:, 0:256], 256),
        "mla1": cols(mla[:, 256:512], 256),
        "mla2": cols(mla[:, 512:640], 128),
        "mlakv": cols(g["mla_w_ukv_2"][0], 2048),
        "mlaq": cols(g["mla_w_uq_2"][0], 768),
        "mlao": cols(g["mla_w_out_2"][0], 256),
    }
    nc = _bacc.Bacc("TRN2", target_bir_lowering=False, num_devices=1)
    arrays, aps = {}, {}
    for name, v in arr.items():
        v = con(v)
        arrays[f"in_{name}"] = v
        aps[name] = nc.dram_tensor(f"in_{name}", v.shape, mybir.dt.from_np(v.dtype), kind="ExternalInput").ap()
    o = nc.dram_tensor("out_0", (P, KD, T), F32, kind="ExternalOutput").ap()
    build(nc, aps, o)
    r = _run(nc, [arrays], core_ids=[0])
    y = r.results[0]["out_0"]
    return con(y.transpose(1, 0, 2).reshape(D, T).T).reshape(1, T, D)
```

```python
from contextlib import ExitStack

import concourse.bass as bass
from concourse import mybir

F32 = mybir.dt.float32
F32R = mybir.dt.float32r
I32 = mybir.dt.int32
ALU = mybir.AluOpType
ACT = mybir.ActivationFunctionType
AX = mybir.AxisListType.X

P = 128
T = 256
D = 1024
KD = D // P
FT = 22
EPS = 1e-6
NRAW = 3
NSPLIT = 3
SLOT = 2048
NEG = -1e30

C_ID, C_ONE, C_TRI, C_NEG, C_INV, C_SGN, C_SEL, C_END = 0, 128, 256, 384, 640, 641, 642, 644
S_CC, S_BMOD, S_GMIX, S_GFFN, S_GFIN, S_GNA, S_LBG, S_NG2, S_QN, S_KVN, S_END = (
    0, 16, 64, 72, 80, 88, 89, 105, 201, 203, 204)


class Lane:

    def __init__(self, eng, sem):
        self.eng, self.sem, self.n, self.met = eng, sem, 0, {}

    def wait(self, *marks):
        for m in marks:
            if not m:
                continue
            if isinstance(m, list):
                self.wait(*m)
                continue
            sem, value = m
            if self.met.get(id(sem), 0) < value:
                self.met[id(sem)] = value
                self.eng.wait_ge(sem, value)

    def do(self, fn, *marks):
        self.wait(*marks)
        self.n += 1
        fn(self.eng).then_inc(self.sem, 1)
        return self.mark

    def quiet(self, fn, *marks):
        self.wait(*marks)
        fn(self.eng)

    @property
    def mark(self):
        return (self.sem, self.n)


class Slot:

    def __init__(self, t):
        self.t, self.busy = t, []


class Turn:
    def __init__(self, slots):
        self.slots, self.i = slots, 0

    def next(self):
        s = self.slots[self.i % len(self.slots)]
        self.i += 1
        return s


def weight_plan():
    plan = [("win", i, 2048, True) for i in range(10)]
    nxt = 8
    for i in range(10, 22):
        n = 2 if i < 14 else 1
        plan += [("mod", nxt + z, 2048, True) for z in range(n)]
        nxt += n
        plan += [("win", i, 2048, True)]
    plan += [("wpa", i, 2048, True) for i in range(2)] + [("wpb", i, 2048, True) for i in range(2)]
    plan += [("wo", i, 2048, True) for i in range(4)]
    plan += [("up", i, 2048, True) for i in range(FT)]
    plan += [("down", i, 1408, True) for i in range(16)]
    for layer in range(2):
        plan += [("up2", 2 * layer * FT + i, 2048, True) for i in range(FT)]
        plan += [("down2", 2 * layer * 16 + i, 1408, True) for i in range(16)]
        if layer == 0:
            plan += [("sbv", i, 2048, True) for i in range(4)]
            plan += [("sbqk", i, 2048, True) for i in range(8)]
            plan += [("sbo", i, 2048, True) for i in range(4)]
        else:
            plan += [("mla0", 0, 2048, True), ("mla1", 0, 2048, True)]
            plan += [("mla2", 0, 1024, True)]
            plan += [("mlakv", 0, 2048, True)]
            plan += [("mlaq", i, 1536, True) for i in range(2)]
            plan += [("mlao", i, 2048, True) for i in range(4)]
        plan += [("up2", (2 * layer + 1) * FT + i, 2048, True) for i in range(FT)]
        plan += [("down2", (2 * layer + 1) * 16 + i, 1408, True) for i in range(16)]
    return plan


def build(nc, a, out, stop=None):
    plan = weight_plan()
    ctx = ExitStack()
    with ctx:
        base = [nc.sbuf_base]

        def at(name, shape, off, dt=F32):
            return nc.alloc_sbuf_tensor_at(name, shape, dt, offset=off)

        def fixed(name, cols, dt=F32, shape=None):
            off = (base[0] + 31) // 32 * 32
            base[0] = off + cols * 4
            return at(name, shape or [P, cols], off, dt)

        def sem(name):
            return ctx.enter_context(nc.semaphore(name))

        CST = fixed("CST", C_END)
        SM = fixed("SM", S_END)
        X = fixed("X", KD * T, shape=[P, KD, T])
        RAW = [fixed(f"RAW{i}", SLOT) for i in range(NRAW)]
        WH = [fixed(f"WH{i}", SLOT, F32R) for i in range(NSPLIT)]
        WL = [fixed(f"WL{i}", SLOT, F32R) for i in range(NSPLIT)]
        SILC = fixed("SILC", 16)
        SILH = fixed("SILH", 32, F32R, [P, 8, 4])
        MOD = fixed("MOD", 96, shape=[P, 48, 2])
        VEC = fixed("VEC", 64)
        LBV = fixed("LBV", 48)
        NG2H = fixed("NG2H", 96)
        RT = Turn([Slot(fixed(f"RT{i}", 2)) for i in range(2)])
        RS = Turn([Slot(fixed(f"RS{i}", 2)) for i in range(2)])
        DG = Turn([Slot(fixed(f"DG{i}", T)) for i in range(2)])
        RB = Turn([Slot(fixed(f"RB{i}", T)) for i in range(2)])
        SQ = Turn([Slot(fixed(f"SQ{i}", T)) for i in range(3)])
        ACC = Turn([Slot(fixed(f"ACC{i}", T)) for i in range(2)])
        ss_at = (base[0] + 31) // 32 * 32
        TA = Turn([Slot(fixed(f"TA{i}", T)) for i in range(2)])
        TB = Turn([Slot(fixed(f"TB{i}", T)) for i in range(2)])
        TC = Turn([Slot(fixed(f"TC{i}", T)) for i in range(2)])
        mr_at = (base[0] + 31) // 32 * 32
        COS = fixed("COS", T)
        SIN = fixed("SIN", T)
        MR = Turn([Slot(at(f"MR{i}", [4, T], mr_at + 1024 * i)) for i in range(2)])
        PB = (base[0] + 31) // 32 * 32
        KB = 1024

        def ph(name, kb, shape, dt=F32):
            return at(name, shape, PB + int(kb * KB), dt)

        BANKS = Turn([Slot(ctx.enter_context(nc.psum_tensor(f"PS{i}", [P, 512], F32))) for i in range(8)])

        PE = Lane(nc.tensor, sem("s_pe"))
        AC = Lane(nc.scalar, sem("s_act"))
        DV = Lane(nc.vector, sem("s_dve"))
        PO = Lane(nc.gpsimd, sem("s_pool"))
        SP = Lane(nc.sync, sem("s_sp"))
        s_raw = [sem(f"s_raw{i}") for i in range(NRAW)]
        s_in = sem("s_in")
        s_mod = [sem(f"s_mod{i}") for i in range(8)]
        s_const, s_ctx, s_x = sem("s_const"), sem("s_ctx"), sem("s_x")
        s_out = sem("s_out")
        ins = [0]

        def load_small(dst, src):
            ins[0] += 16
            AC.quiet(lambda e, d=dst, r=src: e.dma_start(d, r).then_inc(s_in, 16))
            return (s_in, ins[0])

        IDN = CST[:, C_ID:C_ID + 128]
        ONE = CST[:, C_ONE:C_ONE + 128]
        TRI = CST[:, C_TRI:C_TRI + 128]
        NEGM = CST[:, C_NEG:C_NEG + 256]

        loaded, raw_slot, raw_free, order = {}, {}, {}, []
        split_slot, halves, consumed = {}, {}, {}
        nsplit = 0
        sidx = {}
        for j, (_, _, _, sp) in enumerate(plan):
            if sp:
                sidx[j] = nsplit
                nsplit += 1
        at_split = {v: k for k, v in sidx.items()}
        state = {"load": 0, "split": 0, "use": 0}

        def pump(splits=True):
            moved = True
            while moved:
                moved = False
                j = state["load"]
                if j < len(plan) and (j < NRAW or (j - NRAW) in raw_free):
                    src, i, cols, _ = plan[j]
                    r = j % NRAW
                    SP.quiet(lambda e, r=r, c=cols, s=a[src][i]:
                             e.dma_start(RAW[r][:, 0:c], s).then_inc(s_raw[r], 16),
                             raw_free.get(j - NRAW))
                    loaded[j] = (s_raw[r], 16 * (j // NRAW + 1))
                    state["load"] += 1
                    moved = True
                s = state["split"]
                if splits and s < nsplit:
                    j = at_split[s]
                    if j in loaded and (s < NSPLIT or (s - NSPLIT) in consumed):
                        free = consumed.get(s - NSPLIT)
                        c = plan[j][2]
                        r, h = RAW[j % NRAW], s % NSPLIT
                        for x0, x1 in ((0, c // 2), (c // 2, c)):
                            hi = AC.do(lambda e: e.activation(WH[h][:, x0:x1], r[:, x0:x1], ACT.Copy),
                                       loaded[j], free)
                            lo = DV.do(lambda e: e.tensor_tensor(
                                WL[h][:, x0:x1], r[:, x0:x1], WH[h][:, x0:x1].bitcast(F32), ALU.subtract),
                                hi, free)
                        halves[j] = (WH[h], WL[h], [hi, lo])
                        raw_free[j] = [hi, lo]
                        state["split"] += 1
                        moved = True

        def take(kind):
            j = state["use"]
            assert plan[j][0] == kind, (plan[j], kind)
            state["use"] += 1
            pump()
            if plan[j][3]:
                return j, *halves[j]
            return j, RAW[j % NRAW], None, [loaded[j]]

        def done(j):
            if plan[j][3]:
                consumed[sidx[j]] = PE.mark
            else:
                raw_free[j] = PE.mark

        def mm3(out_, lh, ll, rh, rl, first, last, signal, marks=()):
            PE.wait(*marks)
            PE.quiet(lambda e: e.matmul(out_, lh, rh, start=first, stop=False))
            PE.quiet(lambda e: e.matmul(out_, lh, rl, start=False, stop=False))
            f = lambda e: e.matmul(out_, ll, rh, start=False, stop=last)
            if signal:
                return PE.do(f)
            PE.quiet(f)
            return None

        def project(w, wl, cols, kt, xh, xl, out_, marks):
            for k in range(kt):
                lo, hi_ = cols(k)
                m = mm3(out_, w[:, lo:hi_], wl[:, lo:hi_], xh[:, k, :], xl[:, k, :], k == 0, k == kt - 1,
                        k == kt - 1, marks if k == 0 else ())
            return m

        def pair(kind, xh, xl, ready, kt=KD, marks=()):
            j, w, wl, wm = take(kind)
            b = BANKS.next()
            ms = []
            for t in range(2):
                ms.append(project(w, wl, lambda k, t=t: (k * 256 + t * 128, k * 256 + t * 128 + 128), kt, xh, xl,
                                  b.t[:, t * T:(t + 1) * T], [wm, ready, b.busy]))
            return j, b, [ms[1], ms[1]]

        class ByK:

            def __init__(self, kinds, xh, xl, tokens=False, got=None, keep=False):
                self.got, self.keep = got or [take(kind) for kind in kinds], keep
                self.banks = [BANKS.next() for _ in kinds]
                self.xh, self.xl, self.tokens = xh, xl, tokens

            def run(self, k, ready):
                xh, xl = self.xh, self.xl
                for (j, w, wl, wm), b in zip(self.got, self.banks):
                    PE.wait(wm, ready, b.busy)
                    for t in range(2):
                        o_ = b.t[:, t * T:(t + 1) * T]
                        if self.tokens:
                            l, ll = (x[:, k, t * P:(t + 1) * P] for x in (xh, xl))
                            rh, rl = (x[:, k * 256:k * 256 + 256] for x in (w, wl))
                            ops = ((l, rh), (ll, rh), (l, rl))
                        else:
                            l, ll = (x[:, k * 256 + t * P:k * 256 + t * P + P] for x in (w, wl))
                            ops = ((l, xh[:, k, :]), (l, xl[:, k, :]), (ll, xh[:, k, :]))
                        last = k == KD - 1
                        for z, (lhs, rhs) in enumerate(ops):
                            f = lambda e: e.matmul(o_, lhs, rhs, start=(k == 0 and t == 0 and z == 0),
                                                   stop=(last and z == 2), skip_group_check=True)
                            if last and t == 1 and z == 2:
                                b.done = PE.do(f)
                                if not self.keep:
                                    done(j)
                            else:
                                PE.quiet(f)

        def by_k(kinds, xh, xl, ready, tokens=False):
            g = ByK(kinds, xh, xl, tokens)
            for k in range(KD):
                g.run(k, ready[k])
            return g.banks

        def barrier():
            marks = [PE.mark, AC.mark, DV.mark, PO.mark]
            for lane in (PE, AC, DV, PO):
                lane.wait(*marks)

        class Norm:

            def __init__(self, lane=DV):
                self.acc, self.n, self.last, self.lane = ACC.next(), 0, None, lane

            def add(self, src, marks):
                q = SQ.next() if self.n else self.acc
                dst = q.t
                m = AC.do(lambda e: e.activation(dst[:, 0:T], src, ACT.Square), marks, q.busy)
                if self.n:
                    acc = self.acc.t
                    self.last = self.lane.do(lambda e: e.tensor_tensor(acc[:, :], acc[:, :], dst[:, :], ALU.add),
                                             m, self.last)
                    q.busy = [self.last]
                else:
                    self.last = m
                self.n += 1
                return m

            def sums(self, dim):
                acc, b = self.acc.t, BANKS.next()
                self.b = b
                PE.wait(self.last, b.busy, const)
                for t in range(2):
                    f = lambda e: e.matmul(b.t[:, t:t + 1], acc[:, t * P:(t + 1) * P], ONE[:, 0:1],
                                           start=True, stop=True)
                    m = PE.do(f) if t else PE.quiet(f)
                self.acc.busy = [m]
                rs, self.rt, self.dg = RS.next(), RT.next(), DG.next()
                rt, dg = self.rt, self.dg
                self.m = AC.do(lambda e: e.activation(rs.t[:, :], b.t[:, 0:2], ACT.Sqrt, bias=EPSV, scale=1.0 / dim),
                               m, rs.busy)
                self.r = DV.do(lambda e: e.reciprocal(rt.t[:, :], rs.t[:, :]), self.m, rt.busy)
                rs.busy = [self.r]
                for t in range(2):
                    self.g = DV.do(lambda e: e.tensor_scalar(dg.t[:, t * P:(t + 1) * P], IDN, rt.t[:, t:t + 1], None,
                                                             ALU.mult), self.r, dg.busy)
                rt.busy = [self.r, self.g]

            def spread(self, copy=True):
                b, dg = self.b, self.dg
                m = PE.do(lambda e: e.matmul(b.t[:, 0:T], ONE, dg.t[:, :], start=True, stop=True), self.g, self.m)
                dg.busy = [m]
                if not copy:
                    return b, m
                rb = RB.next()
                m = AC.do(lambda e: e.activation(rb.t[:, :], b.t[:, 0:T], ACT.Copy), m, rb.busy)
                b.busy = [m]
                return rb, m

            def finish(self, dim):
                self.sums(dim)
                rb, m = self.spread()
                return rb, self.rt, m, self.r

        SP.quiet(lambda e: e.dma_start(SM[:, :], a["small"]).then_inc(s_const, 16))
        SP.quiet(lambda e: e.dma_start(CST[:, :], a["cst"]).then_inc(s_const, 16))
        const = (s_const, 32)
        XC = ph("XC", 80, [P, KD, T])
        FIRST = {}
        for z, i in enumerate((4, 5, 6, 7, 0, 1, 2, 3)):
            t_ = ph(f"MC{i}", 32 + 8 * z if z < 6 else 40 + 8 * z, [P, SLOT])
            if z == 1:
                SP.quiet(lambda e: e.dma_start(X[:, :, :], a["x"]).then_inc(s_x, 16))
            if z == 4:
                SP.quiet(lambda e: e.dma_start(XC[:, :, :], a["ctx"]).then_inc(s_ctx, 16))
            SP.quiet(lambda e: e.dma_start(t_[:, :], a["mod"][i]).then_inc(s_mod[i], 16))
            FIRST[i] = (t_, (s_mod[i], 16))
        pump(splits=False)
        xin, cin = (s_x, 16), (s_ctx, 16)
        ROW = ph("ROW", 72, [P, 3, 512])
        WST = ph("WST", 78, [P, 4, P])
        EPSV = VEC[:, 60:61]
        PIV = VEC[:, 61:62]
        DV.do(lambda e: e.memset(EPSV, EPS))
        epsb = DV.do(lambda e: e.memset(PIV, 1.5707963267948966))
        AC.wait(epsb)
        for lane in (AC, DV, PE):
            lane.wait(const)
        def rope_tables():
            POS, ANG, NN, NM = (ph(n, 68 + i, [P, T], I32 if i == 0 else F32)
                                for i, n in enumerate(("POS", "ANG", "NN", "NM")))
            d = load_small(POS[:, :], a["pos"].to_broadcast([P, T]))
            d = DV.do(lambda e: e.tensor_copy(ANG[:, :], POS[:, :]), d)
            d = DV.do(lambda e: e.tensor_scalar(ANG[:, :], ANG[:, :], CST[:, C_INV:C_INV + 1], None, ALU.mult), d)
            d = DV.do(lambda e: e.tensor_scalar(NN[:, :], ANG[:, :], 0.15915494309189535, 12582912.0, ALU.mult,
                                                ALU.add), d)
            d = DV.do(lambda e: e.tensor_scalar(NM[:, :], NN[:, :], 12582912.0, None, ALU.subtract), d)
            for c in (6.28125, 0.0019340515136718750, 1.2556659146e-06):
                d = DV.do(lambda e: e.scalar_tensor_tensor(ANG[:, :], NM[:, :], -c, ANG[:, :], ALU.mult, ALU.add), d)
            d = DV.do(lambda e: e.tensor_scalar(ANG[:, :], ANG[:, :], 3.1415925, -3.1415925, ALU.min, ALU.max), d)
            m = AC.do(lambda e: e.activation(SIN[:, :], ANG[:, :], ACT.Sin), d)
            m2 = AC.do(lambda e: e.activation(NN[:, :], ANG[:, :], ACT.Abs), d)
            m2 = AC.do(lambda e: e.activation(COS[:, :], NN[:, :], ACT.Sin, bias=PIV, scale=-1.0), m2)
            return [DV.do(lambda e: e.tensor_scalar(SIN[:, :], SIN[:, :], CST[:, C_SGN:C_SGN + 1], None, ALU.mult), m),
                    m2]

        silc = AC.do(lambda e: e.activation(SILC[:, :], SM[:, S_CC:S_CC + 16], ACT.Silu))
        c2 = SILC[:, :].rearrange("p (k c) -> p k c", c=2)
        silc = AC.do(lambda e: e.activation(SILH[:, :, 0:2], c2, ACT.Copy), silc)
        silc = DV.do(lambda e: e.tensor_tensor(SILH[:, :, 2:4], c2, SILH[:, :, 0:2].bitcast(F32), ALU.subtract), silc)
        mod_rows, mod_ready = [], {}

        def mods_finish():
            m = None
            while mod_rows:
                i, mr, nr, ready = mod_rows.pop(0)
                b = BANKS.next()
                PE.wait(ready, b.busy)
                for t in range(2):
                    f = lambda e: e.matmul(b.t[:, 2 * t:2 * t + 2], mr.t[0:nr, t * P:(t + 1) * P],
                                           CST[0:nr, C_SEL:C_SEL + 2], start=True, stop=True)
                    m = PE.do(f) if t else PE.quiet(f)
                mr.busy = [m]
                m = DV.do(lambda e: e.tensor_tensor(
                    MOD[:, 2 * i:2 * i + 2, :], b.t[:, 0:4].rearrange("p (a b) -> p a b", a=2),
                    SM[:, S_BMOD + 2 * i:S_BMOD + 2 * i + 2].unsqueeze(2).to_broadcast([P, 2, 2]), ALU.add), m)
                b.busy = [m]
                mod_ready[i] = m
            return m

        def mod_chunk(i, w, wl, wm):
            b = BANKS.next()
            PE.wait(wm, silc, b.busy)
            nr = 2 if wl is None else 4
            for k in range(KD):
                c = slice(k * 256, k * 256 + 256)
                last = k == KD - 1
                if wl is None:
                    f = lambda e: e.matmul(b.t[0:2, 0:T], SILC[:, 2 * k:2 * k + 2], w[:, c],
                                           start=(k == 0), stop=last)
                else:
                    PE.quiet(lambda e: e.matmul(b.t[0:4, 0:T], SILH[:, k, :], w[:, c], start=(k == 0), stop=False))
                    f = lambda e: e.matmul(b.t[0:4, 0:T], SILH[:, k, :], wl[:, c], start=False,
                                           stop=last)
                m = PE.do(f) if last else PE.quiet(f)
            mods_finish()
            mr = MR.next()
            m = DV.do(lambda e: e.tensor_copy(mr.t[0:nr, :], b.t[0:nr, 0:T]), m, mr.busy)
            b.busy = [m]
            mod_rows.append((i, mr, nr, m))

        def mods(n):
            for _ in range(n):
                j, w, wl, wm = take("mod")
                mod_chunk(plan[j][1], w, wl, wm)
                done(j)
                pump()

        HH = ph("HH", 0, [P, KD, T], F32R)
        HL = ph("HL", 8, [P, KD, T], F32R)
        HCH = ph("HCH", 16, [P, KD, T], F32R)
        HCL = ph("HCL", 24, [P, KD, T], F32R)

        def scale_of(dst, gcol, mcol, which, marks):
            d = DV.do(lambda e: e.tensor_scalar(VEC[:, dst:dst + 8], MOD[:, mcol:mcol + 8, which], 1.0, None,
                                                ALU.add), marks)
            return DV.do(lambda e: e.tensor_tensor(VEC[:, dst:dst + 8], VEC[:, dst:dst + 8], SM[:, gcol:gcol + 8],
                                                   ALU.mult), d)

        def halves_of(tmp, dh, dl, marks_h=(), marks_l=()):
            h = AC.do(lambda e: e.activation(dh, tmp, ACT.Copy), marks_h)
            low = DV.do(lambda e: e.tensor_tensor(dl, tmp, dh.bitcast(F32), ALU.subtract), h, marks_l)
            return [h, low]

        class Modulated:

            def __init__(self, src, r, av, mcol, which, dh, dl, marks):
                self.a, self.ready = (src, r, av, mcol, which, dh, dl, marks), []

            def run(self, k0, k1, shift_ready=()):
                src, r, av, mcol, which, dh, dl, marks = self.a

                def scaled(k):
                    ta = TA.next()
                    d = DV.do(lambda e: e.scalar_tensor_tensor(ta.t[:, :], src[:, k, :], VEC[:, av + k:av + k + 1],
                                                               r[0].t[:, 0:T], ALU.mult, ALU.mult), r[1], marks,
                              ta.busy)
                    h = AC.do(lambda e: e.activation(dh[:, k, :], ta.t[:, :], ACT.Identity,
                                                     bias=MOD[:, mcol + k, which:which + 1]), d, shift_ready)
                    return ta, h

                nxt = scaled(k0)
                for k in range(k0, k1):
                    ta, h = nxt
                    if k + 1 < k1:
                        nxt = scaled(k + 1)
                    low = DV.do(lambda e: e.scalar_tensor_tensor(
                        dl[:, k, :], ta.t[:, :], MOD[:, mcol + k, which:which + 1], dh[:, k, :].bitcast(F32), ALU.add,
                        ALU.subtract), h, shift_ready)
                    ta.busy = [h, low]
                    self.ready.append([h, low])
                r[0].busy = [low]

        AC.quiet(lambda e: e.preload_act_table_set("sqrt_and_others"))
        def first(i):
            t_, m = FIRST[i]
            mod_chunk(i, t_, None, m)

        nx, nc_ = Norm(), Norm(PO)
        first(4)
        for k in range(KD):
            nx.add(X[:, k, :], xin)
        first(5)
        first(6)
        nx.sums(D)
        first(7)
        rx = nx.spread()
        first(0)
        va = scale_of(0, S_GMIX, 8, 0, mod_ready[7])
        for k in range(KD):
            nc_.add(XC[:, k, :], cin)
        mx_ = Modulated(X, rx, 0, 0, 0, HH, HL, [va])
        first(1)
        mx_.run(0, 2, mod_ready[0])
        nc_.sums(D)
        first(2)
        mx_.run(2, 4, mod_ready[1])
        pump()
        rc = nc_.spread()
        first(3)
        mx_.run(4, 6, mod_ready[2])
        mods_finish()
        mx_.run(6, 8, mod_ready[3])
        vc = scale_of(8, S_GMIX, 8, 1, [])
        mc_ = Modulated(XC, rc, 8, 0, 1, HCH, HCL, [vc])
        mc_.run(0, 8)
        hxs, hcs = mx_.ready, mc_.ready
        hx, hc = hxs[-1], hcs[-1]

        g0 = SM[:, S_LBG:S_LBG + 8]
        g1 = SM[:, S_LBG + 8:S_LBG + 16]
        L = lambda i: LBV[:, 8 * i:8 * i + 8]
        d = DV.do(lambda e: e.tensor_tensor(L(0), g0, g1, ALU.max))
        DV.do(lambda e: e.tensor_tensor(L(1), g0, L(0), ALU.subtract), d)
        d = DV.do(lambda e: e.tensor_tensor(L(2), g1, L(0), ALU.subtract), d)
        m = AC.do(lambda e: e.activation(LBV[:, 8:24], LBV[:, 8:24], ACT.Exp), d)
        d = DV.do(lambda e: e.tensor_tensor(L(0), L(1), L(2), ALU.add), m)
        d = DV.do(lambda e: e.reciprocal(L(3), L(0)), d)
        d = DV.do(lambda e: e.tensor_tensor(L(4), L(1), L(3), ALU.mult), d)
        lbm = DV.do(lambda e: e.tensor_scalar(L(5), L(4), -1.0, 1.0, ALU.mult, ALU.add), d)
        LB = lambda i: LBV[:, 32 + i:33 + i]
        OMLB = lambda i: LBV[:, 40 + i:41 + i]

        g2h = DV.do(lambda e: e.tensor_scalar(NG2H[:, :], SM[:, S_NG2:S_NG2 + 96], 0.5, None, ALU.mult))


        FX = ph("FX", 32, [P, 8, T])
        FC = ph("FC", 40, [P, 8, T])
        VTX = ph("VTX", 48, [P, 2, 512])
        VTC = ph("VTC", 52, [P, 2, 512])
        Q = ph("Q", 56, [P, 4, T])
        VB = ph("VB", 60, [P, 2, 512])
        S0 = ph("S0", 64, [P, 8, P])
        O = ph("O", 68, [P, 4, T])
        GA = ph("GA", 16, [P, 8, T])
        GB = ph("GB", 24, [P, 8, T])
        OG = ph("OG", 40, [P, 4, T])
        UU = ph("UU", 44, [P, 4, T])

        fmark = {}
        for c0 in (0, 2):
            got = None
            for src, (xh, xl, rd, dst) in enumerate(((HH, HL, hxs, FX), (HCH, HCL, hcs, FC))):
                grp = ByK(["win"] * 2, xh, xl, got=got, keep=(src == 0))
                got = grp.got
                for k in range(KD):
                    grp.run(k, rd[k])
                for z, b in enumerate(grp.banks):
                    c = c0 + z
                    m = AC.do(lambda e: e.activation(
                        dst[:, 2 * c:2 * c + 2, :], b.t[:, :].rearrange("p (a b) -> p a b", a=2), ACT.Sigmoid), b.done)
                    b.busy = [m]
                    for t in range(2):
                        i = 2 * c + t
                        fmark[(src, i)] = DV.do(lambda e: e.tensor_scalar(
                            dst[:, i, :], dst[:, i, :], OMLB(i), LB(i), ALU.mult, ALU.add), m, lbm)
            pump()

        def tokens(w, wl, xh, xl, kt, t, out_, cols, marks):
            for k in range(kt):
                m = mm3(out_, xh[:, k, t * P:(t + 1) * P], xl[:, k, t * P:(t + 1) * P], cols(w, k), cols(wl, k),
                        k == 0, k == kt - 1, k == kt - 1, marks if k == 0 else ())
            return m

        c256 = lambda w, k: w[:, k * 256:k * 256 + 256]
        vm = []
        for c in range(2):
            j, w, wl, wm = take("win")
            for src, (xh, xl, rd, dst) in enumerate(((HH, HL, hx, VTX), (HCH, HCL, hc, VTC))):
                b = BANKS.next()
                for t in range(2):
                    m = tokens(w, wl, xh, xl, KD, t, b.t[:, t * T:(t + 1) * T], c256, [wm, rd, b.busy])
                if src:
                    done(j)
                m = AC.do(lambda e, dst=dst, c=c: e.activation(
                    dst[:, :, c * 256:(c + 1) * 256], b.t[:, :].rearrange("p (a b) -> p a b", a=2), ACT.Copy), m)
                b.busy = [m]
                vm.append(m)
            pump()
        ctx_read = PE.mark

        def plain(dst, kind, col, marks=()):
            j, b, ms = pair(kind, HH, HL, hx)
            done(j)
            m = AC.do(lambda e: e.activation(dst[:, col:col + 2, :], b.t[:, :].rearrange("p (a b) -> p a b", a=2),
                                             ACT.Copy), ms[1], marks)
            mods_finish()
            b.busy = [m]
            pump()
            return m

        def vb_chunk(c):
            j, w, wl, wm = take("win")
            b = BANKS.next()
            for t in range(2):
                m = tokens(w, wl, HH, HL, KD, t, b.t[:, t * T:(t + 1) * T], c256, [wm, b.busy])
            done(j)
            m = AC.do(lambda e: e.activation(VB[:, :, c * 256:(c + 1) * 256],
                                             b.t[:, :].rearrange("p (a b) -> p a b", a=2), ACT.Copy), m)
            b.busy = [m]
            pump()

        for i in range(3):
            row = load_small(ROW[:, i, :], a["rows"][i:i + 1, :].to_broadcast([P, 512]))
        row = load_small(WST[:, :, :], a["wst"])

        Lc = ph("Lc", 80, [P, 8, T])
        Pc = ph("Pc", 88, [P, 8, T])
        Kc = ph("Kc", 96, [P, 8, T])
        AC.quiet(lambda e: e.preload_act_table_set("natural_log_exp_and_others"))
        a1 = AC.do(lambda e: e.activation(Lc[:, :, :], FC[:, :, :], ACT.Ln), [fmark[(1, i)] for i in range(8)], hc)
        kc = DV.do(lambda e: e.tensor_scalar(FC[:, :, :], FC[:, :, :], -1.0, 1.0, ALU.mult, ALU.add), a1)
        for i in range(8):
            p1 = DV.do(lambda e: e.tensor_tensor_scan(Pc[:, i, :], ONE[:, 0:1].to_broadcast([P, T]), Lc[:, i, :], 0.0,
                                                      ALU.mult, ALU.add), a1)
        cx = []
        for i in range(4):
            d = DV.do(lambda e: e.tensor_scalar(Pc[:, i, :], Pc[:, i, :], -1.0, Pc[:, i, T - 1:T], ALU.mult, ALU.add), p1)
        a2 = AC.do(lambda e: e.activation(Pc[:, 0:4, :], Pc[:, 0:4, :], ACT.Exp), d)
        d = DV.do(lambda e: e.tensor_tensor(Pc[:, 4:8, :], Pc[:, 4:8, :], Lc[:, 4:8, :], ALU.subtract), p1)
        a3 = AC.do(lambda e: e.activation(Pc[:, 4:8, :], Pc[:, 4:8, :], ACT.Exp), d)
        cx.append(DV.do(lambda e: e.tensor_tensor(Pc[:, 0:4, :], Pc[:, 0:4, :], FC[:, 0:4, :], ALU.mult), a2, kc))
        cx.append(DV.do(lambda e: e.tensor_tensor(Pc[:, 4:8, :], Pc[:, 4:8, :], FC[:, 4:8, :], ALU.mult), a3))
        fc_read = cx[1]
        qm = [plain(Q, "win", 2 * c) for c in range(2)]

        def transposed(src, dst, hs, marks, busy=()):
            b = BANKS.next()
            PE.wait(marks, b.busy)
            for z in range(4):
                f = lambda e: e.transpose(b.t[:, z * P:(z + 1) * P],
                                          src[:, hs + z // 2, (z % 2) * P:(z % 2 + 1) * P], IDN)
                m = PE.do(f) if z == 3 else PE.quiet(f)
            c = AC.do(lambda e: e.activation(dst[:, hs:hs + 2, :], b.t[:, :].rearrange("p (a b) -> p a b", a=2),
                                             ACT.Copy), m, *busy)
            b.busy = [c]
            return c, m

        kcm = [transposed(Pc, Kc, 2 * z, cx[z // 2])[0] for z in range(4)]

        LG = ph("LG", 16, [P, 4, T])
        PF = ph("PF", 20, [P, 4, T])
        DD = ph("DD", 24, [P, 4, T])
        RM = ph("RM", 28, [P, T])
        E0 = ph("E0", 80, [P, 4, T])
        E1 = ph("E1", 84, [P, 4, T])
        QI = ph("QI", 88, [P, 4, T])
        KI = ph("KI", 92, [P, 4, T])
        KD_ = ph("KD_", 96, [P, 4, T])
        KT = ph("KT", 100, [P, 4, T])
        SC = ph("SC", 104, [P, 4, P])
        SS = at("SS", [P, 12, P], ss_at)
        AV = VEC[:, 24:40]
        HV = VEC[:, 44:60]
        rm = DV.do(lambda e: e.memset(RM[:, :], 1.0), ctx_read)
        rm = DV.do(lambda e: e.memset(RM[:, 0:T:64], 0.0), rm)
        use = {n: [] for n in ("lg", "pf", "dd", "e0", "e1", "qi", "ki", "kd", "kt", "sc", "ss", "av", "hv")}

        def c16(t):
            return t[:, :, :].rearrange("p h (n c) -> p (h n) c", c=64)

        def bc(v, n=64):
            return v.unsqueeze(2).to_broadcast([P, v.shape[1], n])

        def gla_terms(dr, first):
            u = {}
            hs = slice(4 * dr, 4 * dr + 4)
            F = FX[:, hs, :]
            a1 = AC.do(lambda e: e.activation(LG[:, :, :], F, ACT.Ln), [fmark[(0, i)] for i in range(8)], first,
                       use["lg"])
            k1 = DV.do(lambda e: e.tensor_scalar(F, F, -1.0, 1.0, ALU.mult, ALU.add), a1)
            for h in range(4):
                p1 = DV.do(lambda e: e.tensor_tensor_scan(PF[:, h, :], RM[:, :], LG[:, h, :], 0.0, ALU.mult, ALU.add),
                           a1, rm, use["pf"])
            tot = c16(PF)[:, :, 63]
            d1 = DV.do(lambda e: e.tensor_scalar(HV, tot, 0.5, None, ALU.mult), p1, use["hv"])
            a2 = AC.do(lambda e: e.activation(AV, tot, ACT.Exp), p1, use["av"])
            if dr:
                d2 = DV.do(lambda e: e.tensor_tensor(LG[:, :, :], PF[:, :, :], LG[:, :, :], ALU.subtract), p1)
                B_, bm = LG, d2
            else:
                B_, bm = PF, p1
            d3 = DV.do(lambda e: e.tensor_tensor(c16(DD), c16(B_), bc(HV), ALU.subtract), d1, bm, use["dd"])
            use["hv"] = [d3]
            sg = 1.0 if dr == 0 else -1.0
            a3 = AC.do(lambda e: e.activation(E0[:, :, :], DD[:, :, :], ACT.Exp, scale=sg), d3, use["e0"], first)
            a4 = AC.do(lambda e: e.activation(E1[:, :, :], DD[:, :, :], ACT.Exp, scale=-sg), d3, use["e1"])
            d4 = DV.do(lambda e: e.tensor_tensor(QI[:, :, :], Q[:, :, :], E0[:, :, :], ALU.mult), a3, qm, use["qi"])
            u["d5"] = DV.do(lambda e: e.tensor_tensor(KI[:, :, :], F, E1[:, :, :], ALU.mult), a4, k1, use["ki"])
            d6 = DV.do(lambda e: e.tensor_tensor(c16(DD), bc(tot), c16(B_), ALU.subtract), a3, a4)
            a5 = AC.do(lambda e: e.activation(E0[:, :, :], B_[:, :, :], ACT.Exp), d4, bm)
            a6 = AC.do(lambda e: e.activation(E1[:, :, :], DD[:, :, :], ACT.Exp), u["d5"], d6)
            use["dd"] = [a6]
            use["lg"] = use["pf"] = [a5, a6, a2, d6]
            eq, ek = (E0, E1) if dr == 0 else (E1, E0)
            u["d7"] = DV.do(lambda e: e.tensor_tensor(KD_[:, :, :], F, ek[:, :, :], ALU.mult), a5, a6, use["kd"], first)
            u.update(d4=d4, a2=a2, eq=eq, am=[a5, a6])
            return u

        def gla_scores(dr, u, first):
            b = BANKS.next()
            PE.wait(u["d4"], u["d5"], b.busy)
            for h in range(4):
                for n in range(4):
                    p0 = 64 * (n % 2)
                    c = h * P + (n // 2) * 64
                    f = lambda e: e.matmul(b.t[p0:p0 + 64, c:c + 64], KI[:, h, n * 64:n * 64 + 64],
                                           QI[:, h, n * 64:n * 64 + 64], start=True, stop=True)
                    m = PE.do(f) if (h == 3 and n == 3) else PE.quiet(f)
            use["ki"] = [m]
            c = AC.do(lambda e: e.activation(SC[:, :, :], b.t[:, :].rearrange("p (a b) -> p a b", a=4), ACT.Copy), m,
                      use["sc"], first)
            b.busy = [c]
            u["d8"] = DV.do(lambda e: e.tensor_tensor(QI[:, :, :], Q[:, :, :], u["eq"][:, :, :], ALU.mult), m, u["am"])
            use["e0"] = use["e1"] = [u["d7"], u["d8"]]
            s_ = 1 if dr == 0 else -1
            for p0 in (0, 64):
                v = SC[p0:p0 + 64, :, :].rearrange("p h (a b) -> p (h a) b", a=2)
                u["g"] = PO.do(lambda e: e.affine_select(out=v, in_=v, compare_op=ALU.is_ge, fill=0.0, base=0,
                                                         pattern=[[0, 8], [s_, 64]], channel_multiplier=-s_), c)
            for z in range(2):
                u["kt"], m = transposed(KD_, KT, 2 * z, u["d7"], (use["kt"], first))
            use["kd"] = [m]

        def gla_states(dr, u):
            b3 = [BANKS.next() for _ in range(3)]
            PE.wait(u["kt"], [b.busy for b in b3], vm)
            adds = [0, 1, 2] if dr == 0 else [3, 2, 1]

            def at_(h, z):
                return (b3[2], h * P) if z == 1 else (b3[h // 2], (2 * (h % 2) + z // 2) * P)

            for h in range(4):
                for z, n in enumerate(adds):
                    p0, t = 64 * (n % 2), n // 2
                    b, c = at_(h, z)
                    f = lambda e: e.matmul(b.t[:, c:c + P], KT[p0:p0 + 64, h, t * P:(t + 1) * P],
                                           VTX[p0:p0 + 64, t, h * P:(h + 1) * P], start=True, stop=True)
                    m = PE.do(f) if (h == 3 and z == 2) else PE.quiet(f)
            use["kt"] = [m]
            pm = [s0m[dr]] * 4
            for z, n in enumerate(adds):
                for h in range(4):
                    b, c = at_(h, z)
                    prev = S0[:, 4 * dr + h, :] if z == 0 else SS[:, 3 * h + z - 1, :]
                    pm[h] = DV.do(lambda e: e.scalar_tensor_tensor(
                        SS[:, 3 * h + z, :], prev, AV[:, 4 * h + n:4 * h + n + 1], b.t[:, c:c + P], ALU.mult, ALU.add),
                        m, pm[h], u["a2"], use["ss"])
            for b in b3:
                b.busy = [pm[3]]
            use["av"] = [pm[3]]
            u["pm"] = pm[3]

        def gla_out(dr, u):
            b2 = [BANKS.next(), BANKS.next()]
            PE.wait(b2[0].busy, b2[1].busy, u["g"], u["d8"], u["pm"])
            for h in range(4):
                for n in range(4):
                    p0, t = 64 * (n % 2), n // 2
                    c = h * P + t * 64
                    z = n if dr == 0 else 3 - n
                    st = S0[:, 4 * dr + h, :] if z == 0 else SS[:, 3 * h + z - 1, :]
                    o_ = b2[n % 2].t[:, c:c + 64]
                    PE.quiet(lambda e: e.matmul(o_, VTX[p0:p0 + 64, t, h * P:(h + 1) * P],
                                                SC[p0:p0 + 64, h, t * 64:t * 64 + 64], start=True, stop=False))
                    f = lambda e: e.matmul(o_, st, QI[:, h, n * 64:n * 64 + 64], start=False, stop=True)
                    m = PE.do(f) if (h == 3 and n == 3) else PE.quiet(f)
            for n in ("sc", "qi", "ss"):
                use[n] = [m]
            for z in range(2):
                v = O[:, :, :].rearrange("p h (t z c) -> p h t z c", t=2, z=2)[:, :, :, z, :]
                s_ = b2[z].t[:, :].rearrange("p (h t c) -> p h t c", h=4, t=2)
                if dr == 0:
                    u["o"] = DV.do(lambda e: e.tensor_copy(v, s_), m)
                else:
                    u["o"] = DV.do(lambda e: e.tensor_tensor(v, v, s_, ALU.add), m, u0["o"])
                b2[z].busy = [u["o"]]

        vb_chunk(0)
        s0m = []
        for dr in range(2):
            b = BANKS.next()
            PE.wait(kcm, b.busy, vm)
            for h in range(4):
                for t in range(2):
                    f = lambda e: e.matmul(b.t[:, h * P:(h + 1) * P], Kc[:, 4 * dr + h, t * P:(t + 1) * P],
                                           VTC[:, t, h * P:(h + 1) * P], start=(t == 0), stop=(t == 1))
                    m = PE.do(f) if (h == 3 and t == 1) else PE.quiet(f)
            s0m.append(DV.do(lambda e: e.tensor_copy(S0[:, 4 * dr:4 * dr + 4, :],
                                                     b.t[:, :].rearrange("p (a b) -> p a b", a=4)), m))
            b.busy = [s0m[-1]]
        ctx_done = [m, s0m[1]]
        u0 = gla_terms(0, ctx_done)
        vb_chunk(1)
        ogm, um, gam, gbm = [], [], [], []
        mods(2)
        ogm.append(plain(OG, "win", 0, fc_read))
        gla_scores(0, u0, ctx_done)
        mods(2)
        gla_states(0, u0)
        ogm.append(plain(OG, "win", 2, fc_read))
        mods(1)
        gla_out(0, u0)
        u1 = gla_terms(1, [])
        mods(1)
        um.append(plain(UU, "win", 0, fc_read))
        gla_scores(1, u1, [])
        mods(2)
        gla_states(1, u1)
        um.append(plain(UU, "win", 2, fc_read))
        mods(1)
        gla_out(1, u1)
        gla_free = [use["lg"], use["dd"], DV.mark]
        gam.append(plain(GA, "win", 0, gla_free))
        om = u1["o"]
        AH = ph("AH", 80, [P, 8, T], F32R)
        AL = ph("AL", 88, [P, 8, T], F32R)
        SG = ph("SG", 96, [P, 4, T])
        DG4 = ph("DG4", 100, [P, 4, T])
        GV = ph("GV", 64, [P, 2, 512])
        GU = ph("GU", 48, [P, 4, T])
        ST = ph("ST", 52, [P, 48])

        def gates():
            mods(1)
            c = len(gam) + len(gbm)
            if c < 4:
                gam.append(plain(GA, "win", 2 * c, []))
            else:
                gbm.append(plain(GB, "win", 2 * (c - 4), []))

        gates()
        m = AC.do(lambda e: e.activation(SG[:, :, :], O[:, :, :], ACT.Square), om)
        b = BANKS.next()
        PE.wait(m, b.busy)
        for h in range(4):
            for t in range(2):
                f = lambda e: e.matmul(b.t[:, 2 * h + t:2 * h + t + 1], SG[:, h, t * P:(t + 1) * P],
                                       ONE[:, 0:1], start=True, stop=True)
                m = PE.do(f) if (h == 3 and t == 1) else PE.quiet(f)
        m = AC.do(lambda e: e.activation(ST[:, 24:32], b.t[:, 0:8], ACT.Sqrt, bias=EPSV, scale=1.0 / P), m)
        b.busy = [m]
        d = DV.do(lambda e: e.reciprocal(ST[:, 32:40], ST[:, 24:32]), m)
        for z in range(8):
            dg = DV.do(lambda e: e.tensor_scalar(DG4[:, z // 2, (z % 2) * P:(z % 2 + 1) * P], IDN,
                                                 ST[:, 32 + z:33 + z], None, ALU.mult), d)
        gv = AC.do(lambda e: e.activation(GV[:, :, :], VB[:, :, :], ACT.Gelu_apprx_tanh))
        gu = AC.do(lambda e: e.activation(GU[:, :, :], UU[:, :, :], ACT.Gelu_apprx_tanh))
        for t in range(2):
            d = DV.do(lambda e: e.bn_stats(ST[:, 6 * t:6 * t + 6], GV[:, t, :]), gv)
            d = DV.do(lambda e: e.bn_aggr(ST[:, 12 + 2 * t:14 + 2 * t], ST[:, 6 * t:6 * t + 6]), d)
        m = AC.do(lambda e: e.activation(ST[:, 16:18], ST[:, 13:17:2], ACT.Sqrt, bias=EPSV, scale=1.0), d)
        d = DV.do(lambda e: e.reciprocal(ST[:, 18:20], ST[:, 16:18]), m)
        sg = AC.do(lambda e: e.activation(SG[:, :, :], OG[:, :, :], ACT.Sigmoid), m)
        gates()
        for t in range(2):
            b = BANKS.next()
            m = PE.do(lambda e: e.matmul(b.t[:, :], ONE, DG4[:, 2 * t:2 * t + 2, :].rearrange("p a b -> p (a b)"),
                                         start=True, stop=True), dg, b.busy)
            o_ = O[:, 2 * t:2 * t + 2, :]
            om = DV.do(lambda e: e.scalar_tensor_tensor(o_, o_, SM[:, S_GNA:S_GNA + 1],
                                                        b.t[:, :].rearrange("p (a b) -> p a b", a=2), ALU.mult,
                                                        ALU.mult), m, om)
            b.busy = [om]
        for t in range(2):
            d1 = DV.do(lambda e: e.tensor_scalar(GV[:, t, :], GV[:, t, :], ST[:, 12 + 2 * t:13 + 2 * t],
                                                 ST[:, 18 + t:19 + t], ALU.subtract, ALU.mult), d)
            d1 = DV.do(lambda e: e.tensor_tensor(GV[:, t, :], GV[:, t, :], ROW[:, 0, :], ALU.mult), d1, row)
            d1 = DV.do(lambda e: e.tensor_tensor(GV[:, t, :], GV[:, t, :], ROW[:, 1, :], ALU.add), d1)
        gates()
        d = DV.do(lambda e: e.tensor_tensor(SG[:, :, :], SG[:, :, :], OG[:, :, :], ALU.mult), sg, ogm)
        d = DV.do(lambda e: e.tensor_tensor(O[:, :, :], O[:, :, :], SG[:, :, :], ALU.mult), d, om)
        ah, al = halves_of(O[:, :, :], AH[:, 0:4, :], AL[:, 0:4, :], d)
        gates()
        for g in range(4):
            b = BANKS.next()
            PE.wait(d1, row, b.busy)
            for n in range(2):
                f = lambda e: e.matmul(b.t[:, n * P:(n + 1) * P], GV[:, n, g * P:(g + 1) * P],
                                       WST[:, g, :], start=True, stop=True)
                m = PE.do(f) if n else PE.quiet(f)
            ta = TA.next()
            d2 = DV.do(lambda e: e.tensor_tensor(
                ta.t[:, :].rearrange("p (a b) -> p a b", a=2), b.t[:, 0:T].rearrange("p (a b) -> p a b", a=2),
                ROW[:, 2, g * P:(g + 1) * P].unsqueeze(1).to_broadcast([P, 2, P]), ALU.add), m, ta.busy)
            b.busy = [d2]
            d2 = DV.do(lambda e: e.tensor_tensor(GU[:, g, :], GU[:, g, :], ta.t[:, :], ALU.mult), d2, gu)
            ta.busy = [d2]
        gates()
        bh, bl = halves_of(GU[:, :, :], AH[:, 4:8, :], AL[:, 4:8, :], d2)
        gates()
        m3 = AC.do(lambda e: e.activation(GA[:, :, :], GA[:, :, :], ACT.Sigmoid), gam)
        gates()
        mods_finish()
        m3 = AC.do(lambda e: e.activation(GB[:, :, :], GB[:, :, :], ACT.Sigmoid), gbm)

        MG = ph("MG", 32, [P, 8, T])
        MH = ph("MH", 48, [P, 8, T], F32R)
        ML = ph("ML", 56, [P, 8, T], F32R)
        for which, (kind, g_, rd) in enumerate((("wpa", GA, [ah, al]), ("wpb", GB, [bh, bl]))):
            for c in range(2):
                j, w, wl, wm = take(kind)
                for t2 in range(2):
                    b = BANKS.next()
                    for t in range(2):
                        col = (2 * t2 + t) * P
                        m = project(w, wl, lambda k, col=col: (k * 512 + col, k * 512 + col + P), 4,
                                    AH[:, 4 * which:4 * which + 4, :], AL[:, 4 * which:4 * which + 4, :],
                                    b.t[:, t * T:(t + 1) * T], [wm, rd, b.busy])
                    mt = 4 * c + 2 * t2
                    v = b.t[:, :].rearrange("p (a b) -> p a b", a=2)
                    if which == 0:
                        d = DV.do(lambda e, mt=mt, v=v: e.tensor_tensor(MG[:, mt:mt + 2, :], v, GA[:, mt:mt + 2, :],
                                                                        ALU.mult), m, m3)
                        b.busy = [d]
                    else:
                        d = DV.do(lambda e, mt=mt, v=v: e.tensor_tensor(GB[:, mt:mt + 2, :], v, GB[:, mt:mt + 2, :],
                                                                        ALU.mult), m, m3)
                        b.busy = [d]
                        d = DV.do(lambda e, mt=mt: e.tensor_tensor(MG[:, mt:mt + 2, :], MG[:, mt:mt + 2, :],
                                                                   GB[:, mt:mt + 2, :], ALU.add), d)
                        mh, ml = halves_of(MG[:, mt:mt + 2, :], MH[:, mt:mt + 2, :], ML[:, mt:mt + 2, :], d)
                done(j)
                pump()

        n2 = Norm()
        for c in range(4):
            j, b, ms = pair("wo", MH, ML, [mh, ml])
            done(j)
            for t in range(2):
                mt = 2 * c + t
                d = DV.do(lambda e, mt=mt, t=t: e.scalar_tensor_tensor(
                    X[:, mt, :], b.t[:, t * T:(t + 1) * T], MOD[:, 16 + mt, 0:1], X[:, mt, :], ALU.mult, ALU.add),
                    ms[t])
                n2.add(X[:, mt, :], d)
            b.busy = [d]
            pump()
        vf = scale_of(40, S_GFFN, 32, 0, [])
        n2.sums(D)
        r2 = n2.spread(copy=False)
        XH = ph("XH", 0, [P, KD, T], F32R)
        XL = ph("XL", 8, [P, KD, T], F32R)
        GH = ph("GH", 16, [P, FT, T], F32R)
        GL = ph("GL", 38, [P, FT, T], F32R)
        FG = ph("FG", 60, [P, KD, T])
        mf_ = Modulated(X, r2, 40, 24, 0, XH, XL, [vf])
        mf_.run(0, 8)
        hx2 = mf_.ready

        def ffn_up(kind, ready, nn):
            banks = by_k([kind] * 2, XH, XL, ready)
            if nn:
                nn.sums(D)
            AC.quiet(lambda e: e.preload_act_table_set("silu_and_others"))
            marks, pend = [], None

            def low_half(c, tc, h):
                low = DV.do(lambda e: e.tensor_tensor(GL[:, c, :], tc.t[:, :], GH[:, c, :].bitcast(F32),
                                                      ALU.subtract), h)
                tc.busy = [h, low]
                marks.append([h, low])

            ms = [None, None]
            for c in range(FT):
                if c < 2:
                    b = banks[c]
                    m = b.done
                    if c == 0:
                        j, b2, m2 = pair(kind, XH, XL, ready[-1])
                        done(j)
                        if nn:
                            rb, rbm = nn.spread()
                elif c == 2:
                    b, m = b2, m2[1]
                else:
                    j, b, ms = pair(kind, XH, XL, ready[-1])
                    done(j)
                    m = ms[1]
                ta, tb, tc = TA.next(), TB.next(), TC.next()
                gate, up = b.t[:, 0:T], b.t[:, T:2 * T]
                if nn is None:
                    s2 = AC.do(lambda e: e.activation(tb.t[:, :], gate, ACT.Silu), m, tb.busy)
                    f2 = tb
                else:
                    g = DV.do(lambda e: e.tensor_tensor(ta.t[:, :], gate, rb.t[:, :], ALU.mult), m, ta.busy, rbm)
                    s1 = AC.do(lambda e: e.activation(tb.t[:, :], ta.t[:, :], ACT.Silu), g, tb.busy)
                    s2 = PO.do(lambda e: e.tensor_tensor(ta.t[:, :], tb.t[:, :], rb.t[:, :], ALU.mult), s1, rbm)
                    tb.busy = [s2]
                    f2 = ta
                if pend:
                    low_half(*pend)
                pump()
                d = DV.do(lambda e: e.tensor_tensor(tc.t[:, :], up, f2.t[:, :], ALU.mult), s2, tc.busy)
                f2.busy = [d]
                b.busy = [d]
                h = AC.do(lambda e: e.activation(GH[:, c, :], tc.t[:, :], ACT.Copy), d)
                pend = (c, tc, h)
            low_half(*pend)
            if nn:
                rb.busy = [PO.mark, DV.mark]
            return marks

        def ffn_down(kind, ready, each):
            for mt in range(KD):
                b = BANKS.next()
                for half in range(2):
                    j, w, wl, wm = take(kind)
                    for k in range(11):
                        kk = 11 * half + k
                        m = mm3(b.t[:, 0:T], w[:, k * P:(k + 1) * P], wl[:, k * P:(k + 1) * P], GH[:, kk, :],
                                GL[:, kk, :], kk == 0, kk == 21, k == 10, [wm, ready[kk], b.busy])
                    done(j)
                    if half == 0:
                        pump()
                each(mt, b, m)
                pump()

        up_ready = ffn_up("up", hx2, None)
        AC.quiet(lambda e: e.preload_act_table_set("sqrt_and_others"))
        nf = Norm()

        def after_first(mt, b, m):
            d = DV.do(lambda e: e.scalar_tensor_tensor(X[:, mt, :], b.t[:, 0:T], MOD[:, 40 + mt, 0:1], X[:, mt, :],
                                                       ALU.mult, ALU.add), m)
            b.busy = [d]
            nf.add(X[:, mt, :], d)

        ffn_down("down", up_ready, after_first)

        def G2(layer, i, k):
            c = S_NG2 + (layer * 6 + i) * 8 + k
            return SM[:, c:c + 1]

        def G2H(layer, i, k):
            c = (layer * 6 + i) * 8 + k
            return NG2H[:, c:c + 1]

        def next_halves(k, layer, i, d):
            h = AC.do(lambda e: e.activation(XH[:, k, :], X[:, k, :], ACT.Copy, scale=G2(layer, i, k)), d)
            return DV.do(lambda e: e.scalar_tensor_tensor(XL[:, k, :], X[:, k, :], G2(layer, i, k),
                                                          XH[:, k, :].bitcast(F32), ALU.mult, ALU.subtract), h)

        r = nf.finish(D)
        n2 = Norm()
        xs = []
        for k in range(KD):
            d = DV.do(lambda e, k=k: e.scalar_tensor_tensor(X[:, k, :], X[:, k, :], SM[:, S_GFIN + k:S_GFIN + k + 1],
                                                            r[0].t[:, :], ALU.mult, ALU.mult), r[2])
            xs.append(next_halves(k, 0, 0, d))
            n2.add(X[:, k, :], d)
        r[0].busy = [d]

        def collect(layer, i, half):
            n = Norm()
            marks = {}

            def each(mt, src, m):
                g = G2H(layer, i, mt) if half else G2(layer, i, mt)
                marks["sq"] = n.add(src, m)
                marks[mt] = AC.do(lambda e: e.activation(FG[:, mt, :], src, ACT.Copy, scale=g), m)
                return [marks[mt], marks["sq"]]

            return n, marks, each

        def residual(n, marks, layer, i):
            n.sums(D)
            rb, rbm = n.spread(copy=False)
            nn = Norm(PO) if layer is not None else None
            last, pend = [], None

            def low_half(k, h):
                low = DV.do(lambda e: e.scalar_tensor_tensor(XL[:, k, :], X[:, k, :], G2(layer, i, k),
                                                             XH[:, k, :].bitcast(F32), ALU.mult, ALU.subtract), h)
                last.append([h, low])

            def scaled(k):
                ta = TA.next()
                d = DV.do(lambda e: e.tensor_tensor(ta.t[:, :], FG[:, k, :], rb.t[:, 0:T], ALU.mult), rbm, marks[k],
                          ta.busy)
                return ta, d

            nxt = scaled(0)
            for k in range(KD):
                ta, d0 = nxt
                if k + 1 < KD:
                    nxt = scaled(k + 1)
                d = DV.do(lambda e: e.tensor_tensor(X[:, k, :], X[:, k, :], ta.t[:, :], ALU.add), d0)
                ta.busy = [d]
                if layer is not None:
                    h = AC.do(lambda e: e.activation(XH[:, k, :], X[:, k, :], ACT.Copy, scale=G2(layer, i, k)), d)
                    nn.add(X[:, k, :], d)
                    if pend:
                        low_half(*pend)
                    pend = (k, h)
                else:
                    last.append(d)
            if pend:
                low_half(*pend)
            rb.busy = [d]
            return nn, last

        def ffn2(layer, first, xs, n2):
            rd = ffn_up("up2", xs, n2)
            n, marks, each = collect(layer, 1 if first else 5, True)
            AC.quiet(lambda e: e.preload_act_table_set("sqrt_and_others"))

            def f(mt, b, m):
                b.busy = each(mt, b.t[:, 0:T], m)

            ffn_down("down2", rd, f)
            return n, marks

        def project_out(kind, AHt, ALt, rd, layer, group):
            AC.quiet(lambda e: e.preload_act_table_set("sqrt_and_others"))
            n, marks, each = collect(layer, 3, False)
            for c in range(4):
                if c < len(group.banks):
                    b = group.banks[c]
                    m = b.done
                else:
                    j, b, ms = pair(kind, AHt, ALt, rd[-1])
                    done(j)
                    m = ms[1]
                for t in range(2):
                    b.busy = each(2 * c + t, b.t[:, t * T:(t + 1) * T], m)
                pump()
            return n, marks

        n, marks = ffn2(0, True, xs, n2)
        n2, xs = residual(n, marks, 0, 2)
        VT = ph("VT", 16, [P, 2, 1024])
        OH = ph("OH", 24, [P, 8, T], F32R)
        OL = ph("OL", 32, [P, 8, T], F32R)
        QK = Turn([Slot(ph(f"QK{i}", 40 + 2 * i, [P, 2, T])) for i in range(2)])
        AB = Turn([Slot(ph(f"AB{i}", 60 + 1.5 * i, [P, 384])) for i in range(4)])
        LNB = Turn([Slot(ph(f"LNB{i}", 66 + 1.5 * i, [P, 384])) for i in range(4)])
        SPB = Turn([Slot(ph(f"SPB{i}", 72 + 1.5 * i, [P, 384])) for i in range(4)])
        AW = Turn([Slot(ph(f"AW{i}", 78 + 1.5 * i, [P, 384])) for i in range(4)])
        NU = at("NU", [P, 2, P], PB + 57 * KB)
        nu = DV.do(lambda e: e.tensor_scalar(NU[:, 0, :], TRI, -1.0, None, ALU.mult))
        nu = DV.do(lambda e: e.tensor_scalar(NU[:, 1, :], ONE, -1.0, None, ALU.mult))
        vts = []
        vb = by_k(["sbv"] * 2, XH, XL, xs, tokens=True)
        n2.sums(D)
        AC.quiet(lambda e: e.preload_act_table_set("natural_log_exp_and_others"))
        rt, rtm = n2.rt, n2.r
        for c in range(4):
            if c < 2:
                b, m = vb[c], vb[c].done
            else:
                j, w, wl, wm = take("sbv")
                b = BANKS.next()
                for t in range(2):
                    m = tokens(w, wl, XH, XL, KD, t, b.t[:, t * T:(t + 1) * T], c256, [wm, b.busy])
                done(j)
                if c == 2:
                    rb, rbm = n2.spread()
            for t in range(2):
                v = AC.do(lambda e, c=c, t=t: e.activation(VT[:, t, c * 256:(c + 1) * 256], b.t[:, t * T:(t + 1) * T],
                                                           ACT.Copy, scale=rt.t[:, t:t + 1]), m, rtm)
            b.busy = [v]
            vts.append(v)
            pump()
        rt.busy = [v]

        def sb_scores(qk, e_, ready):
            p0 = 64 * e_
            b = BANKS.next()
            kT = lambda t: qk.t[p0:p0 + 64, 1, t * P:(t + 1) * P]
            PE.wait(ready, b.busy)
            PE.quiet(lambda e: e.matmul(b.t[:, 0:256], kT(0), qk.t[p0:p0 + 64, 0, :], start=True, stop=False,
                                        skip_group_check=True))
            m = PE.do(lambda e: e.matmul(b.t[:, 256:384], kT(1), qk.t[p0:p0 + 64, 0, P:T], start=False, stop=False,
                                         skip_group_check=True))
            return b, m

        def sb_softplus(fr):
            st = [(b, m, AB.next(), LNB.next(), SPB.next()) for b, m in fr]
            s1 = [AC.do(lambda e: e.activation(ab.t[:, :], b.t[:, 0:384], ACT.Abs), m, ab.busy)
                  for b, m, ab, ln, sp in st]
            s2 = [AC.do(lambda e: e.activation(ab.t[:, :], ab.t[:, :], ACT.Exp, scale=-1.0), s)
                  for s, (b, m, ab, ln, sp) in zip(s1, st)]
            res = []
            for s, (b, m, ab, ln, sp) in zip(s2, st):
                s3 = AC.do(lambda e: e.activation(ln.t[:, :], ab.t[:, :], ACT.Ln, bias=ONE[:, 0:1]), s, ln.busy)
                ab.busy = [s3]
                d = DV.do(lambda e: e.scalar_tensor_tensor(sp.t[:, :], b.t[:, 0:384], 0.0, ln.t[:, :], ALU.max,
                                                           ALU.add), s3, sp.busy)
                ln.busy = [d]
                for o in (0, 256):
                    g = PO.do(lambda e: e.affine_select(
                        out=sp.t[:, o:o + P], in_=sp.t[:, o:o + P], compare_op=ALU.is_gt, fill=0.0, base=0,
                        pattern=[[1, P]], channel_multiplier=-1), d)
                res.append((b, sp, g))
            return res

        def sb_mid(b, sp, g):
            PE.wait(g, nu)
            PE.quiet(lambda e: e.matmul(b.t[:, 0:256], NU[:, 0, :], sp.t[:, 0:256], start=False, stop=False,
                                        skip_group_check=True))
            PE.quiet(lambda e: e.matmul(b.t[:, 128:256], NU[:, 1, :], sp.t[:, 256:384], start=False, stop=False,
                                        skip_group_check=True))
            m = PE.do(lambda e: e.matmul(b.t[:, 256:384], NU[:, 0, :], sp.t[:, 256:384], start=False, stop=True,
                                         skip_group_check=True))
            sp.busy = [m]
            return b, m

        def sb_weights(b, m):
            aw = AW.next()
            s = AC.do(lambda e: e.activation(aw.t[:, :], b.t[:, 0:384], ACT.Exp), m, aw.busy)
            b.busy = [s]
            for o in (0, 256):
                g = PO.do(lambda e: e.affine_select(
                    out=aw.t[:, o:o + P], in_=aw.t[:, o:o + P], compare_op=ALU.is_gt, fill=0.0, base=0,
                    pattern=[[1, P]], channel_multiplier=-1), s)
            return aw, g

        def sb_back(ob, h, aw, g):
            p0 = 64 * (h % 2)
            PE.wait(g, vts, ob.busy if h % 2 == 0 else [])
            v = lambda t: VT[:, t, h * 64:h * 64 + 64]
            PE.quiet(lambda e: e.matmul(ob.t[p0:p0 + 64, 0:256], v(0), aw.t[:, 0:256], start=True, stop=False,
                                        skip_group_check=True))
            m = PE.do(lambda e: e.matmul(ob.t[p0:p0 + 64, 128:256], v(1), aw.t[:, 256:384], start=False, stop=True,
                                         skip_group_check=True))
            aw.busy = [m]
            return m

        def heads_out(ob, pr, m):
            h = AC.do(lambda e: e.activation(OH[:, pr, :], ob.t[:, 0:T], ACT.Copy), m)
            low = DV.do(lambda e: e.tensor_tensor(OL[:, pr, :], ob.t[:, 0:T], OH[:, pr, :].bitcast(F32),
                                                  ALU.subtract), h)
            ob.busy = [low]
            oready.append([h, low])

        def sb_outputs(pr, w2):
            ob = BANKS.next()
            for e_ in range(2):
                m = sb_back(ob, 2 * pr + e_, *w2[e_])
            return ob, m

        oready = []
        scores, weights = {}, {}
        for pr in range(10):
            if pr < 8:
                j, b, ms = pair("sbqk", XH, XL, xs[-1])
                done(j)
            elif pr == 8:
                group = ByK(["sbo"] * 2, OH, OL)
                for k in range(6):
                    group.run(k, oready[k])
            if pr >= 1 and pr - 1 < 8:
                sp2 = sb_softplus(scores.pop(pr - 1))
            if pr >= 2:
                ob, m = sb_outputs(pr - 2, weights.pop(pr - 2))
                heads_out(ob, pr - 2, m)
                if pr >= 8:
                    group.run(pr - 2, oready[pr - 2])
            if pr >= 1 and pr - 1 < 8:
                md = [sb_mid(*z) for z in sp2]
            if pr < 8:
                qk = QK.next()
                DV.do(lambda e: e.scalar_tensor_tensor(qk.t[:, 0, :], b.t[:, 0:T], 0.125, rb.t[:, :], ALU.mult,
                                                       ALU.mult), ms[1], qk.busy, rbm)
                d = DV.do(lambda e: e.tensor_tensor(qk.t[:, 1, :], b.t[:, T:2 * T], rb.t[:, :], ALU.mult))
                b.busy = [d]
                scores[pr] = [sb_scores(qk, e_, d) for e_ in range(2)]
                qk.busy = [scores[pr][1][1]]
                rb.busy = [d]
            if pr >= 1 and pr - 1 < 8:
                weights[pr - 1] = [sb_weights(*z) for z in md]
            pump()
        n, marks = project_out("sbo", OH, OL, oready, 0, group)
        n2, xs = residual(n, marks, 0, 4)
        n, marks = ffn2(0, False, xs, n2)
        n2, xs = residual(n, marks, 1, 0)

        rope = rope_tables()
        n, marks = ffn2(1, True, xs, n2)
        n2, xs = residual(n, marks, 1, 2)
        VT1 = ph("VT1", 16, [P, 2, 1024])
        OH = ph("OH1", 24, [P, 8, T], F32R)
        OL = ph("OL1", 32, [P, 8, T], F32R)
        CQ = ph("CQ", 40, [P, 5, T])
        CH = ph("CH", 45, [P, 3, T], F32R)
        CL = ph("CL", 48, [P, 3, T], F32R)
        QF = ph("QF", 51, [P, 16, T])
        KF = ph("KF", 67, [P, 16, T])
        SW = Turn([Slot(ph(f"SW{i}", 83 + 4 * i, [P, 4, T])) for i in range(2)])
        SM_ = Turn([Slot(ph(f"SX{i}", 91 + 1.5 * i, [P, 384])) for i in range(5)])
        PT = Turn([Slot(ph(f"PT{i}", 98.5 + 1.5 * i, [P, 384])) for i in range(3)])
        MX = Turn([Slot(ph(f"MX{i}", 103 + 0.125 * i, [P, 8])) for i in range(6)])
        cq = []
        mb = by_k(["mla0", "mla1"], XH, XL, xs)
        n2.sums(D)
        j, w, wl, wm = take("mla2")
        b = BANKS.next()
        m = project(w, wl, lambda k: (k * P, k * P + P), KD, XH, XL, b.t[:, 0:T], [wm, b.busy])
        done(j)
        rb, rbm = n2.spread()
        for c in range(3):
            if c < 2:
                bb, mm = mb[c], mb[c].done
            else:
                bb, mm = b, m
            for t in range(2 if c < 2 else 1):
                d = DV.do(lambda e: e.tensor_tensor(CQ[:, 2 * c + t, :], bb.t[:, t * T:(t + 1) * T], rb.t[:, :],
                                                    ALU.mult), mm, rbm)
                cq.append(d)
            bb.busy = [d]
        pump()
        rb.busy = [d]
        nq = Norm()
        nq.add(CQ[:, 0, :], cq[0])
        nq.add(CQ[:, 1, :], cq[1])
        rq = nq.finish(256)
        nk = Norm()
        nk.add(CQ[:, 2, :], cq[2])
        rk = nk.finish(128)
        for t in range(3):
            g = SM[:, S_QN + t:S_QN + t + 1]
            rr = rq if t < 2 else rk
            ta = TA.next()
            d = DV.do(lambda e, t=t, g=g, rr=rr: e.scalar_tensor_tensor(ta.t[:, :], CQ[:, t, :], g, rr[0].t[:, :],
                                                                        ALU.mult, ALU.mult), rr[2], ta.busy)
            ch = halves_of(ta.t[:, :], CH[:, t, :], CL[:, t, :], d)
            ta.busy = [*ch]
            rr[0].busy = [d]
        R4 = slice(64, 96)
        swap = [(i + 16) % 32 for i in range(32)]

        def rotate(dst, n, marks, eng=None):
            sw = SW.next()
            d = DV.do(lambda e: e.stream_shuffle(sw.t[R4, 0:n, :], dst, swap), marks, sw.busy)
            d1 = DV.do(lambda e: e.tensor_tensor(sw.t[R4, 0:n, :], sw.t[R4, 0:n, :],
                                                 SIN[R4, :].unsqueeze(1).to_broadcast([32, n, T]), ALU.mult), d, rope)
            d2 = DV.do(lambda e: e.tensor_tensor(dst, dst, COS[R4, :].unsqueeze(1).to_broadcast([32, n, T]), ALU.mult),
                       d)
            d3 = DV.do(lambda e: e.tensor_tensor(dst, dst, sw.t[R4, 0:n, :], ALU.add), d1, d2)
            sw.busy = [d3]
            return d3

        kr = rotate(CQ[R4, 3:4, :], 1, cq[3])
        krc = AC.do(lambda e: e.activation(KF[R4, :, :], CQ[R4, 3, :].unsqueeze(1).to_broadcast([32, 16, T]),
                                           ACT.Copy), kr)
        j, w, wl, wm = take("mlakv")
        kfm = {}
        for h2 in range(8):
            b = BANKS.next()
            for e_ in range(2):
                h = 2 * h2 + e_
                m = mm3(b.t[:, e_ * T:(e_ + 1) * T], w[:, h * P:(h + 1) * P], wl[:, h * P:(h + 1) * P],
                        CH[:, 2, :], CL[:, 2, :], True, True, True, [wm, ch, b.busy])
            c = AC.do(lambda e, h2=h2: e.activation(KF[0:64, 2 * h2:2 * h2 + 2, :],
                                                    b.t[0:64, :].rearrange("p (a b) -> p a b", a=2), ACT.Copy), m)
            b.busy = [c]
            kfm[h2] = c
        vts = []
        for t in range(2):
            for g in range(4):
                b = BANKS.next()
                vv = lambda w_, g=g: w_[:, g * 512:(g + 1) * 512].rearrange("p (a b) -> p a b", a=4)[:, :, 64:128]
                m = mm3(b.t[:, 0:256].rearrange("p (a b) -> p a b", a=4), CH[:, 2, t * P:(t + 1) * P],
                        CL[:, 2, t * P:(t + 1) * P], vv(w), vv(wl), True, True, True, [b.busy])
                c = DV.do(lambda e, t=t, g=g: e.tensor_copy(VT1[:, t, g * 256:(g + 1) * 256], b.t[:, 0:256]), m)
                b.busy = [c]
                vts.append(c)
        done(j)
        pump()
        MSC = 1.0 / 96 ** 0.5
        qfm = {}

        def mla_q(c):
            j, w, wl, wm = take("mlaq")
            for h2 in range(4):
                b = BANKS.next()
                for e_ in range(2):
                    o = (2 * h2 + e_) * 96
                    m = project(w, wl, lambda k, o=o: (k * 768 + o, k * 768 + o + 96), 2, CH, CL,
                                b.t[0:96, e_ * T:(e_ + 1) * T], [wm, b.busy])
                hh = 8 * c + 2 * h2
                q = AC.do(lambda e, hh=hh: e.activation(QF[0:96, hh:hh + 2, :],
                                                        b.t[0:96, :].rearrange("p (a b) -> p a b", a=2), ACT.Copy), m)
                b.busy = [q]
                if h2 % 2:
                    r_ = rotate(QF[R4, hh - 2:hh + 2, :], 4, q)
                    for x in range(hh - 2, hh + 2):
                        qfm[x] = [r_, q]
            done(j)
            pump()

        def mla_scores(h):
            b = BANKS.next()
            PE.wait(qfm[h], kfm[h // 2], krc, b.busy)
            PE.quiet(lambda e: e.matmul(b.t[:, 0:128], QF[0:96, h, 0:P], KF[0:96, h, 0:P], start=True, stop=False,
                                        skip_group_check=True))
            PE.quiet(lambda e: e.matmul(b.t[:, 128:384], QF[0:96, h, P:T], KF[0:96, h, :], start=False, stop=False,
                                        skip_group_check=True))
            PE.quiet(lambda e: e.matmul(b.t[:, 0:128], IDN, NEGM[:, P:2 * P], start=False, stop=False,
                                        skip_group_check=True))
            m = PE.do(lambda e: e.matmul(b.t[:, 256:384], IDN, NEGM[:, P:2 * P], start=False, stop=True,
                                         skip_group_check=True))
            return b, m

        def mla_exp(b, m):
            sx, mx = SM_.next(), MX.next()
            DV.do(lambda e: e.tensor_reduce(mx.t[:, 0:1], b.t[:, 0:128], AX, ALU.max), m, mx.busy)
            d = DV.do(lambda e: e.tensor_reduce(mx.t[:, 1:2], b.t[:, 128:384], AX, ALU.max))
            d = DV.do(lambda e: e.tensor_scalar(mx.t[:, 2:4], mx.t[:, 0:2], -MSC, None, ALU.mult), d)
            AC.do(lambda e: e.activation(sx.t[:, 0:128], b.t[:, 0:128], ACT.Exp, bias=mx.t[:, 2:3], scale=MSC,
                                         accum_out=mx.t[:, 4:5]), d, sx.busy)
            s = AC.do(lambda e: e.activation(sx.t[:, 128:384], b.t[:, 128:384], ACT.Exp, bias=mx.t[:, 3:4], scale=MSC,
                                             accum_out=mx.t[:, 5:6]))
            b.busy = [s]
            return sx, mx, s

        def mla_divide(sx, mx, s):
            d = DV.do(lambda e: e.reciprocal(mx.t[:, 6:8], mx.t[:, 4:6]), s)
            DV.do(lambda e: e.tensor_scalar(sx.t[:, 0:128], sx.t[:, 0:128], mx.t[:, 6:7], None, ALU.mult), d)
            d = DV.do(lambda e: e.tensor_scalar(sx.t[:, 128:384], sx.t[:, 128:384], mx.t[:, 7:8], None, ALU.mult))
            mx.busy = [d]
            return sx, d

        def mla_mid(sx, d):
            b = BANKS.next()
            PE.wait(d, b.busy)
            for z in range(3):
                f = lambda e, z=z: e.transpose(b.t[:, z * P:(z + 1) * P], sx.t[:, z * P:(z + 1) * P], IDN)
                m = PE.do(f) if z == 2 else PE.quiet(f)
            sx.busy = [m]
            pt = PT.next()
            c = AC.do(lambda e: e.activation(pt.t[:, :], b.t[:, 0:384], ACT.Copy), m, pt.busy)
            b.busy = [c]
            return pt, c

        def mla_back(ob, h, pt, c):
            p0 = 64 * (h % 2)
            PE.wait(c, vts, ob.busy if h % 2 == 0 else [])
            v = lambda t: VT1[:, t, h * 64:h * 64 + 64]
            PE.quiet(lambda e: e.matmul(ob.t[p0:p0 + 64, 0:256], v(0), pt.t[:, 0:256], start=True, stop=False,
                                        skip_group_check=True))
            m = PE.do(lambda e: e.matmul(ob.t[p0:p0 + 64, 128:256], v(1), pt.t[:, 256:384], start=False, stop=True,
                                         skip_group_check=True))
            pt.busy = [m]
            return m

        oready = []
        sc, ex, dv, pt_ = {}, {}, {}, {}
        group = None
        for h in range(-3, 19):
            if h == -3:
                mla_q(0)
                AC.quiet(lambda e: e.preload_act_table_set("exp_and_others"))
            if h == 2:
                mla_q(1)
            if 0 <= h + 3 < 16:
                sc[h + 3] = mla_scores(h + 3)
            if 0 <= h + 2 < 16:
                ex[h + 2] = mla_exp(*sc.pop(h + 2))
            if 0 <= h + 1 < 16:
                dv[h + 1] = mla_divide(*ex.pop(h + 1))
            if 0 <= h < 16:
                pt_[h] = mla_mid(*dv.pop(h))
            if 0 <= h - 1 < 16:
                if (h - 1) % 2 == 0:
                    ob = BANKS.next()
                m = mla_back(ob, h - 1, *pt_.pop(h - 1))
                if (h - 1) % 2:
                    heads_out(ob, (h - 1) // 2, m)
            if h == 14:
                group = ByK(["mlao"] * 2, OH, OL)
                for k in range(6):
                    group.run(k, oready[k])
        for k in range(6, 8):
            group.run(k, oready[k])
        n, marks = project_out("mlao", OH, OL, oready, 1, group)
        n2, xs = residual(n, marks, 1, 4)
        n, marks = ffn2(1, False, xs, n2)
        _, last = residual(n, marks, None, None)
        SP.quiet(lambda e: e.dma_start(out, X[:, :, :]).then_inc(s_out, 16), last)
        SP.wait((s_out, 16))


def kernel(**inputs):
    import numpy as np
    import concourse.bacc as _bacc
    from concourse.bass_utils import run_bass_kernel_spmd as _run

    g = {k: np.asarray(v) for k, v in inputs.items()}

    def con(a):
        return np.ascontiguousarray(a)

    def cols(w, n):
        K, N = w.shape
        return con(w.reshape(K // P, P, N // n, n).transpose(2, 1, 0, 3)).reshape(N // n, P, K // P * n)

    def paired(w):
        K, N = w.shape
        F = N // 2 // P
        return con(w.reshape(K // P, P, 2, F, P).transpose(3, 1, 0, 2, 4)).reshape(F, P, K // P * 2 * P)

    def down(w):
        return con(w.reshape(2, 11, P, KD, P).transpose(3, 0, 2, 1, 4)).reshape(16, P, 11 * P)

    def vec(v):
        return v.reshape(-1, P).T

    win = g["w_in"][0]
    AK = 512
    parts = [win[:, 0:3 * AK], win[:, 3 * AK:4 * AK], win[:, 6 * AK:7 * AK], win[:, 4 * AK:5 * AK],
             win[:, 5 * AK:6 * AK], win[:, 7 * AK:]]
    win = np.concatenate(parts, axis=1)
    cst = np.zeros((P, C_END), np.float32)
    cst[:, C_ID:C_ID + P] = np.eye(P)
    cst[:, C_ONE:C_ONE + P] = 1
    cst[:, C_TRI:C_TRI + P] = np.tril(np.ones((P, P)))
    cst[:, C_NEG + P:C_NEG + 2 * P] = np.triu(np.full((P, P), NEG), 1)
    inv = (np.float32(10000.0) ** (-np.arange(0, 32, 2, dtype=np.float32) / np.float32(32))).astype(np.float32)
    cst[:, C_INV] = np.tile(inv, 8)
    cst[:, C_SGN] = np.tile(np.repeat([-1.0, 1.0], 16), 4)
    cst[0:4, C_SEL:C_SEL + 2] = np.tile(np.eye(2), (2, 1))
    cc = np.stack([vec(g["c"][0]), vec(g["c_ctx"])], axis=2).reshape(P, 16)
    small = np.concatenate(
        [cc, vec(g["b_mod"][0]), vec(g["g_mix"][0]), vec(g["g_ffn"][0]), vec(g["g_final"]), vec(g["g_norm_a"][0]),
         vec(g["lb_gamma"].reshape(-1)), vec(g["norm_g_2"].reshape(-1)), vec(g["mla_q_norm_2"][0]),
         vec(g["mla_kv_norm_2"][0])], axis=1)
    sb = g["sb_w_in_2"][0]
    mla = g["mla_w_in_2"][0]
    mla = np.concatenate([mla[:, 0:384]] + [mla[:, 384:416]] * 8, axis=1)
    wu2 = g["ffn_w_in_2"].reshape(4, D, 2 * FT * P)
    wd2 = g["ffn_w_out_2"].reshape(4, FT * P, D)
    arr = {
        "cst": cst,
        "small": small,
        "x": g["x"][0].T.reshape(KD, P, T).transpose(1, 0, 2),
        "ctx": g["ctx"][0].T.reshape(KD, P, T).transpose(1, 0, 2),
        "rows": np.concatenate([g["ln_v_g"], g["ln_v_b"], g["b_s"].reshape(1, 512)], axis=0),
        "wst": g["w_s"][0].transpose(2, 0, 1),
        "pos": g["positions_2"],
        "mod": cols(g["w_mod"][0], 256),
        "win": cols(win, 256),
        "wpa": cols(g["w_pa"][0], 512),
        "wpb": cols(g["w_pb"][0], 512),
        "wo": cols(g["w_o"][0], 256),
        "up": paired(g["w_up"][0]),
        "down": down(g["w_down"][0]),
        "up2": np.concatenate([paired(w) for w in wu2], axis=0),
        "down2": np.concatenate([down(w) for w in wd2], axis=0),
        "sbv": cols(sb[:, 2048:3072], 256),
        "sbqk": paired(sb[:, 0:2048]),
        "sbo": cols(g["sb_w_out_2"][0], 256),
        "mla0": cols(mla[:, 0:256], 256),
        "mla1": cols(mla[:, 256:512], 256),
        "mla2": cols(mla[:, 512:640], 128),
        "mlakv": cols(g["mla_w_ukv_2"][0], 2048),
        "mlaq": cols(g["mla_w_uq_2"][0], 768),
        "mlao": cols(g["mla_w_out_2"][0], 256),
    }
    nc = _bacc.Bacc("TRN2", target_bir_lowering=False, num_devices=1)
    arrays, aps = {}, {}
    for name, v in arr.items():
        v = con(v)
        arrays[f"in_{name}"] = v
        aps[name] = nc.dram_tensor(f"in_{name}", v.shape, mybir.dt.from_np(v.dtype), kind="ExternalInput").ap()
    o = nc.dram_tensor("out_0", (P, KD, T), F32, kind="ExternalOutput").ap()
    build(nc, aps, o)
    r = _run(nc, [arrays], core_ids=[0])
    y = r.results[0]["out_0"]
    return con(y.transpose(1, 0, 2).reshape(D, T).T).reshape(1, T, D)
```
